# Optimizing a Trainium2 kernel written in Bass

```python
import jax, jax.numpy as jnp
from jax import lax
import numpy as np

D_MODEL = 1024
BATCH = 1
SEQ = 256
DEPTH = 2

GRID_W = 64
CTX_LEN = 256
EPS = 1e-6
F_FLOOR = 1e-20
N_MOD = 6
HG_WIDTH = 512
HG_HEADS = 4
HG_DIM = HG_WIDTH // HG_HEADS
CHUNK = 16
SC_WIDTH = 512
SC_HALF = SC_WIDTH // 2
CONV_W = 3
IN_COLS = 5 * HG_WIDTH + 3 * SC_WIDTH
SPLITS = tuple(HG_WIDTH * i for i in range(1, 6)) + (5 * HG_WIDTH + SC_WIDTH, 5 * HG_WIDTH + 2 * SC_WIDTH)
PEER_HEADS = 8
PEER_QDIM = 256
PEER_HALF = PEER_QDIM // 2
N_KEYS = 128
N_EXPERTS = N_KEYS * N_KEYS
PEER_TOPK = 16
PEER_BLOCK = 128


def rms_norm(x, g):
    xf = x.astype(jnp.float32)
    y = xf * lax.rsqrt(jnp.mean(xf * xf, axis=-1, keepdims=True) + EPS)
    return (y * g.astype(jnp.float32)).astype(x.dtype)

def modulate(h, shift, scale):
    return h * (1 + scale) + shift

def to_heads(a):
    return a.reshape(a.shape[0], a.shape[1], HG_HEADS, HG_DIM).astype(jnp.float32)

def flip(a):
    return a[:, ::-1]

def forget_terms(z, lb):
    f = lb + (1.0 - lb) * jax.nn.sigmoid(z)
    logf = jnp.log(jnp.maximum(f, F_FLOOR))
    key = (1.0 - lb) * jax.nn.sigmoid(-z)
    return logf, key

def gla_chunk(q, k, v, logf, s0):
    bsz, t, h, _ = q.shape
    dv = v.shape[-1]
    n = t // CHUNK
    q, k, v, logf = (a.reshape(bsz, n, CHUNK, h, a.shape[-1]) for a in (q, k, v, logf))
    b = jnp.cumsum(logf, axis=2)
    mask = jnp.tril(jnp.ones((CHUNK, CHUNK), bool))[None, None, :, :, None, None]
    diff = b[:, :, :, None] - b[:, :, None, :]
    decay = jnp.where(mask, jnp.exp(jnp.where(mask, diff, 0.0)), 0.0)
    att = jnp.einsum('bnthk,bntshk,bnshk->bnhts', q, decay, k)
    o_intra = jnp.einsum('bnhts,bnshv->bnthv', att, v)
    b_last = b[:, :, -1]
    q_in = q * jnp.exp(b)
    k_out = k * jnp.exp(b_last[:, :, None] - b)

    def step(s, xs):
        qc, kc, vc, dc = xs
        o = jnp.einsum('bchk,bhkv->bchv', qc, s)
        s = dc[..., None] * s + jnp.einsum('bchk,bchv->bhkv', kc, vc)
        return s, o

    xs = tuple(jnp.moveaxis(a, 1, 0) for a in (q_in, k_out, v, jnp.exp(b_last)))
    s_final, o_inter = lax.scan(step, s0, xs)
    o = o_intra + jnp.moveaxis(o_inter, 0, 1)
    return o.reshape(bsz, t, h, dv), s_final

def gla_final_state(k, v, logf):
    b = jnp.cumsum(logf, axis=1)
    kd = k * jnp.exp(b[:, -1:] - b)
    return jnp.einsum('bthk,bthv->bhkv', kd, v)

def hgrn2_mix(q, iv, zf, zb, g, lbf, lbb, s0f, s0b):
    q, iv, zf, zb = (to_heads(a) for a in (q, iv, zf, zb))
    logf_f, k_f = forget_terms(zf, lbf)
    o_f, s_f = gla_chunk(q, k_f, iv, logf_f, s0f)
    logf_b, k_b = forget_terms(zb, lbb)
    o_b, s_b = gla_chunk(flip(q), flip(k_b), flip(iv), flip(logf_b), s0b)
    o = o_f + flip(o_b)
    o = o * lax.rsqrt(jnp.mean(o * o, axis=-1, keepdims=True) + EPS)
    o = o.reshape(g.shape).astype(g.dtype) * jax.nn.silu(g)
    return o, s_f, s_b

def hgrn2_final_states(iv, zf, zb, lbf, lbb):
    iv, zf, zb = (to_heads(a) for a in (iv, zf, zb))
    logf_f, k_f = forget_terms(zf, lbf)
    s_f = gla_final_state(k_f, iv, logf_f)
    logf_b, k_b = forget_terms(zb, lbb)
    s_b = gla_final_state(flip(k_b), flip(iv), flip(logf_b))
    return s_f, s_b

def conv3(u, w, axis):
    n = u.shape[axis]
    pad = [(0, 0)] * u.ndim
    pad[axis] = (1, 1)
    up = jnp.pad(u, pad)
    return (w[0] * lax.slice_in_dim(up, 0, n, axis=axis)
            + w[1] * lax.slice_in_dim(up, 1, n + 1, axis=axis)
            + w[2] * lax.slice_in_dim(up, 2, n + 2, axis=axis))

def grid_conv(u, w, rows):
    bsz, t, ch = u.shape
    grid = u.reshape(bsz, rows, GRID_W, ch)
    horiz = conv3(grid[..., :SC_HALF], w[:, :SC_HALF], axis=2)
    vert = conv3(grid[..., SC_HALF:], w[:, SC_HALF:], axis=1)
    return jnp.concatenate([horiz, vert], axis=-1).reshape(bsz, t, ch)

def seq_conv(u, w):
    return conv3(u, w, axis=1)

def token_mixer(h, w_in_l, w_out_l, conv_w_l, lbf, lbb, s0f, s0b, conv_fn):
    iv, zf, zb, q, g, cg, bg, hv = jnp.split(h @ w_in_l, SPLITS, axis=-1)
    o_rec, s_f, s_b = hgrn2_mix(q, iv, zf, zb, g, lbf, lbb, s0f, s0b)
    o_conv = bg * conv_fn(cg * hv, conv_w_l)
    y = jnp.concatenate([o_rec, o_conv], axis=-1) @ w_out_l
    return y, s_f, s_b

def peer_ffn(h, wq, subkeys, u, v):
    bsz, t, d = h.shape
    qr = (h @ wq).astype(jnp.float32).reshape(bsz, t, PEER_HEADS, 2, PEER_HALF)
    scores = jnp.einsum('bthpd,hpkd->bthpk', qr, subkeys.astype(jnp.float32))
    s1, i1 = lax.top_k(scores[..., 0, :], PEER_TOPK)
    s2, i2 = lax.top_k(scores[..., 1, :], PEER_TOPK)
    n_cand = PEER_TOPK * PEER_TOPK
    cand = (s1[..., :, None] + s2[..., None, :]).reshape(bsz, t, PEER_HEADS, n_cand)
    cidx = (i1[..., :, None] * N_KEYS + i2[..., None, :]).reshape(bsz, t, PEER_HEADS, n_cand)
    top, pos = lax.top_k(cand, PEER_TOPK)
    eidx = jnp.take_along_axis(cidx, pos, axis=-1)
    gate = jax.nn.softmax(top, axis=-1).astype(h.dtype)
    n_blk = bsz * t // PEER_BLOCK
    n_sel = PEER_HEADS * PEER_TOPK
    hb = h.reshape(n_blk, PEER_BLOCK, d)
    eb = eidx.reshape(n_blk, PEER_BLOCK, n_sel)
    gb = gate.reshape(n_blk, PEER_BLOCK, n_sel)

    def block(args):
        hk, ek, gk = args
        act = jax.nn.gelu(jnp.einsum('ted,td->te', u[ek], hk), approximate=False)
        return jnp.einsum('te,ted->td', gk * act, v[ek])

    return lax.map(block, (hb, eb, gb)).reshape(bsz, t, d)

def first_inputs(seed: int = 0) -> dict:
    key = jax.random.key(seed)
    ks = jax.random.split(key, 17)
    nrm = lambda k, shape, scale: jax.random.normal(k, shape, jnp.float32) * scale
    mix_w = HG_WIDTH + SC_WIDTH
    return {
        'x': nrm(ks[0], (BATCH, SEQ, D_MODEL), 1.0),
        'c': nrm(ks[1], (BATCH, D_MODEL), 1.0),
        'ctx': nrm(ks[2], (BATCH, CTX_LEN, D_MODEL), 1.0),
        'c_ctx': nrm(ks[3], (D_MODEL,), 1.0),
        'w_mod': nrm(ks[4], (DEPTH, D_MODEL, N_MOD * D_MODEL), 0.5 * D_MODEL ** -0.5),
        'b_mod': nrm(ks[5], (DEPTH, N_MOD * D_MODEL), 0.01),
        'norm1_g': 1.0 + nrm(ks[6], (DEPTH, D_MODEL), 0.1),
        'norm2_g': 1.0 + nrm(ks[7], (DEPTH, D_MODEL), 0.1),
        'w_in': nrm(ks[8], (DEPTH, D_MODEL, IN_COLS), D_MODEL ** -0.5),
        'conv_w': nrm(ks[9], (DEPTH, CONV_W, SC_WIDTH), CONV_W ** -0.5),
        'w_out': nrm(ks[10], (DEPTH, mix_w, D_MODEL), mix_w ** -0.5),
        'lb_logits': nrm(ks[11], (DEPTH, 2, HG_WIDTH), 0.5),
        'peer_wq': nrm(ks[12], (DEPTH, D_MODEL, PEER_HEADS * PEER_QDIM), D_MODEL ** -0.5),
        'peer_subkeys': nrm(ks[13], (DEPTH, PEER_HEADS, 2, N_KEYS, PEER_HALF), PEER_HALF ** -0.5),
        'peer_u': nrm(ks[14], (DEPTH, N_EXPERTS, D_MODEL), D_MODEL ** -0.5),
        'peer_v': nrm(ks[15], (DEPTH, N_EXPERTS, D_MODEL), PEER_HEADS ** -0.5),
        'final_g': 1.0 + nrm(ks[16], (D_MODEL,), 0.1),
    }

def first_block(x, c, ctx, c_ctx, w_mod, b_mod, norm1_g, norm2_g, w_in, conv_w, w_out,
              lb_logits, peer_wq, peer_subkeys, peer_u, peer_v, final_g):
    rows = x.shape[1] // GRID_W
    p_lb = jax.nn.softmax(lb_logits.astype(jnp.float32), axis=0)
    lower = jnp.cumsum(p_lb, axis=0) - p_lb[0]
    cond_x = jax.nn.silu(c)
    cond_c = jax.nn.silu(c_ctx)
    latent_conv = lambda u, w: grid_conv(u, w, rows)
    zero_state = jnp.zeros((ctx.shape[0], HG_HEADS, HG_DIM, HG_DIM), jnp.float32)
    xc = ctx
    for l in range(DEPTH):
        lbf = lower[l, 0].reshape(HG_HEADS, HG_DIM)
        lbb = lower[l, 1].reshape(HG_HEADS, HG_DIM)
        mod_x = (cond_x @ w_mod[l] + b_mod[l])[:, None, :]
        mod_c = (cond_c @ w_mod[l] + b_mod[l])[None, None, :]
        sh1x, sc1x, g1x, sh2x, sc2x, g2x = jnp.split(mod_x, N_MOD, axis=-1)
        sh1c, sc1c, g1c, sh2c, sc2c, g2c = jnp.split(mod_c, N_MOD, axis=-1)
        hc = modulate(rms_norm(xc, norm1_g[l]), sh1c, sc1c)
        if l < DEPTH - 1:
            yc, s_f, s_b = token_mixer(hc, w_in[l], w_out[l], conv_w[l], lbf, lbb,
                                       zero_state, zero_state, seq_conv)
            xc = xc + g1c * yc
            hc2 = modulate(rms_norm(xc, norm2_g[l]), sh2c, sc2c)
            xc = xc + g2c * peer_ffn(hc2, peer_wq[l], peer_subkeys[l], peer_u[l], peer_v[l])
        else:
            iv_c, zf_c, zb_c = jnp.split(hc @ w_in[l][:, :3 * HG_WIDTH], 3, axis=-1)
            s_f, s_b = hgrn2_final_states(iv_c, zf_c, zb_c, lbf, lbb)
        hx = modulate(rms_norm(x, norm1_g[l]), sh1x, sc1x)
        yx, _, _ = token_mixer(hx, w_in[l], w_out[l], conv_w[l], lbf, lbb, s_f, s_b, latent_conv)
        x = x + g1x * yx
        hx2 = modulate(rms_norm(x, norm2_g[l]), sh2x, sc2x)
        x = x + g2x * peer_ffn(hx2, peer_wq[l], peer_subkeys[l], peer_u[l], peer_v[l])
    return rms_norm(x, final_g)


DEPTH_2 = 4

N_MIXERS = 3
N_META = 16
NORM_EPS = 1e-6

FOX_HEADS = 16
FOX_HEAD_DIM = D_MODEL // FOX_HEADS
FOX_Q_BLOCK = 128
FOX_IN = 4 * D_MODEL + FOX_HEADS

GLA_HEADS = 4
GLA_DK = D_MODEL // 2 // GLA_HEADS
GLA_DV = D_MODEL // GLA_HEADS
GLA_GATE_RANK = 16
GLA_GATE_NORMALIZER = 16.0
GLA_CHUNK = 64
GLA_QK = GLA_HEADS * GLA_DK
GLA_V = GLA_HEADS * GLA_DV
GLA_IN = 2 * GLA_QK + 2 * GLA_V + GLA_GATE_RANK

GDN_HEADS = 8
GDN_DK = 128
GDN_DV = 128
GDN_CONV = 4
GDN_CHUNK = 64
GDN_CONV_DIM = 2 * GDN_HEADS * GDN_DK + GDN_HEADS * GDN_DV
GDN_IN = GDN_CONV_DIM + GDN_HEADS * GDN_DV + 2 * GDN_HEADS

D_FF = ((-(-8 * D_MODEL // 3) + 255) // 256) * 256

N_FOX = (DEPTH_2 + 2) // 3
N_GLA = (DEPTH_2 + 1) // 3
N_GDN = DEPTH_2 // 3


def rmsnorm(x, g):
    xf = x.astype(jnp.float32)
    y = xf * lax.rsqrt(jnp.mean(xf * xf, axis=-1, keepdims=True) + NORM_EPS)
    return (y * g.astype(jnp.float32)).astype(x.dtype)

def l2norm(x):
    xf = x.astype(jnp.float32)
    return (xf * lax.rsqrt(jnp.sum(xf * xf, axis=-1, keepdims=True) + NORM_EPS)).astype(x.dtype)

def to_chunks(a, chunk):
    b, t = a.shape[0], a.shape[1]
    return jnp.moveaxis(a.reshape((b, t // chunk, chunk) + a.shape[2:]), 1, 0)

def from_chunks(a):
    a = jnp.moveaxis(a, 0, 1)
    return a.reshape((a.shape[0], a.shape[1] * a.shape[2]) + a.shape[3:])

def chunked_scan(chunk_fn, state0, seqs, chunk):
    state, o_meta = chunk_fn(state0, tuple(a[:, :N_META] for a in seqs))
    real = tuple(to_chunks(a[:, N_META:], chunk) for a in seqs)
    _, o_real = lax.scan(chunk_fn, state, real)
    return jnp.concatenate([o_meta, from_chunks(o_real)], axis=1)

def fox_attend(q, cq, qpos, k, v, ck, kpos):
    s = jnp.einsum('bqhd,bkhd->bhqk', q, k).astype(jnp.float32)
    bias = cq[..., :, None] - ck[..., None, :]
    mask = kpos[None, :] <= qpos[:, None]
    s = jnp.where(mask, s + bias, -jnp.inf)
    p = jax.nn.softmax(s, axis=-1)
    return jnp.einsum('bhqk,bkhd->bqhd', p.astype(v.dtype), v)

def fox_mixer(h, w_in, b_f, q_gain, k_gain, w_out):
    B, L, _ = h.shape
    H, Dh = FOX_HEADS, FOX_HEAD_DIM
    proj = h @ w_in
    q, k, v, gate, f = jnp.split(proj, [D_MODEL, 2 * D_MODEL, 3 * D_MODEL, 4 * D_MODEL], axis=-1)
    q = rmsnorm(q.reshape(B, L, H, Dh), q_gain) * (Dh ** -0.5)
    k = rmsnorm(k.reshape(B, L, H, Dh), k_gain)
    v = v.reshape(B, L, H, Dh)
    log_f = jax.nn.log_sigmoid((f + b_f).astype(jnp.float32))
    c = jnp.cumsum(log_f, axis=1).transpose(0, 2, 1)
    kpos = jnp.arange(L)

    o_meta = fox_attend(q[:, :N_META], c[:, :, :N_META], kpos[:N_META],
                        k[:, :N_META], v[:, :N_META], c[:, :, :N_META], kpos[:N_META])

    n_blk = (L - N_META) // FOX_Q_BLOCK
    q_blocks = q[:, N_META:].reshape(B, n_blk, FOX_Q_BLOCK, H, Dh).swapaxes(0, 1)
    cq_blocks = c[:, :, N_META:].reshape(B, H, n_blk, FOX_Q_BLOCK).transpose(2, 0, 1, 3)
    qpos_blocks = (N_META + jnp.arange(n_blk * FOX_Q_BLOCK)).reshape(n_blk, FOX_Q_BLOCK)

    def block(args):
        qb, cqb, qp = args
        return fox_attend(qb, cqb, qp, k, v, c, kpos)

    o_real = from_chunks(lax.map(block, (q_blocks, cq_blocks, qpos_blocks)))
    o = jnp.concatenate([o_meta, o_real], axis=1).reshape(B, L, H * Dh)
    o = o * jax.nn.sigmoid(gate)
    return (o @ w_out).astype(h.dtype)

def gla_chunk_2(state, inputs):
    q, k, v, g = inputs
    C = q.shape[1]
    b = jnp.cumsum(g, axis=1)
    causal = jnp.tril(jnp.ones((C, C), dtype=bool))
    diff = b[:, :, None] - b[:, None, :]
    decay = jnp.exp(jnp.where(causal[None, :, :, None, None], diff, -jnp.inf))
    A = jnp.einsum('bthd,bshd,btshd->bhts', q, k, decay)
    o_intra = jnp.einsum('bhts,bshv->bthv', A, v)
    o_inter = jnp.einsum('bthd,bhdv->bthv', q * jnp.exp(b), state)
    b_last = b[:, -1]
    k_dec = k * jnp.exp(b_last[:, None] - b)
    new_state = state * jnp.exp(b_last)[..., None] + jnp.einsum('bshd,bshv->bhdv', k_dec, v)
    return new_state, (o_intra + o_inter).astype(v.dtype)

def gla_mixer(h, w_in, w_alpha2, b_alpha, o_gain, w_out):
    B, L, _ = h.shape
    H = GLA_HEADS
    proj = h @ w_in
    q, k, v, r, a_lr = jnp.split(proj, [GLA_QK, 2 * GLA_QK, 2 * GLA_QK + GLA_V, 2 * GLA_QK + 2 * GLA_V], axis=-1)
    q = q.reshape(B, L, H, GLA_DK) * (GLA_DK ** -0.5)
    k = k.reshape(B, L, H, GLA_DK)
    v = v.reshape(B, L, H, GLA_DV)
    g = jax.nn.log_sigmoid((a_lr @ w_alpha2 + b_alpha).astype(jnp.float32)) / GLA_GATE_NORMALIZER
    g = g.reshape(B, L, H, GLA_DK)
    state0 = jnp.zeros((B, H, GLA_DK, GLA_DV), jnp.float32)
    o = chunked_scan(gla_chunk_2, state0, (q, k, v, g), GLA_CHUNK)
    o = rmsnorm(o, o_gain) * jax.nn.silu(r.reshape(B, L, H, GLA_DV))
    return (o.reshape(B, L, GLA_V) @ w_out).astype(h.dtype)

def causal_depthwise_conv(x, w):
    return lax.conv_general_dilated(
        x, w.astype(x.dtype), window_strides=(1,), padding=[(GDN_CONV - 1, 0)],
        dimension_numbers=('NWC', 'WIO', 'NWC'), feature_group_count=x.shape[-1])

def gdn_chunk(state, inputs):
    q, k, v, g, beta = inputs
    C = q.shape[1]
    qh = q.transpose(0, 2, 1, 3)
    kh = k.transpose(0, 2, 1, 3)
    vh = v.transpose(0, 2, 1, 3)
    bt = beta.transpose(0, 2, 1).astype(jnp.float32)[..., None]
    b = jnp.cumsum(g, axis=1).transpose(0, 2, 1)
    diff = b[..., :, None] - b[..., None, :]
    incl = jnp.tril(jnp.ones((C, C), dtype=bool))
    strict = jnp.tril(jnp.ones((C, C), dtype=bool), k=-1)
    kb = kh.astype(jnp.float32) * bt
    vb = vh.astype(jnp.float32) * bt
    lower = jnp.einsum('bhtd,bhsd->bhts', kb, kh) * jnp.exp(jnp.where(strict, diff, -jnp.inf))
    t_mat = jnp.eye(C, dtype=jnp.float32) + lower
    rhs = jnp.concatenate([vb, kb * jnp.exp(b)[..., None]], axis=-1)
    sol = lax.linalg.triangular_solve(t_mat, rhs, left_side=True, lower=True, unit_diagonal=True)
    u, w = sol[..., :GDN_DV], sol[..., GDN_DV:]
    v_new = u - jnp.einsum('bhcd,bhdv->bhcv', w, state)
    attn = jnp.einsum('bhtd,bhsd->bhts', qh, kh) * jnp.exp(jnp.where(incl, diff, -jnp.inf))
    o = jnp.einsum('bhts,bhsv->bhtv', attn, v_new) + \
        jnp.einsum('bhtd,bhdv->bhtv', qh * jnp.exp(b)[..., None], state)
    b_last = b[..., -1]
    k_dec = kh * jnp.exp(b_last[..., None] - b)[..., None]
    new_state = state * jnp.exp(b_last)[..., None, None] + jnp.einsum('bhsd,bhsv->bhdv', k_dec, v_new)
    return new_state, o.transpose(0, 2, 1, 3).astype(v.dtype)

def gdn_mixer(h, w_in, conv_w, a_log, dt_bias, o_gain, w_out):
    B, L, _ = h.shape
    H = GDN_HEADS
    proj = h @ w_in
    qkv, gate, a, beta_logit = jnp.split(
        proj, [GDN_CONV_DIM, GDN_CONV_DIM + H * GDN_DV, GDN_CONV_DIM + H * GDN_DV + H], axis=-1)
    qkv = jax.nn.silu(causal_depthwise_conv(qkv, conv_w))
    q, k, v = jnp.split(qkv, [H * GDN_DK, 2 * H * GDN_DK], axis=-1)
    q = l2norm(q.reshape(B, L, H, GDN_DK)) * (GDN_DK ** -0.5)
    k = l2norm(k.reshape(B, L, H, GDN_DK))
    v = v.reshape(B, L, H, GDN_DV)
    beta = jax.nn.sigmoid(beta_logit)
    g = -jnp.exp(a_log.astype(jnp.float32)) * jax.nn.softplus((a + dt_bias).astype(jnp.float32))
    state0 = jnp.zeros((B, H, GDN_DK, GDN_DV), jnp.float32)
    o = chunked_scan(gdn_chunk, state0, (q, k, v, g, beta), GDN_CHUNK)
    o = rmsnorm(o, o_gain) * jax.nn.silu(gate.reshape(B, L, H, GDN_DV))
    return (o.reshape(B, L, H * GDN_DV) @ w_out).astype(h.dtype)

def swiglu(h, w_gate_up, w_down):
    gu = h @ w_gate_up
    gt, up = gu[..., :D_FF], gu[..., D_FF:]
    return ((jax.nn.silu(gt) * up) @ w_down).astype(h.dtype)

def second_inputs(seed: int = 0) -> dict:
    key = jax.random.key(seed)
    ks = jax.random.split(key, 24)

    def nrm(k, shape, fan_in):
        return jax.random.normal(k, shape, jnp.float32) * (fan_in ** -0.5)

    def gain(k, shape):
        return 1.0 + 0.02 * jax.random.normal(k, shape, jnp.float32)

    dt = jnp.exp(jax.random.uniform(ks[20], (N_GDN, GDN_HEADS), jnp.float32, np.log(1e-3), np.log(1e-1)))
    return {
        "x": jax.random.normal(ks[0], (BATCH, SEQ, D_MODEL), jnp.float32),
        "meta_tokens": jax.random.normal(ks[1], (N_META, D_MODEL), jnp.float32),
        "norm_mix": gain(ks[2], (DEPTH_2, D_MODEL)),
        "norm_ffn": gain(ks[3], (DEPTH_2, D_MODEL)),
        "w_gate_up": nrm(ks[4], (DEPTH_2, D_MODEL, 2 * D_FF), D_MODEL),
        "w_down": nrm(ks[5], (DEPTH_2, D_FF, D_MODEL), D_FF),
        "fox_w_in": nrm(ks[6], (N_FOX, D_MODEL, FOX_IN), D_MODEL),
        "fox_b_f": 2.0 + 0.5 * jax.random.normal(ks[7], (N_FOX, FOX_HEADS), jnp.float32),
        "fox_q_gain": gain(ks[8], (N_FOX, FOX_HEAD_DIM)),
        "fox_k_gain": gain(ks[9], (N_FOX, FOX_HEAD_DIM)),
        "fox_w_out": nrm(ks[10], (N_FOX, D_MODEL, D_MODEL), D_MODEL),
        "gla_w_in": nrm(ks[11], (N_GLA, D_MODEL, GLA_IN), D_MODEL),
        "gla_w_alpha2": nrm(ks[12], (N_GLA, GLA_GATE_RANK, GLA_QK), GLA_GATE_RANK),
        "gla_b_alpha": 0.1 * jax.random.normal(ks[13], (N_GLA, GLA_QK), jnp.float32),
        "gla_o_gain": gain(ks[14], (N_GLA, GLA_DV)),
        "gla_w_out": nrm(ks[15], (N_GLA, GLA_V, D_MODEL), GLA_V),
        "gdn_w_in": nrm(ks[16], (N_GDN, D_MODEL, GDN_IN), D_MODEL),
        "gdn_conv_w": nrm(ks[17], (N_GDN, GDN_CONV, 1, GDN_CONV_DIM), GDN_CONV),
        "gdn_a_log": jnp.log(jax.random.uniform(ks[18], (N_GDN, GDN_HEADS), jnp.float32, 1.0, 16.0)),
        "gdn_dt_bias": dt + jnp.log(-jnp.expm1(-dt)),
        "gdn_o_gain": gain(ks[19], (N_GDN, GDN_DV)),
        "gdn_w_out": nrm(ks[21], (N_GDN, GDN_HEADS * GDN_DV, D_MODEL), GDN_HEADS * GDN_DV),
    }

def second_block(x, meta_tokens, norm_mix, norm_ffn, w_gate_up, w_down,
              fox_w_in, fox_b_f, fox_q_gain, fox_k_gain, fox_w_out,
              gla_w_in, gla_w_alpha2, gla_b_alpha, gla_o_gain, gla_w_out,
              gdn_w_in, gdn_conv_w, gdn_a_log, gdn_dt_bias, gdn_o_gain, gdn_w_out):
    B = x.shape[0]
    meta = jnp.broadcast_to(meta_tokens[None].astype(x.dtype), (B, N_META, D_MODEL))
    h = jnp.concatenate([meta, x], axis=1)
    for i in range(DEPTH_2):
        kind, j = i % N_MIXERS, i // N_MIXERS
        y = rmsnorm(h, norm_mix[i])
        if kind == 0:
            mix = fox_mixer(y, fox_w_in[j], fox_b_f[j], fox_q_gain[j], fox_k_gain[j], fox_w_out[j])
        elif kind == 1:
            mix = gla_mixer(y, gla_w_in[j], gla_w_alpha2[j], gla_b_alpha[j], gla_o_gain[j], gla_w_out[j])
        else:
            mix = gdn_mixer(y, gdn_w_in[j], gdn_conv_w[j], gdn_a_log[j], gdn_dt_bias[j], gdn_o_gain[j], gdn_w_out[j])
        h = h + mix
        h = h + swiglu(rmsnorm(h, norm_ffn[i]), w_gate_up[i], w_down[i])
    return h[:, N_META:]


def setup_inputs(seed=0):
    out = dict(first_inputs(seed))
    for name, value in second_inputs(seed + 1).items():
        if name != "x":
            out[name + "_2"] = value
    return out


def reference(
    x, c, ctx, c_ctx, w_mod, b_mod, norm1_g, norm2_g, w_in, conv_w, w_out, lb_logits, peer_wq,
    peer_subkeys, peer_u, peer_v, final_g, meta_tokens_2, norm_mix_2, norm_ffn_2, w_gate_up_2,
    w_down_2, fox_w_in_2, fox_b_f_2, fox_q_gain_2, fox_k_gain_2, fox_w_out_2, gla_w_in_2,
    gla_w_alpha2_2, gla_b_alpha_2, gla_o_gain_2, gla_w_out_2, gdn_w_in_2, gdn_conv_w_2,
    gdn_a_log_2, gdn_dt_bias_2, gdn_o_gain_2, gdn_w_out_2,
):
    x = first_block(
        x, c, ctx, c_ctx, w_mod, b_mod, norm1_g, norm2_g, w_in, conv_w, w_out, lb_logits,
        peer_wq, peer_subkeys, peer_u, peer_v, final_g,
    )
    return second_block(
        x, meta_tokens_2, norm_mix_2, norm_ffn_2, w_gate_up_2, w_down_2, fox_w_in_2, fox_b_f_2,
        fox_q_gain_2, fox_k_gain_2, fox_w_out_2, gla_w_in_2, gla_w_alpha2_2, gla_b_alpha_2,
        gla_o_gain_2, gla_w_out_2, gdn_w_in_2, gdn_conv_w_2, gdn_a_log_2, gdn_dt_bias_2,
        gdn_o_gain_2, gdn_w_out_2,
    )


_drawn_inputs = setup_inputs


def setup_inputs(seed=0):
    import zlib

    import numpy as np

    out = dict(_drawn_inputs(seed))
    spreads = {}
    factors = {'ctx': 2.673,
     'c_ctx': 3.692,
     'fox_q_gain_2': 8.0,
     'fox_k_gain_2': 8.0,
     'gla_o_gain_2': 4.93,
     'gdn_o_gain_2': 7.38}
    for name, (base, spread) in spreads.items():
        noise = np.random.default_rng([zlib.crc32(name.encode()), seed]).standard_normal(out[name].shape)
        drawn = base * np.exp(spread * noise) if base else spread * noise
        out[name] = __import__('jax').numpy.asarray(drawn.astype(out[name].dtype))
    for name, factor in factors.items():
        out[name] = (out[name] * factor).astype(out[name].dtype)
    return out
```

```python
import numpy as np
from collections import namedtuple
from contextlib import ExitStack, contextmanager

import concourse.bass as bass
from concourse import mybir
from concourse.alu_op_type import AluOpType as ALU

F32 = mybir.dt.float32
I32 = mybir.dt.int32
U32 = mybir.dt.uint32
ACT = mybir.ActivationFunctionType
AX = mybir.AxisListType.X

P = 128
D = 1024
KD = D // P
EPS = 1e-6
LN2 = float(np.log(2.0))

SEQ = 256
TWO = 2 * SEQ
DEPTH = 2
N_MOD = 6
HG_HEADS = 4
GRID_W = 64
PEER_HEADS = 8
TOPK = 16
N_KEYS = 128
SEL = PEER_HEADS * TOPK
LEVELS = 7

META = 16
T2 = META + SEQ
TILES2 = ((0, 128), (128, 128), (256, 16))
FOX_HEADS = 16
DK_FOX = 64
GDN_HEADS = 8
D_FF = 2816
KF = D_FF // P

RING = 8
BANKS = 8
NEG = -1e30

SMALL = {}


def small_columns():
    at = 0
    for name, n in (("c_ctx", KD), ("c", KD), ("b_mod", DEPTH * 48), ("norm1_g", DEPTH * KD),
                    ("norm2_g", DEPTH * KD), ("conv_w", DEPTH * 12), ("lb_logits", DEPTH * 8),
                    ("final_g", KD), ("norm_mix_2", 4 * KD), ("norm_ffn_2", 4 * KD),
                    ("fox_q_gain_2", 2), ("fox_k_gain_2", 2), ("gla_b_alpha_2", 4),
                    ("gla_o_gain_2", 2), ("gdn_conv_w_2", 96), ("gdn_o_gain_2", 1)):
        SMALL[name] = (at, n)
        at += n
    return at


N_SMALL = small_columns()

CONST = {}


def const_columns():
    at = 0
    for name, n in (("ident", P), ("ones", P), ("ones64", P), ("causal", 3 * P), ("decay_incl", P),
                    ("decay_strict", P), ("fwd", LEVELS * P), ("iota", TOPK)):
        CONST[name] = (at, n)
        at += n
    return at


N_CONST = const_columns()


def constants():
    c = np.zeros((P, N_CONST), np.float32)

    def put(name, value):
        a, n = CONST[name]
        c[:, a:a + n] = value

    i = np.arange(P)
    put("ident", np.eye(P))
    put("ones", 1.0)
    put("ones64", (i[:, None] // 64) == (i[None, :] // 64))
    put("causal", np.concatenate([np.zeros((P, 2 * P)), np.where(i[None, :] > i[:, None], NEG, 0.0)], 1))
    put("decay_incl", np.where(i[:, None] > i[None, :], NEG, 0.0))
    put("decay_strict", np.where(i[:, None] < i[None, :], 1.0, 0.0))
    both = np.zeros((P, LEVELS + 1, P), np.int32)
    fwd = np.zeros((P, LEVELS, P), np.float32)
    for l in range(LEVELS):
        m = 1 << l
        same = (i[:, None] // (2 * m)) == (i[None, :] // (2 * m))
        left = (i // m) % 2 == 0
        fwd[:, l] = same & left[:, None] & ~left[None, :]
        both[:, l] = same & (left[:, None] != left[None, :])
    both[:, LEVELS] = np.eye(P)
    put("fwd", fwd.reshape(P, -1))
    put("iota", np.arange(TOPK)[None, :])
    scan = np.ones((P, 2, HG_HEADS, SEQ), np.float32)
    scan[:, :, :, 0] = 0.0
    return c, both.reshape(P, -1), scan.reshape(P, -1)


class Program:

    def __init__(self, nc):
        self.nc, self.stages, self.used = nc, 0, 0


@contextmanager
def stage(k, name, signals):
    k.stages += 1
    sems = [k.nc.alloc_semaphore(f"{name}_{s}_{k.stages}") for s in signals.split()]
    with k.nc.Block(no_gpsimd_drain=True) as block:
        yield block, namedtuple("Signals", signals)(*sems)
    if sems:
        k.nc.clear_and_free_semaphores(sems)
    k.nc.all_engine_barrier()


def sbuf(k, es, name, shape, dtype=F32):
    k.stages += 1
    return es.enter_context(k.nc.sbuf_tensor(f"{name}_{k.stages}", shape, dtype))


class Order:

    def __init__(self, eng, sem):
        self.eng, self.sem, self.n = eng, sem, 0

    def __call__(self, ins):
        self.n += 1
        ins.then_inc(self.sem, 1)
        self.eng.wait_ge(self.sem, self.n)



def plan_weights(a):
    units = []

    def chunks(w, order):
        for c in order:
            units.append((w[c], w.shape[-1]))

    for l in range(DEPTH):
        chunks(a.w_mod[l], range(48))
    for l in range(DEPTH):
        chunks(a.w_in[l], range(32))
        chunks(a.w_out[l], range(8))
        chunks(a.peer_wq[l], range(16))
    for i in range(4):
        kind, j = i % 3, i // 3
        w_in, extra, w_out = {0: (a.fox_w_in_2, a.fox_w_f, a.fox_w_out_2), 1: (a.gla_w_in_2, a.gla_w_a, a.gla_w_out_2),
                              2: (a.gdn_w_in_2, a.gdn_w_ab, a.gdn_w_out_2)}[kind]
        chunks(w_in[j], range(w_in.shape[1]))
        chunks(extra[j], range(extra.shape[1]))
        chunks(w_out[j], range(8))
        gate_up = a.w_gate_up_2[i]
        for c in range(KF):
            chunks(gate_up, (c, KF + c))
        for c in range(KD):
            for k0 in range(0, KF, KD):
                n = min(KD, KF - k0) * P
                units.append((a.w_down_2[i][c][:, k0 * P:k0 * P + n], n))
    return units


def load_unit(k, sp, u):
    if u < len(k.units):
        src, n = k.units[u]
        sp.dma_start(k.ring[:, u % RING, 0:n], src).then_inc(k.landed[u % RING], 16)


def project(k, name, outs, x, evict):
    first, n_units = k.used, sum(len(o) for o in outs)
    k.used += n_units
    act_name, dve_name = 0, 1
    with stage(k, name, "act_took dve_took tmp order") as (block, s):

        @block.sync
        def _(sp):
            for u in range(first, first + n_units):
                sp.wait_ge(k.unit_done, u + 1)
                load_unit(k, sp, u + RING)

        @block.tensor
        def _(pe):
            u = first
            for c, out in enumerate(outs):
                if c >= BANKS:
                    pe.wait_ge((s.act_took, s.dve_took)[c % 2], (c - BANKS) // 2 + 1)
                for unit in out:
                    pe.wait_ge(k.landed[u % RING], 16 * (u // RING + 1))
                    for dst, lhsT, rhs, start, stop in unit(k.bank[c % BANKS], k.ring[:, u % RING, :]):
                        last = pe.matmul(dst, lhsT, rhs, start=start, stop=stop)
                    last.then_inc(k.unit_done, 1)
                    u += 1

        def take(eng, mine, took):
            u = first
            for c, out in enumerate(outs):
                u += len(out)
                if c % 2 == mine:
                    eng.wait_ge(k.unit_done, u)
                    evict(eng, c, k.bank[c % BANKS], s).then_inc(took, 1)

        @block.scalar
        def _(act):
            take(act, act_name, s.act_took)

        @block.vector
        def _(dve):
            take(dve, dve_name, s.dve_took)


def fm_out(x, T, n_units=1, kt=KD, m=P):
    def unit(j):
        def made(bank, w):
            for i in range(min(KD, kt - j * KD)):
                t = j * KD + i
                yield bank[0:m, 0:T], w[:, i * m:(i + 1) * m], x(t), t == 0, t == kt - 1
        return made
    return [unit(j) for j in range(n_units)]


def tm_out(x, tiles):
    def made(bank, w):
        for i, (t0, n) in enumerate(tiles):
            for t in range(KD):
                yield (bank[0:n, i * P:(i + 1) * P], x(t)[:, t0:t0 + n], w[:, t * P:(t + 1) * P],
                       t == 0, t == KD - 1)
    return [made]


def copy(k, eng, out, in_):
    if eng is k.nc.scalar:
        return eng.copy(out, in_)
    return eng.tensor_copy(out, in_)



def rms_norm(k, name, x, T, gain, shift, out, kd=KD):
    with ExitStack() as es, stage(k, name, "squares sum root order scaled done") as (block, s):
        sq = sbuf(k, es, "sq", [P, kd, T])
        rstd = sbuf(k, es, "rstd", [P, T])
        bank = k.bank[0]

        @block.scalar
        def _(act):
            act.activation(sq[:, :, :], x, ACT.Square).then_inc(s.squares, 1)
            act.wait_ge(s.sum, 1)
            act.activation(rstd[:, :], bank[:, 0:T], ACT.Sqrt, scale=1.0 / (kd * P), bias=k.eps[:, 0:1]).then_inc(s.root, 1)
            if shift is not None:
                for c in range(kd):
                    act.wait_ge(s.scaled, c + 1)
                    for t0, n, b in shift(c):
                        last = act.activation(out[:, c, t0:t0 + n], out[:, c, t0:t0 + n], ACT.Identity, bias=b)
                last.then_inc(s.done, 1)

        @block.tensor
        def _(pe):
            pe.wait_ge(s.squares, 1)
            for c in range(kd):
                last = pe.matmul(bank[:, 0:T], k.ones, sq[:, c, :], start=(c == 0), stop=(c == kd - 1))
            last.then_inc(s.sum, 1)

        @block.vector
        def _(dve):
            order = Order(dve, s.order)
            dve.wait_ge(s.root, 1)
            order(dve.reciprocal(rstd[:, :], rstd[:, :]))
            for c in range(kd):
                for t0, n, g in gain(c):
                    last = dve.scalar_tensor_tensor(out=out[:, c, t0:t0 + n], in0=x[:, c, t0:t0 + n], scalar=g,
                                                    in1=rstd[:, t0:t0 + n], op0=ALU.mult, op1=ALU.mult)
                last.then_inc(s.scaled, 1)


def transpose_chunks(k, name, jobs):
    groups = [jobs[i:i + 4] for i in range(0, len(jobs), 4)]
    with stage(k, name, "turned act_took dve_took") as (block, s):

        @block.tensor
        def _(pe):
            for g, group in enumerate(groups):
                if g >= BANKS:
                    pe.wait_ge((s.act_took, s.dve_took)[g % 2], (g - BANKS) // 2 + 1)
                for i, (out, in_) in enumerate(group):
                    m, n = in_.shape
                    last = pe.transpose(k.bank[g % BANKS][0:n, i * P:i * P + m], in_, k.ident[0:m, 0:m])
                last.then_inc(s.turned, 1)

        def take(eng, mine, took):
            for g, group in enumerate(groups):
                if g % 2 == mine:
                    eng.wait_ge(s.turned, g + 1)
                    for i, (out, in_) in enumerate(group):
                        m, n = in_.shape
                        last = copy(k, eng, out, k.bank[g % BANKS][0:n, i * P:i * P + m])
                    last.then_inc(took, 1)

        @block.scalar
        def _(act):
            take(act, 0, s.act_took)

        @block.vector
        def _(dve):
            take(dve, 1, s.dve_took)



def modulation(k):
    with ExitStack() as es:
        cond = sbuf(k, es, "cond", [P, KD, 2])
        with stage(k, "cond", "done") as (block, s):
            @block.scalar
            def _(act):
                act.activation(cond[:, :, 0], k.small("c_ctx"), ACT.Silu)
                act.activation(cond[:, :, 1], k.small("c"), ACT.Silu).then_inc(s.done, 1)

        def evict(eng, c, bank, s):
            bias = k.small("b_mod")[:, c:c + 1]
            out = k.mods[:, c // 48, c % 48, :]
            if eng is k.nc.scalar:
                return eng.activation(out, bank[:, 0:2], ACT.Identity, bias=bias)
            return eng.tensor_scalar(out, bank[:, 0:2], bias, None, ALU.add)

        project(k, "modulate", [fm_out(lambda t: cond[:, t, :], 2)[0:1] for _ in range(DEPTH * 48)], None, evict)

    with ExitStack() as es, stage(k, "bounds", "order exps subs") as (block, s):
        lb = k.small("lb_logits").rearrange("p (l n) -> p l n", l=DEPTH)
        top = sbuf(k, es, "top", [P, 8])
        e = sbuf(k, es, "e", [P, DEPTH, 8])
        total = sbuf(k, es, "total", [P, 8])

        @block.vector
        def _(dve):
            order = Order(dve, s.order)
            for l in range(DEPTH):
                for n, (scale0, name) in enumerate(((8, "norm1_g"), (32, "norm2_g"))):
                    g = k.small(name)[:, l * KD:(l + 1) * KD].unsqueeze(2).broadcast_to([P, KD, 2])
                    dve.scalar_tensor_tensor(out=k.gain[:, l, n, :, :], in0=k.mods[:, l, scale0:scale0 + KD, :],
                                             scalar=1.0, in1=g, op0=ALU.add, op1=ALU.mult)
            order(dve.tensor_tensor(top[:, :], lb[:, 0, :], lb[:, 1, :], ALU.max))
            for l in range(DEPTH):
                dve.tensor_tensor(e[:, l, :], lb[:, l, :], top[:, :], ALU.subtract).then_inc(s.subs, 1)
            dve.wait_ge(s.exps, 1)
            order(dve.tensor_tensor(total[:, :], e[:, 0, :], e[:, 1, :], ALU.add))
            order(dve.reciprocal(total[:, :], total[:, :]))
            for l in range(DEPTH):
                order(dve.tensor_tensor(e[:, l, :], e[:, l, :], total[:, :], ALU.mult))
            order(dve.tensor_tensor(total[:, :], e[:, 0, :], e[:, 1, :], ALU.add))
            order(dve.tensor_tensor(k.lower[:, 0, :], e[:, 0, :], e[:, 0, :], ALU.subtract))
            order(dve.tensor_tensor(k.lower[:, 1, :], total[:, :], e[:, 0, :], ALU.subtract))
            order(dve.tensor_scalar(k.upper[:, :, :], k.lower[:, :, :], -1.0, 1.0, ALU.mult, ALU.add))

        @block.scalar
        def _(act):
            act.wait_ge(s.subs, 2)
            act.activation(e[:, :, :], e[:, :, :], ACT.Exp).then_inc(s.exps, 1)


def both_ways(gain):
    return lambda c: [(0, SEQ, gain(c)[:, 0:1]), (SEQ, SEQ, gain(c)[:, 1:2])]


def halves(ap, m, side):
    return ap.rearrange("p h (n two m) -> p h n two m", two=2, m=m)[:, :, :, side, :]


def hgrn_gates(k, l, z, bc, key):
    n = 2 * HG_HEADS
    with ExitStack() as es, stage(k, "gates", "sig logs order fed") as (block, s):
        low = sbuf(k, es, "low", [P, n, SEQ])
        high = sbuf(k, es, "high", [P, n, SEQ])
        b = bc[:, :, :, :].rearrange("p d h t -> p (d h) t")
        keys = key[:, :, :, :].rearrange("p d h t -> p (d h) t")

        @block.scalar
        def _(act):
            act.activation(high[:, :, :], z, ACT.Sigmoid).then_inc(s.sig, 1)
            act.activation(keys, z, ACT.Sigmoid, scale=-1.0).then_inc(s.sig, 1)
            act.wait_ge(s.fed, 1)
            act.activation(low[:, :, :], low[:, :, :], ACT.Ln).then_inc(s.logs, 1)
            act.activation(high[:, :, :], high[:, :, :], ACT.Ln).then_inc(s.logs, 1)

        @block.vector
        def _(dve):
            order = Order(dve, s.order)
            dve.wait_ge(s.sig, 2)
            for i in range(n):
                up, lo = k.upper[:, l, i:i + 1], k.lower[:, l, i:i + 1]
                dve.tensor_scalar(high[:, i, :], high[:, i, :], up, lo, ALU.mult, ALU.add)
                last = dve.tensor_scalar(keys[:, i, :], keys[:, i, :], up, None, ALU.mult)
            order(last)
            order(dve.tensor_scalar(low[:, :, :], high[:, :, :], 1e-20, 2.0 ** 60, ALU.max, ALU.mult))
            order(dve.tensor_scalar(low[:, :, :], low[:, :, :], 1.0, None, ALU.min))
            dve.tensor_scalar(high[:, :, :], high[:, :, :], 2.0 ** -60, None, ALU.max).then_inc(s.fed, 1)
            dve.wait_ge(s.logs, 2)
            order(dve.tensor_tensor(high[:, :, :], high[:, :, :], low[:, :, :], ALU.add))
            one = k.ones[:, 0:1].broadcast_to([P, SEQ])
            for i in range(n):
                last = dve.tensor_tensor_scan(b[:, i, :], one, high[:, i, :], 0.0, ALU.mult, ALU.add)
            order(last)
            back = high[:, HG_HEADS:n, :]
            order(dve.tensor_tensor(bc[:, 1, :, :], back, bc[:, 1, :, :], ALU.subtract))
            last_gate = high[:, HG_HEADS:n, SEQ - 1]
            order(dve.tensor_tensor(k.back_total[:, :], last_gate, bc[:, 1, :, SEQ - 1], ALU.subtract))


def hgrn_attention(k, q, key, bc, att):
    with ExitStack() as es, stage(k, "attend", "apart decayed scaled scored took order") as (block, s):
        dif = sbuf(k, es, "dif", [P, 2, 2, HG_HEADS, SEQ])
        kh = sbuf(k, es, "kh", [P, 2, HG_HEADS, SEQ])
        qh = sbuf(k, es, "qh", [P, 2, HG_HEADS, SEQ])
        steps = LEVELS + 2
        shape = lambda m: [P, HG_HEADS, SEQ // (2 * m), m]

        @block.gpsimd
        def _(pool):
            for j in range(1, steps):
                m = 1 << (j - 1)
                if j >= 3:
                    pool.wait_ge(s.scaled, j - 1)
                for d in range(2):
                    b = bc[:, d, :, :]
                    out = dif[:, j % 2, d, :, :]
                    mid = (halves(b, m, 0)[:, :, :, m - 1:m] if d == 0 else halves(b, m, 1)[:, :, :, 0:1]).broadcast_to(shape(m))
                    near, far = (0, 1) if d == 0 else (1, 0)
                    pool.tensor_tensor(halves(out, m, near), mid, halves(b, m, near), ALU.subtract)
                    last = pool.tensor_tensor(halves(out, m, far), halves(b, m, far), mid, ALU.subtract)
                last.then_inc(s.apart, 1)

        @block.scalar
        def _(act):
            for j in range(1, steps):
                act.wait_ge(s.apart, j)
                act.activation(dif[:, j % 2, :, :, :], dif[:, j % 2, :, :, :], ACT.Exp).then_inc(s.decayed, 1)

        @block.vector
        def _(dve):
            order = Order(dve, s.order)

            def factors(j):
                if j >= 2:
                    dve.wait_ge(s.scored, j - 1)
                ks, qs = kh[:, j % 2, :, :], qh[:, j % 2, :, :]
                if j == 0:
                    dve.tensor_tensor(ks, key[:, 0, :, :], key[:, 1, :, :], ALU.add)
                    dve.tensor_copy(qs, q).then_inc(s.scaled, 1)
                    return
                m = 1 << (j - 1)
                dve.wait_ge(s.decayed, j)
                fwd, back = dif[:, j % 2, 0, :, :], dif[:, j % 2, 1, :, :]
                dve.tensor_tensor(halves(ks, m, 0), halves(key[:, 0, :, :], m, 0), halves(fwd, m, 0), ALU.mult)
                dve.tensor_tensor(halves(ks, m, 1), halves(key[:, 1, :, :], m, 1), halves(back, m, 1), ALU.mult)
                dve.tensor_tensor(halves(qs, m, 1), halves(q, m, 1), halves(fwd, m, 1), ALU.mult)
                dve.tensor_tensor(halves(qs, m, 0), halves(q, m, 0), halves(back, m, 0), ALU.mult).then_inc(s.scaled, 1)

            def take(j):
                dve.wait_ge(s.scored, j + 1)
                for i in range(2):
                    data = k.bank[2 * (j % 2) + i][:, :].rearrange("p (h t) -> p h t", h=HG_HEADS)
                    own = att[:, i, :, i * P:(i + 1) * P]
                    if j == 0:
                        last = dve.tensor_copy(own, data)
                    elif j == steps - 1:
                        last = dve.tensor_copy(att[:, i, :, (1 - i) * P:(2 - i) * P], data)
                    else:
                        mask = k.both[:, j - 1, :].unsqueeze(1).broadcast_to([P, HG_HEADS, P])
                        last = dve.copy_predicated(own, mask, data)
                last.then_inc(s.took, 1)
                dve.wait_ge(s.took, j + 1)

            factors(0)
            for j in range(1, steps):
                factors(j)
                take(j - 1)
            take(steps - 1)

        @block.tensor
        def _(pe):
            for j in range(steps):
                pe.wait_ge(s.scaled, j + 1)
                if j >= 2:
                    pe.wait_ge(s.took, j - 1)
                for i in range(2):
                    t = i if j < steps - 1 else 1 - i
                    for h in range(HG_HEADS):
                        last = pe.matmul(k.bank[2 * (j % 2) + i][:, h * P:(h + 1) * P],
                                         kh[:, j % 2, h, i * P:(i + 1) * P], qh[:, j % 2, h, t * P:(t + 1) * P],
                                         start=True, stop=True)
                last.then_inc(s.scored, 1)


def hgrn_outputs(k, s0, q, gate, key, bc, att, from_state, out):
    with ExitStack() as es, stage(k, "outputs", "shifted grown fed mixed squares sums root order gated") as (block, s):
        grow = sbuf(k, es, "grow", [P, 2, HG_HEADS, SEQ])
        sq = sbuf(k, es, "sq", [P, HG_HEADS * SEQ])
        rstd = sbuf(k, es, "rstd", [P, HG_HEADS * SEQ])

        @block.vector
        def _(dve):
            order = Order(dve, s.order)
            if from_state:
                for h in range(HG_HEADS):
                    last = dve.tensor_scalar(grow[:, 1, h, :], bc[:, 1, h, :], k.back_total[:, h:h + 1], None, ALU.add)
                last.then_inc(s.shifted, 1)
                dve.wait_ge(s.grown, 2)
                for d in range(2):
                    last = dve.tensor_tensor(grow[:, d, :, :], grow[:, d, :, :], q, ALU.mult)
                last.then_inc(s.fed, 1)
            dve.wait_ge(s.root, 1)
            order(dve.reciprocal(rstd[:, :], rstd[:, :]))
            for n in range(2):
                half = slice(512 * n, 512 * (n + 1))
                last = dve.tensor_tensor(rstd[:, half], rstd[:, half], k.bank[n][:, :], ALU.mult)
            order(last)
            dve.wait_ge(s.gated, 1)
            dve.tensor_tensor(out, rstd[:, :].rearrange("p (h t) -> p h t", h=HG_HEADS), gate, ALU.mult)

        @block.scalar
        def _(act):
            if from_state:
                act.activation(grow[:, 0, :, :], bc[:, 0, :, :], ACT.Exp).then_inc(s.grown, 1)
                act.wait_ge(s.shifted, 1)
                act.activation(grow[:, 1, :, :], grow[:, 1, :, :], ACT.Exp).then_inc(s.grown, 1)
            act.wait_ge(s.mixed, 1)
            for n in range(2):
                last = act.activation(sq[:, 512 * n:512 * (n + 1)], k.bank[n][:, :], ACT.Square)
            last.then_inc(s.squares, 1)
            act.activation(gate, gate, ACT.Silu).then_inc(s.gated, 1)
            act.wait_ge(s.sums, 1)
            for n in range(2):
                last = act.activation(rstd[:, 512 * n:512 * (n + 1)], k.bank[2 + n][:, :], ACT.Sqrt, scale=1.0 / P, bias=k.eps[:, 0:1])
            last.then_inc(s.root, 1)

        @block.tensor
        def _(pe):
            if from_state:
                pe.wait_ge(s.fed, 1)
            for h in range(HG_HEADS):
                o = k.bank[h // 2][:, (h % 2) * SEQ:(h % 2 + 1) * SEQ]
                parts = [(k.v[:, s0 // P + i, h * P:(h + 1) * P], att[:, i, h, :]) for i in range(2)]
                if from_state:
                    parts += [(k.state[:, d, h, :], grow[:, d, h, :]) for d in range(2)]
                for i, (lhsT, rhs) in enumerate(parts):
                    last = pe.matmul(o, lhsT, rhs, start=(i == 0), stop=(i == len(parts) - 1))
            last.then_inc(s.mixed, 1)
            pe.wait_ge(s.squares, 1)
            for n in range(2):
                last = pe.matmul(k.bank[2 + n][:, :], k.ones, sq[:, 512 * n:512 * (n + 1)], start=True, stop=True)
            last.then_inc(s.sums, 1)


def hgrn_states(k, s0, key, bc):
    with ExitStack() as es, stage(k, "states", "shifted grown fed turned took summed order") as (block, s):
        dec = sbuf(k, es, "dec", [P, 2, HG_HEADS, SEQ])
        turned = sbuf(k, es, "turned", [P, 2, 2, HG_HEADS, P])

        @block.scalar
        def _(act):
            for h in range(HG_HEADS):
                act.activation(dec[:, 0, h, :], bc[:, 0, h, :], ACT.Exp, scale=-1.0, bias=bc[:, 0, h, SEQ - 1:SEQ])
            act.activation(dec[:, 1, :, :], bc[:, 1, :, :], ACT.Exp, scale=-1.0).then_inc(s.grown, 1)

        @block.vector
        def _(dve):
            dve.wait_ge(s.grown, 1)
            dve.tensor_tensor(dec[:, :, :, :], dec[:, :, :, :], key[:, :, :, :], ALU.mult).then_inc(s.fed, 1)
            for n in range(4):
                dve.wait_ge(s.turned, n + 1)
                dve.tensor_copy(turned[:, n // 2, n % 2, :, :],
                                k.bank[n][:, :].rearrange("p (h d) -> p h d", h=HG_HEADS)).then_inc(s.took, 1)
            dve.wait_ge(s.summed, 1)
            for d in range(2):
                dve.tensor_copy(k.state[:, d, :, :], k.bank[4 + d][:, :].rearrange("p (h d) -> p h d", h=HG_HEADS))

        @block.tensor
        def _(pe):
            pe.wait_ge(s.fed, 1)
            for n in range(4):
                for h in range(HG_HEADS):
                    i, d = n // 2, n % 2
                    last = pe.transpose(k.bank[n][:, h * P:(h + 1) * P], dec[:, d, h, i * P:(i + 1) * P], k.ident)
                last.then_inc(s.turned, 1)
            pe.wait_ge(s.took, 4)
            for d in range(2):
                for h in range(HG_HEADS):
                    for i in range(2):
                        last = pe.matmul(k.bank[4 + d][:, h * P:(h + 1) * P], turned[:, i, d, h, :],
                                         k.v[:, s0 // P + i, h * P:(h + 1) * P], start=(i == 0), stop=(i == 1))
            last.then_inc(s.summed, 1)


def short_conv(k, l, s0, grid, cg, bg, hv, out):
    with ExitStack() as es, stage(k, "conv", "order") as (block, s):
        u = sbuf(k, es, "u", [P, 4, SEQ])
        y = sbuf(k, es, "y", [P, 4, SEQ])

        @block.vector
        def _(dve):
            order = Order(dve, s.order)
            order(dve.tensor_tensor(u[:, :, :], cg, hv, ALU.mult))
            w = k.small("conv_w").rearrange("p (l tap c) -> p l tap c", l=DEPTH, tap=3)
            for c in range(4):
                last = dve.tensor_scalar(y[:, c, :], u[:, c, :], w[:, l, 1, c:c + 1], None, ALU.mult)
            order(last)
            for tap in (0, 2):
                for c in range(4):
                    step = GRID_W if grid and c >= 2 else 1
                    rows = SEQ // GRID_W if grid and c < 2 else 1
                    uu = u[:, c, :].rearrange("p (r w) -> p r w", r=rows)
                    yy = y[:, c, :].rearrange("p (r w) -> p r w", r=rows)
                    width = SEQ // rows
                    near, far = slice(0, width - step), slice(step, width)
                    src, dst = (near, far) if tap == 0 else (far, near)
                    last = dve.scalar_tensor_tensor(out=yy[:, :, dst], in0=uu[:, :, src], scalar=w[:, l, tap, c:c + 1],
                                                    in1=yy[:, :, dst], op0=ALU.mult, op1=ALU.add)
                order(last)
            dve.tensor_tensor(out, y[:, :, :], bg, ALU.mult)


def residual_project(k, name, x, gate, seqs):
    first = k.used
    k.used += KD
    t0, t1 = seqs[0] * SEQ, (seqs[-1] + 1) * SEQ
    with stage(k, name, "took") as (block, s):
        @block.sync
        def _(sp):
            for u in range(first, first + KD):
                sp.wait_ge(k.unit_done, u + 1)
                load_unit(k, sp, u + RING)

        @block.tensor
        def _(pe):
            for c in range(KD):
                u = first + c
                pe.wait_ge(k.landed[u % RING], 16 * (u // RING + 1))
                for t in range(KD):
                    last = pe.matmul(k.bank[c][:, 0:t1 - t0], k.ring[:, u % RING, t * P:(t + 1) * P], x[:, t, t0:t1],
                                     start=(t == 0), stop=(t == KD - 1))
                last.then_inc(k.unit_done, 1)

        @block.vector
        def _(dve):
            for c in range(KD):
                dve.wait_ge(k.unit_done, first + c + 1)
                for q in seqs:
                    half = slice(q * SEQ, (q + 1) * SEQ)
                    dve.scalar_tensor_tensor(out=k.X[:, c, half], in0=k.bank[c][:, q * SEQ - t0:(q + 1) * SEQ - t0],
                                             scalar=gate[:, c, q:q + 1], in1=k.X[:, c, half], op0=ALU.mult, op1=ALU.add)


def token_mixer_1(k, l):
    with ExitStack() as es:
        proj = sbuf(k, es, "proj", [P, 28, TWO])
        H = k.H
        last_layer = l == DEPTH - 1
        x = lambda t: H[:, t, :]
        xs = lambda t: H[:, t, SEQ:TWO]
        outs = [tm_out(x, [(i * P, P) for i in range(4)]) for _ in range(4)]
        outs += [fm_out(x, TWO) for _ in range(8)]
        outs += [fm_out(xs, SEQ) if last_layer else fm_out(x, TWO) for _ in range(20)]

        def evict(eng, c, bank, s):
            if c < 4:
                return copy(k, eng, k.v[:, :, c * P:(c + 1) * P], bank[:, :].rearrange("p (i n) -> p i n", i=4))
            if c >= 12 and last_layer:
                return copy(k, eng, proj[:, c - 4, SEQ:TWO], bank[:, 0:SEQ])
            return copy(k, eng, proj[:, c - 4, :], bank[:, :])

        project(k, "w_in", outs, None, evict)
        bc = sbuf(k, es, "bc", [P, 2, HG_HEADS, SEQ])
        key = sbuf(k, es, "key", [P, 2, HG_HEADS, SEQ])
        for n, s0 in enumerate((0, SEQ)):
            part = lambda c: proj[:, c:c + 4, s0:s0 + SEQ]
            hgrn_gates(k, l, proj[:, 0:8, s0:s0 + SEQ], bc, key)
            if n == 1 or not last_layer:
                with ExitStack() as inner:
                    att = sbuf(k, inner, "att", [P, 2, HG_HEADS, SEQ])
                    hgrn_attention(k, part(8), key, bc, att)
                    hgrn_outputs(k, s0, part(8), part(12), key, bc, att, n == 1, H[:, 0:4, s0:s0 + SEQ])
                short_conv(k, l, s0, n == 1, part(16), part(20), part(24), H[:, 4:8, s0:s0 + SEQ])
            if n == 0:
                hgrn_states(k, s0, key, bc)
    residual_project(k, "w_out", k.H, k.mods[:, l, 16:24, :], (1,) if last_layer else (0, 1))



GATHER = 6


def peer(k, a, l, tiles):
    H = k.H
    with ExitStack() as es:
        T0 = tiles[0] * P
        T = len(tiles) * P
        qr = sbuf(k, es, "qr", [P, 2 * PEER_HEADS, T])
        project(k, "peer_wq", [fm_out(lambda t: H[:, t, T0:T0 + T], T) for _ in range(2 * PEER_HEADS)], None,
                lambda eng, c, bank, s: copy(k, eng, qr[:, c, :], bank[:, 0:T]))
        hT = sbuf(k, es, "hT", [P, len(tiles), D])
        transpose_chunks(k, "h_rows", [(hT[:, i, c * P:(c + 1) * P], H[:, c, t * P:(t + 1) * P])
                                       for i, t in enumerate(tiles) for c in range(KD)])
        keys = sbuf(k, es, "subkeys", [P, 2 * PEER_HEADS, N_KEYS])
        scores = sbuf(k, es, "scores", [P, 2 * PEER_HEADS, N_KEYS])
        rows = sbuf(k, es, "rows", [P, GATHER, D])
        junk = sbuf(k, es, "junk", [P, D])
        for i, t in enumerate(tiles):
            with ExitStack() as inner:
                expert = sbuf(k, inner, "expert", [P, SEL], U32)
                weight = sbuf(k, inner, "weight", [P, SEL])
                peer_select(k, a, l, i, qr, keys, scores, expert, weight)
                peer_experts(k, a, l, i, hT, expert, weight, rows, junk)
            with stage(k, "peer_add", "turned") as (block, s):
                @block.tensor
                def _(pe):
                    for c in range(KD):
                        last = pe.transpose(k.bank[2 + c // 4][:, (c % 4) * P:(c % 4 + 1) * P], junk[:, c * P:(c + 1) * P], k.ident)
                    last.then_inc(s.turned, 1)

                @block.vector
                def _(dve):
                    dve.wait_ge(s.turned, 1)
                    for c in range(KD):
                        cols = slice(t * P, (t + 1) * P)
                        dve.scalar_tensor_tensor(out=k.X[:, c, cols], in0=k.bank[2 + c // 4][:, (c % 4) * P:(c % 4 + 1) * P],
                                                 scalar=k.mods[:, l, 40 + c, t // 2:t // 2 + 1], in1=k.X[:, c, cols],
                                                 op0=ALU.mult, op1=ALU.add)


def peer_select(k, a, l, i, qr, keys, scores, expert, weight):
    NH = 2 * PEER_HEADS
    with ExitStack() as es, stage(k, "select", "keys scored took order spread grown") as (block, s):
        best = sbuf(k, es, "best", [P, NH, TOPK])
        where = sbuf(k, es, "where", [P, NH, TOPK], U32)
        where_f = sbuf(k, es, "where_f", [P, NH, TOPK])
        cand = sbuf(k, es, "cand", [P, PEER_HEADS, TOPK, TOPK])
        top = sbuf(k, es, "top", [P, PEER_HEADS, TOPK])
        pos = sbuf(k, es, "pos", [P, PEER_HEADS, TOPK], U32)
        part = sbuf(k, es, "part", [P, 2, PEER_HEADS, TOPK], U32)
        part_f = sbuf(k, es, "part_f", [P, 2, PEER_HEADS, TOPK])
        hot = sbuf(k, es, "hot", [P, PEER_HEADS, TOPK, TOPK])
        index = sbuf(k, es, "index", [P, 2, PEER_HEADS, TOPK])
        total = sbuf(k, es, "total", [P, PEER_HEADS])

        @block.sync
        def _(sp):
            if i == 0:
                sp.dma_start(keys[:, :, :], a.peer_subkeys[l]).then_inc(s.keys, 16)

        @block.tensor
        def _(pe):
            if i == 0:
                pe.wait_ge(s.keys, 16)
            for c in range(NH):
                last = pe.matmul(k.bank[c // 4][:, (c % 4) * P:(c % 4 + 1) * P], qr[:, c, i * P:(i + 1) * P],
                                 keys[:, c, :], start=True, stop=True)
                if c % 4 == 3:
                    last.then_inc(s.scored, 1)

        @block.scalar
        def _(act):
            for n in range(NH // 4):
                act.wait_ge(s.scored, n + 1)
                act.copy(scores[:, 4 * n:4 * n + 4, :], k.bank[n][:, :].rearrange("p (c n) -> p c n", c=4)).then_inc(s.took, 1)
            act.wait_ge(s.spread, 1)
            act.activation(top[:, :, :], top[:, :, :], ACT.Exp).then_inc(s.grown, 1)

        @block.vector
        def _(dve):
            order = Order(dve, s.order)

            def top16(values, best, where):
                order(dve.max(best[:, 0:8], values))
                order(dve.max_index(where[:, 0:8], best[:, 0:8], values))
                order(dve.match_replace(values, best[:, 0:8], values, -3e38))
                order(dve.max(best[:, 8:16], values))
                order(dve.max_index(where[:, 8:16], best[:, 8:16], values))

            for c in range(NH):
                if c % 4 == 0:
                    dve.wait_ge(s.took, c // 4 + 1)
                top16(scores[:, c, :], best[:, c, :], where[:, c, :])
            order(dve.tensor_copy(where_f[:, :, :], where[:, :, :]))
            pairs = best[:, :, :].rearrange("p (h two) n -> p h two n", two=2)
            full = [P, PEER_HEADS, TOPK, TOPK]
            order(dve.tensor_tensor(cand[:, :, :, :], pairs[:, :, 0, :].unsqueeze(3).broadcast_to(full),
                                    pairs[:, :, 1, :].unsqueeze(2).broadcast_to(full), ALU.add))
            for h in range(PEER_HEADS):
                top16(cand[:, h, :, :].rearrange("p a b -> p (a b)"), top[:, h, :], pos[:, h, :])
            dve.tensor_scalar(part[:, 0, :, :], pos[:, :, :], 4, None, ALU.logical_shift_right)
            order(dve.tensor_scalar(part[:, 1, :, :], pos[:, :, :], TOPK - 1, None, ALU.bitwise_and))
            order(dve.tensor_copy(part_f[:, :, :, :], part[:, :, :, :]))
            places = where_f[:, :, :].rearrange("p (h two) n -> p h two n", two=2)
            iota = k.const("iota").unsqueeze(1).broadcast_to([P, PEER_HEADS * TOPK, TOPK]).rearrange("p (h j) n -> p h j n", h=PEER_HEADS)
            for half in range(2):
                order(dve.tensor_tensor(hot[:, :, :, :], part_f[:, half, :, :].unsqueeze(3).broadcast_to(full), iota, ALU.is_equal))
                order(dve.tensor_tensor(hot[:, :, :, :], hot[:, :, :, :],
                                        places[:, :, half, :].unsqueeze(2).broadcast_to(full), ALU.mult))
                order(dve.tensor_reduce(index[:, half, :, :], hot[:, :, :, :], AX, ALU.add))
            order(dve.scalar_tensor_tensor(out=expert[:, :], in0=index[:, 0, :, :].rearrange("p h j -> p (h j)"), scalar=float(N_KEYS),
                                           in1=index[:, 1, :, :].rearrange("p h j -> p (h j)"), op0=ALU.mult, op1=ALU.add))
            cand_top = sbuf(k, es, "largest", [P, PEER_HEADS])
            order(dve.tensor_copy(cand_top[:, :], top[:, :, 0]))
            dve.tensor_tensor(top[:, :, :], top[:, :, :],
                              cand_top[:, :].unsqueeze(2).broadcast_to([P, PEER_HEADS, TOPK]), ALU.subtract).then_inc(s.spread, 1)
            dve.wait_ge(s.grown, 1)
            order(dve.tensor_reduce(total[:, :], top[:, :, :], AX, ALU.add))
            order(dve.reciprocal(total[:, :], total[:, :]))
            order(dve.tensor_tensor(weight[:, :].rearrange("p (h j) -> p h j", h=PEER_HEADS), top[:, :, :],
                                    total[:, :].unsqueeze(2).broadcast_to([P, PEER_HEADS, TOPK]), ALU.mult))


def peer_experts(k, a, l, i, hT, expert, weight, rows, out):
    slots = " ".join(f"landed{n}" for n in range(GATHER))
    with ExitStack() as es, stage(k, "experts", slots + " dotted gelu weighed diag summed taken") as (block, s):
        landed = [s.landed0, s.landed1, s.landed2, s.landed3, s.landed4, s.landed5]
        act_in = sbuf(k, es, "act_in", [P, SEL])
        act_out = sbuf(k, es, "act_out", [P, SEL])
        diag = sbuf(k, es, "diag", [P, 4, P])
        table = (a.peer_u[l], a.peer_v[l])

        @block.gpsimd
        def _(pool):
            for n in range(2 * SEL):
                e = n % SEL
                if n >= GATHER:
                    if n - GATHER < SEL:
                        pool.wait_ge(s.dotted, n - GATHER + 1)
                    else:
                        pool.wait_ge(s.summed, n - GATHER - SEL + 1)
                pool.indirect_dma_start(rows[:, n % GATHER, :], None, table[n // SEL],
                                        bass.IndirectOffsetOnAxis(ap=expert[:, e:e + 1], axis=0)
                                        ).then_inc(landed[n % GATHER], 16)

        @block.vector
        def _(dve):
            for e in range(SEL):
                dve.wait_ge(landed[e % GATHER], 16 * (e // GATHER + 1))
                if e > 0:
                    dve.wait_ge(s.dotted, e)
                dve.tensor_tensor_reduce(out[:, :], rows[:, e % GATHER, :], hT[:, i, :], 1.0, 0.0, ALU.mult, ALU.add,
                                         act_in[:, e:e + 1]).then_inc(s.dotted, 1)
            dve.wait_ge(s.gelu, 1)
            dve.tensor_tensor(act_out[:, :], act_out[:, :], weight[:, :], ALU.mult).then_inc(s.weighed, 1)
            dve.wait_ge(s.summed, SEL)
            dve.tensor_copy(out[:, 0:512], k.bank[0][:, :])
            dve.tensor_copy(out[:, 512:1024], k.bank[1][:, :])

        @block.scalar
        def _(act):
            act.wait_ge(s.dotted, SEL)
            act.activation(act_out[:, :], act_in[:, :], ACT.Gelu).then_inc(s.gelu, 1)
            act.wait_ge(s.weighed, 1)
            for e in range(SEL):
                if e >= 4:
                    act.wait_ge(s.summed, e - 3)
                act.mul(diag[:, e % 4, :], k.ident, act_out[:, e:e + 1]).then_inc(s.diag, 1)

        @block.tensor
        def _(pe):
            for e in range(SEL):
                n = SEL + e
                pe.wait_ge(s.diag, e + 1)
                pe.wait_ge(landed[n % GATHER], 16 * (n // GATHER + 1))
                for half in range(2):
                    last = pe.matmul(k.bank[half][:, :], diag[:, e % 4, :], rows[:, n % GATHER, half * 512:(half + 1) * 512],
                                     start=(e == 0), stop=(e == SEL - 1))
                last.then_inc(s.summed, 1)


def first_block(k, a):
    modulation(k)
    for l in range(DEPTH):
        gain = lambda n: both_ways(lambda c: k.gain[:, l, n, c, :])
        shift = lambda c0: both_ways(lambda c: k.mods[:, l, c0 + c, :])
        rms_norm(k, "norm1", k.X[:, :, :], TWO, gain(0), shift(0), k.H)
        with ExitStack() as es:
            k.v = sbuf(k, es, "values", [P, 4, HG_HEADS * P])
            k.state = sbuf(k, es, "states", [P, 2, HG_HEADS, P])
            token_mixer_1(k, l)
        rms_norm(k, "norm2", k.X[:, :, :], TWO, gain(1), shift(24), k.H)
        peer(k, a, l, (0, 1, 2, 3) if l < DEPTH - 1 else (2, 3))



def add_to_residual(k):
    def evict(dve, c, bank):
        return dve.tensor_tensor(k.Y[:, c, :], bank[:, 0:T2], k.Y[:, c, :], ALU.add)
    return evict


def project_residual_2(k, name, x, n_units=1, kt=KD):
    first = k.used
    k.used += KD * n_units
    with stage(k, name, "took") as (block, s):
        @block.sync
        def _(sp):
            for u in range(first, first + KD * n_units):
                sp.wait_ge(k.unit_done, u + 1)
                load_unit(k, sp, u + RING)

        @block.tensor
        def _(pe):
            for c in range(KD):
                for j in range(n_units):
                    u = first + c * n_units + j
                    pe.wait_ge(k.landed[u % RING], 16 * (u // RING + 1))
                    for t in range(min(KD, kt - j * KD)):
                        kk = j * KD + t
                        last = pe.matmul(k.bank[c][:, 0:T2], k.ring[:, u % RING, t * P:(t + 1) * P], x[:, kk, :],
                                         start=(kk == 0), stop=(kk == kt - 1))
                    last.then_inc(k.unit_done, 1)

        @block.vector
        def _(dve):
            for c in range(KD):
                dve.wait_ge(k.unit_done, first + (c + 1) * n_units)
                dve.tensor_tensor(k.Y[:, c, :], k.bank[c][:, 0:T2], k.Y[:, c, :], ALU.add)


def head_norms(k, name, x, chunks, ones, width, eps_chunks=None, gain=None, factor=1.0, mean=True):
    with ExitStack() as es, stage(k, name, "squares summed root order taken") as (block, s):
        n = len(chunks)
        sq = sbuf(k, es, "sq", [P, 2, T2])
        rstd = sbuf(k, es, "rstd", [P, 2, T2])

        @block.scalar
        def _(act):
            for i, c in enumerate(chunks):
                if i >= 2:
                    act.wait_ge(s.summed, i - 1)
                act.activation(sq[:, i % 2, :], x[:, c, :], ACT.Square).then_inc(s.squares, 1)
                act.wait_ge(s.summed, i + 1)
                if i >= 2:
                    act.wait_ge(s.taken, i - 1)
                act.activation(rstd[:, i % 2, :], k.bank[i % 4][:, 0:T2], ACT.Sqrt, scale=1.0 / width if mean else 1.0,
                               bias=k.eps[:, 0:1]).then_inc(s.root, 1)

        @block.tensor
        def _(pe):
            for i, c in enumerate(chunks):
                pe.wait_ge(s.squares, i + 1)
                if i >= 4:
                    pe.wait_ge(s.root, i - 3)
                pe.matmul(k.bank[i % 4][:, 0:T2], ones, sq[:, i % 2, :], start=True, stop=True).then_inc(s.summed, 1)

        @block.vector
        def _(dve):
            order = Order(dve, s.order)
            for i, c in enumerate(chunks):
                dve.wait_ge(s.root, i + 1)
                order(dve.reciprocal(rstd[:, i % 2, :], rstd[:, i % 2, :]))
                g = factor if gain is None else gain(c)
                dve.scalar_tensor_tensor(out=x[:, c, :], in0=x[:, c, :], scalar=g, in1=rstd[:, i % 2, :],
                                         op0=ALU.mult, op1=ALU.mult).then_inc(s.taken, 1)




def fox(k, a, j):
    H = k.H
    with ExitStack() as es:
        q = sbuf(k, es, "q", [P, KD, T2])
        kk = sbuf(k, es, "k", [P, KD, T2])
        v = sbuf(k, es, "v", [P, 3, D])
        gate = sbuf(k, es, "gate", [P, KD, T2])
        f = sbuf(k, es, "f", [FOX_HEADS, 3, T2])
        x = lambda t: H[:, t, 0:T2]

        def evict(eng, c, bank, s):
            if c == 32:
                return copy(k, eng, f[:, 0, :], bank[0:FOX_HEADS, 0:T2])
            if 16 <= c < 24:
                c -= 16
                copy(k, eng, v[:, 0:2, c * P:(c + 1) * P], bank[:, 0:2 * P].rearrange("p (i n) -> p i n", i=2))
                return copy(k, eng, v[0:META, 2, c * P:(c + 1) * P], bank[0:META, 2 * P:3 * P])
            out = q[:, c, :] if c < 8 else kk[:, c - 8, :] if c < 16 else gate[:, c - 24, :]
            return copy(k, eng, out, bank[:, 0:T2])

        outs = [fm_out(x, T2) for _ in range(16)] + [tm_out(x, TILES2) for _ in range(8)]
        outs += [fm_out(x, T2) for _ in range(8)] + [fm_out(x, T2, m=FOX_HEADS)]
        project(k, "fox_in", outs, None, evict)
        gq, gk = k.small("fox_q_gain_2")[:, j:j + 1], k.small("fox_k_gain_2")[:, j:j + 1]
        with ExitStack() as es2, stage(k, "fox_gates", "order ready absd expd lned scaled") as (block, s):
            tmp = sbuf(k, es2, "tmp", [FOX_HEADS, T2])

            @block.vector
            def _(dve):
                order = Order(dve, s.order)
                order(dve.tensor_scalar(k.qgain[:, 0:1], gq, DK_FOX ** -0.5, None, ALU.mult))
                order(dve.tensor_scalar(f[:, 0, :], f[:, 0, :], k.fox_b[:, j:j + 1], None, ALU.add))
                dve.scalar_tensor_tensor(out=tmp[:, :], in0=f[:, 0, :], scalar=-1.0, in1=f[:, 0, :], op0=ALU.mult, op1=ALU.max).then_inc(s.absd, 1)
                dve.wait_ge(s.lned, 1)
                order(dve.scalar_tensor_tensor(out=f[:, 0, :], in0=f[:, 0, :], scalar=0.0, in1=tmp[:, :], op0=ALU.min, op1=ALU.subtract))
                order(dve.tensor_tensor_scan(f[:, 1, :], k.ones[0:FOX_HEADS, 0:1].broadcast_to([FOX_HEADS, T2]), f[:, 0, :], 0.0, ALU.mult, ALU.add))
                order(dve.tensor_scalar(f[:, 2, :], f[:, 1, :], -1.0, None, ALU.mult))

            @block.scalar
            def _(act):
                act.wait_ge(s.absd, 1)
                act.activation(tmp[:, :], tmp[:, :], ACT.Exp, scale=-1.0).then_inc(s.expd, 1)
                act.wait_ge(s.expd, 1)
                act.activation(tmp[:, :], tmp[:, :], ACT.Ln, bias=k.one[0:FOX_HEADS, 0:1]).then_inc(s.lned, 1)
                act.activation(gate[:, :, :], gate[:, :, :], ACT.Sigmoid)

        head_norms(k, "q_norm", q, range(KD), k.ones64, DK_FOX, gain=lambda c: k.qgain[:, 0:1])
        head_norms(k, "k_norm", kk, range(KD), k.ones64, DK_FOX, gain=lambda c: gk)
        fox_attention(k, q, kk, v, gate, f)
    project_residual_2(k, "fox_out", H[:, :, 0:T2])


def fox_attention(k, q, kk, v, gate, f):
    H = k.H
    steps = [(h, i) for h in range(FOX_HEADS) for i in range(3)]
    with ExitStack() as es, stage(k, "attention", "scored maxed negated exped summed rcp normed turned copied mixed gated") as (block, s):
        sc = sbuf(k, es, "sc", [P, 2, T2])
        pr = sbuf(k, es, "pr", [P, 2, T2])
        pT = sbuf(k, es, "pT", [P, 2, 3, P])
        mx = sbuf(k, es, "mx", [P, 2])
        nmx = sbuf(k, es, "nmx", [P, 2])
        total = sbuf(k, es, "total", [P, 2])
        inv = sbuf(k, es, "inv", [P, 2])

        def score(pe, n):
            h, i = steps[n]
            t0, nq = TILES2[i]
            nk = t0 + nq
            lo = (h % 2) * DK_FOX
            if n >= 2:
                pe.wait_ge(s.maxed, n - 1)
            bank = k.bank[n % 2][0:nq, 0:nk]
            pe.matmul(bank, q[lo:lo + DK_FOX, h // 2, t0:t0 + nq], kk[lo:lo + DK_FOX, h // 2, 0:nk], start=True, stop=False)
            pick = k.ident[0:FOX_HEADS, h:h + 1]
            pe.matmul(bank, f[:, 1, t0:t0 + nq], pick.broadcast_to([FOX_HEADS, nk]), start=False, stop=False)
            pe.matmul(bank, pick.broadcast_to([FOX_HEADS, nq]), f[:, 2, 0:nk], start=False, stop=True).then_inc(s.scored, 1)

        def turn(pe, n):
            h, i = steps[n]
            t0, nq = TILES2[i]
            pe.wait_ge(s.normed, n + 1)
            if n >= 2:
                pe.wait_ge(s.copied, n - 1)
            for j in range(i + 1):
                k0, nk = TILES2[j]
                last = pe.transpose(k.bank[2 + n % 2][0:nk, j * P:j * P + nq], pr[0:nq, n % 2, k0:k0 + nk], k.ident[0:nq, 0:nq])
            last.then_inc(s.turned, 1)

        def mix(pe, n):
            h, i = steps[n]
            t0, nq = TILES2[i]
            pe.wait_ge(s.copied, n + 1)
            if i == 0 and h % 2 == 0 and h >= 4:
                pe.wait_ge(s.gated, h // 2 - 1)
            lo = (h % 2) * DK_FOX
            for j in range(i + 1):
                nk = TILES2[j][1]
                last = pe.matmul(k.bank[4 + (h // 2) % 2][lo:lo + DK_FOX, t0:t0 + nq], v[0:nk, j, h * DK_FOX:(h + 1) * DK_FOX],
                                 pT[0:nk, n % 2, j, 0:nq], start=(j == 0), stop=(j == i))
            last.then_inc(s.mixed, 1)

        @block.tensor
        def _(pe):
            for n in range(len(steps) + 2):
                if n < len(steps):
                    score(pe, n)
                if 1 <= n <= len(steps):
                    turn(pe, n - 1)
                if n >= 2:
                    mix(pe, n - 2)

        @block.vector
        def _(dve):
            for n in range(len(steps) + 2):
                if n < len(steps):
                    h, i = steps[n]
                    t0, nq = TILES2[i]
                    nk = t0 + nq
                    b = n % 2
                    dve.wait_ge(s.scored, n + 1)
                    if n >= 2:
                        dve.wait_ge(s.summed, n - 1)
                    dve.tensor_tensor_reduce(sc[0:nq, b, 0:nk], k.bank[n % 2][0:nq, 0:nk],
                                             k.causal[0:nq, 2 * P - t0:2 * P - t0 + nk], 1.0, NEG, ALU.add, ALU.max,
                                             mx[0:nq, b:b + 1]).then_inc(s.maxed, 1)
                    dve.wait_ge(s.maxed, n + 1)
                    dve.tensor_scalar(nmx[0:nq, b:b + 1], mx[0:nq, b:b + 1], -1.0, None, ALU.mult).then_inc(s.negated, 1)
                if 1 <= n <= len(steps):
                    m = n - 1
                    h, i = steps[m]
                    t0, nq = TILES2[i]
                    nk = t0 + nq
                    b = m % 2
                    dve.wait_ge(s.summed, m + 1)
                    dve.reciprocal(inv[0:nq, b:b + 1], total[0:nq, b:b + 1]).then_inc(s.rcp, 1)
                    dve.wait_ge(s.rcp, m + 1)
                    dve.tensor_scalar(pr[0:nq, b, 0:nk], pr[0:nq, b, 0:nk], inv[0:nq, b:b + 1], None, ALU.mult).then_inc(s.normed, 1)
                if n >= 2 and steps[n - 2][1] == 2 and steps[n - 2][0] % 2 == 1:
                    pair = steps[n - 2][0] // 2
                    dve.wait_ge(s.mixed, n - 1)
                    dve.tensor_tensor(H[:, pair, 0:T2], k.bank[4 + pair % 2][:, 0:T2], gate[:, pair, :], ALU.mult).then_inc(s.gated, 1)

        @block.scalar
        def _(act):
            for n in range(len(steps) + 1):
                if n < len(steps):
                    h, i = steps[n]
                    t0, nq = TILES2[i]
                    nk = t0 + nq
                    b = n % 2
                    act.wait_ge(s.negated, n + 1)
                    if n >= 2:
                        act.wait_ge(s.turned, n - 1)
                    act.activation(pr[0:nq, b, 0:nk], sc[0:nq, b, 0:nk], ACT.Exp, bias=nmx[0:nq, b:b + 1],
                                   accum_out=total[0:nq, b:b + 1]).then_inc(s.summed, 1)
                if n >= 1:
                    m = n - 1
                    h, i = steps[m]
                    t0, nq = TILES2[i]
                    act.wait_ge(s.turned, m + 1)
                    if m >= 2:
                        act.wait_ge(s.mixed, m - 1)
                    for j in range(i + 1):
                        nk = TILES2[j][1]
                        last = act.copy(pT[0:nk, m % 2, j, 0:nq], k.bank[2 + m % 2][0:nk, j * P:j * P + nq])
                    last.then_inc(s.copied, 1)


def gla(k, a):
    H = k.H
    NH = 4
    with ExitStack() as es:
        q = sbuf(k, es, "q", [P, NH, T2])
        kk = sbuf(k, es, "k", [P, NH, T2])
        v = sbuf(k, es, "v", [P, 3, D])
        r = sbuf(k, es, "r", [P, KD, T2])
        low = sbuf(k, es, "low", [16, T2])
        b = sbuf(k, es, "b", [P, NH, T2])
        att = sbuf(k, es, "att", [P, 3, NH, T2])
        o = sbuf(k, es, "o", [P, KD, T2])
        alpha = sbuf(k, es, "alpha", [16, NH * P])
        x = lambda t: H[:, t, 0:T2]

        def evict(eng, c, bank, s):
            if c == 24:
                return copy(k, eng, low[:, :], bank[0:16, 0:T2])
            if 8 <= c < 16:
                c -= 8
                copy(k, eng, v[:, 0:2, c * P:(c + 1) * P], bank[:, 0:2 * P].rearrange("p (i n) -> p i n", i=2))
                return copy(k, eng, v[0:META, 2, c * P:(c + 1) * P], bank[0:META, 2 * P:3 * P])
            if c < NH:
                if eng is k.nc.scalar:
                    return eng.mul(q[:, c, :], bank[:, 0:T2], float(P) ** -0.5)
                return eng.tensor_scalar(q[:, c, :], bank[:, 0:T2], float(P) ** -0.5, None, ALU.mult)
            return copy(k, eng, kk[:, c - NH, :] if c < 8 else r[:, c - 16, :], bank[:, 0:T2])

        outs = [fm_out(x, T2) for _ in range(8)] + [tm_out(x, TILES2) for _ in range(8)]
        outs += [fm_out(x, T2) for _ in range(8)] + [fm_out(x, T2, m=16)]
        project(k, "gla_in", outs, None, evict)

        with ExitStack() as es2, stage(k, "gla_gates", "alpha made order ready expd lned") as (block, s):
            tmp = sbuf(k, es2, "tmp", [P, NH, T2])
            z = sbuf(k, es2, "z", [P, NH, T2])

            @block.sync
            def _(sp):
                sp.dma_start(alpha[:, :], a.gla_w_alpha2_2[0]).then_inc(s.alpha, 16)

            @block.tensor
            def _(pe):
                pe.wait_ge(s.alpha, 16)
                for h in range(NH):
                    last = pe.matmul(k.bank[h][:, 0:T2], alpha[:, h * P:(h + 1) * P], low[:, :], start=True, stop=True)
                last.then_inc(s.made, 1)

            @block.vector
            def _(dve):
                order = Order(dve, s.order)
                bias = k.small("gla_b_alpha_2")
                dve.wait_ge(s.made, 1)
                for h in range(NH):
                    last = dve.tensor_scalar(z[:, h, :], k.bank[h][:, 0:T2], bias[:, h:h + 1], None, ALU.add)
                order(last)
                dve.scalar_tensor_tensor(out=tmp[:, :, :], in0=z[:, :, :], scalar=-1.0, in1=z[:, :, :], op0=ALU.mult, op1=ALU.max).then_inc(s.ready, 1)
                dve.wait_ge(s.lned, 1)
                order(dve.tensor_scalar(z[:, :, :], z[:, :, :], 0.0, None, ALU.min))
                order(dve.tensor_tensor(z[:, :, :], z[:, :, :], tmp[:, :, :], ALU.subtract))
                order(dve.tensor_scalar(z[:, :, :], z[:, :, :], 1.0 / 16.0, None, ALU.mult))
                one = k.ones[:, 0:1].broadcast_to([P, T2])
                for h in range(NH):
                    last = dve.tensor_tensor_scan(b[:, h, :], one, z[:, h, :], 0.0, ALU.mult, ALU.add)
                order(last)

            @block.scalar
            def _(act):
                act.wait_ge(s.ready, 1)
                act.activation(tmp[:, :, :], tmp[:, :, :], ACT.Exp, scale=-1.0).then_inc(s.expd, 1)
                act.wait_ge(s.expd, 1)
                act.activation(tmp[:, :, :], tmp[:, :, :], ACT.Ln, bias=k.one[:, 0:1]).then_inc(s.lned, 1)
                act.activation(r[:, :, :], r[:, :, :], ACT.Silu)

        gla_attention(k, q, kk, b, att)

        with ExitStack() as es2, stage(k, "gla_mix", "mixed act_took dve_took squares summed root order") as (block, s):
            sq = sbuf(k, es2, "sq", [P, KD, T2])
            rstd = sbuf(k, es2, "rstd", [P, NH, T2])

            @block.tensor
            def _(pe):
                for c in range(KD):
                    h = c // 2
                    for i, (s0, n) in enumerate(TILES2):
                        last = pe.matmul(k.bank[c][:, s0:T2], v[0:n, i, c * P:(c + 1) * P], att[0:n, i, h, s0:T2],
                                         start=(i == 0), stop=(i == 2))
                    last.then_inc(s.mixed, 1)
                pe.wait_ge(s.squares, KD)
                pe.wait_ge(s.dve_took, KD)
                for h in range(NH):
                    for c in range(2):
                        last = pe.matmul(k.bank[h][:, 0:T2], k.ones, sq[:, 2 * h + c, :], start=(c == 0), stop=(c == 1))
                last.then_inc(s.summed, 1)

            @block.scalar
            def _(act):
                for c in range(KD):
                    act.wait_ge(s.mixed, c + 1)
                    act.activation(sq[:, c, :], k.bank[c][:, 0:T2], ACT.Square).then_inc(s.squares, 1)
                act.wait_ge(s.summed, 1)
                for h in range(NH):
                    last = act.activation(rstd[:, h, :], k.bank[h][:, 0:T2], ACT.Sqrt, scale=1.0 / (2 * P), bias=k.eps[:, 0:1])
                last.then_inc(s.root, 1)

            @block.vector
            def _(dve):
                order = Order(dve, s.order)
                gain = k.small("gla_o_gain_2")
                for c in range(KD):
                    dve.wait_ge(s.squares, c + 1)
                    dve.scalar_tensor_tensor(out=o[:, c, :], in0=k.bank[c][:, 0:T2], scalar=gain[:, c % 2:c % 2 + 1],
                                             in1=r[:, c, :], op0=ALU.mult, op1=ALU.mult).then_inc(s.dve_took, 1)
                dve.wait_ge(s.dve_took, KD)
                dve.wait_ge(s.root, 1)
                order(dve.reciprocal(rstd[:, :, :], rstd[:, :, :]))
                for c in range(KD):
                    dve.tensor_tensor(H[:, c, 0:T2], o[:, c, :], rstd[:, c // 2, :], ALU.mult)
    project_residual_2(k, "gla_out", H[:, :, 0:T2])


def gla_attention(k, q, kk, b, att):
    NH = 4
    whole, full_tiles = T2, 2 * P
    steps = [("diag", 0)] + [("level", l) for l in range(LEVELS)] + [("cross", 0), ("cross", 1)]
    with ExitStack() as es, stage(k, "gla_attend", "apart decayed scaled scored took order") as (block, s):
        dif = sbuf(k, es, "dif", [P, 2, NH, T2])
        kh = sbuf(k, es, "kh", [P, 2, NH, T2])
        qh = sbuf(k, es, "qh", [P, 2, NH, T2])

        def spans(kind, l):
            if kind == "level":
                m = 1 << l
                n = whole if 2 * m <= META else full_tiles
                view = lambda ap, side: halves(ap[:, :, 0:n], m, side)
                return view, (lambda ap: view(ap, 0)[:, :, :, m - 1:m]), [P, NH, n // (2 * m), m], [P, NH, n // (2 * m), m]
            e = (l + 1) * P
            view = lambda ap, side: ap[:, :, l * P:e] if side == 0 else ap[:, :, e:T2]
            return view, (lambda ap: ap[:, :, e - 1:e]), [P, NH, P], [P, NH, T2 - e]

        def blocks(j):
            kind, l = steps[j]
            if kind == "cross":
                return [(0, P, 2 * P, P), (0, 2 * P, T2, P)] if l == 0 else [(1, 2 * P, T2, P)]
            tiles = TILES2 if kind == "diag" or (2 << l) <= META else TILES2[:2]
            return [(i, t0, t0 + n, n) for i, (t0, n) in enumerate(tiles)]

        def banks(j):
            return [k.bank[4 * (j % 2) + n] for n in range(3)]

        @block.gpsimd
        def _(pool):
            for j in range(1, len(steps)):
                view, middle, near, far = spans(*steps[j])
                if j >= 3:
                    pool.wait_ge(s.scaled, j - 1)
                out = dif[:, j % 2, :, :]
                pool.tensor_tensor(view(out, 0), middle(b[:, :, :]).broadcast_to(near), view(b[:, :, :], 0), ALU.subtract)
                pool.tensor_tensor(view(out, 1), view(b[:, :, :], 1), middle(b[:, :, :]).broadcast_to(far), ALU.subtract).then_inc(s.apart, 1)

        @block.scalar
        def _(act):
            for j in range(1, len(steps)):
                view, *_ = spans(*steps[j])
                act.wait_ge(s.apart, j)
                d = dif[:, j % 2, :, :]
                for side in range(2):
                    last = act.activation(view(d, side), view(d, side), ACT.Exp)
                last.then_inc(s.decayed, 1)

        @block.vector
        def _(dve):
            order = Order(dve, s.order)

            def factors(j):
                if j >= 2:
                    dve.wait_ge(s.scored, j - 1)
                ks, qs = kh[:, j % 2, :, :], qh[:, j % 2, :, :]
                if j == 0:
                    dve.tensor_copy(ks, kk[:, :, :])
                    dve.tensor_copy(qs, q[:, :, :]).then_inc(s.scaled, 1)
                    return
                view, *_ = spans(*steps[j])
                dve.wait_ge(s.decayed, j)
                d = dif[:, j % 2, :, :]
                dve.tensor_tensor(view(ks, 0), view(kk[:, :, :], 0), view(d, 0), ALU.mult)
                dve.tensor_tensor(view(qs, 1), view(q[:, :, :], 1), view(d, 1), ALU.mult).then_inc(s.scaled, 1)

            def take(j):
                kind, l = steps[j]
                dve.wait_ge(s.scored, j + 1)
                for n, (i, t0, t1, m) in enumerate(blocks(j)):
                    data = banks(j)[n][0:m, :].rearrange("p (h t) -> p h t", h=NH)[:, :, 0:t1 - t0]
                    out = att[0:m, i, :, t0:t1]
                    if kind == "level":
                        mask = k.fwd[0:m, l, 0:t1 - t0].bitcast(I32).unsqueeze(1).broadcast_to([m, NH, t1 - t0])
                        last = dve.copy_predicated(out, mask, data)
                    else:
                        last = dve.tensor_copy(out, data)
                last.then_inc(s.took, 1)
                dve.wait_ge(s.took, j + 1)

            def take_diag():
                dve.wait_ge(s.scored, 1)
                for n, (i, t0, t1, m) in enumerate(blocks(0)):
                    data = banks(0)[n][0:m, :].rearrange("p (h t) -> p h t", h=NH)[:, :, 0:t1 - t0]
                    mask = k.both[0:m, LEVELS, 0:t1 - t0].unsqueeze(1).broadcast_to([m, NH, t1 - t0])
                    last = dve.copy_predicated(att[0:m, i, :, t0:t1], mask, data)
                last.then_inc(s.took, 1)
                dve.wait_ge(s.took, 1)

            order(dve.memset(att[:, :, :, :], 0.0))
            order(dve.memset(kh[:, 1, :, :], 0.0))
            order(dve.memset(qh[:, 1, :, :], 0.0))
            factors(0)
            for j in range(1, len(steps)):
                factors(j)
                take_diag() if j - 1 == 0 else take(j - 1)
            take(len(steps) - 1)

        @block.tensor
        def _(pe):
            for j in range(len(steps)):
                pe.wait_ge(s.scaled, j + 1)
                if j >= 2:
                    pe.wait_ge(s.took, j - 1)
                for n, (i, t0, t1, m) in enumerate(blocks(j)):
                    s0 = TILES2[i][0]
                    for h in range(NH):
                        last = pe.matmul(banks(j)[n][0:m, h * P:h * P + t1 - t0], kh[:, j % 2, h, s0:s0 + m],
                                         qh[:, j % 2, h, t0:t1], start=True, stop=True)
                last.then_inc(s.scored, 1)


def gdn(k, a):
    H = k.H
    NH = GDN_HEADS
    with ExitStack() as es:
        qkv = sbuf(k, es, "qkv", [P, 24, T2])
        gate = sbuf(k, es, "gate", [P, NH, T2])
        rows = sbuf(k, es, "rows", [NH, 6, T2])
        o = sbuf(k, es, "o", [P, NH, T2])
        with ExitStack() as es1:
            raw = sbuf(k, es1, "raw", [P, 24, T2])
            x = lambda t: H[:, t, 0:T2]

            def evict(eng, c, bank, s):
                if c >= 32:
                    return copy(k, eng, rows[:, c - 32, :], bank[0:NH, 0:T2])
                return copy(k, eng, raw[:, c, :] if c < 24 else gate[:, c - 24, :], bank[:, 0:T2])

            outs = [fm_out(x, T2) for _ in range(32)] + [fm_out(x, T2, m=NH) for _ in range(2)]
            project(k, "gdn_in", outs, None, evict)
            gdn_conv(k, raw, qkv)
        head_norms(k, "q_norm", qkv, range(0, NH), k.ones, P, factor=float(P) ** -0.5, mean=False)
        head_norms(k, "k_norm", qkv, range(NH, 2 * NH), k.ones, P, mean=False)

        with ExitStack() as es2, stage(k, "gdn_gates", "ready lned expd order done") as (block, s):
            tmp = sbuf(k, es2, "tmp", [NH, T2])
            ea = sbuf(k, es2, "ea", [NH, 1])

            @block.vector
            def _(dve):
                order = Order(dve, s.order)
                order(dve.tensor_scalar(rows[:, 0, :], rows[:, 0, :], k.gdn_ab[:, 1:2], None, ALU.add))
                dve.scalar_tensor_tensor(out=tmp[:, :], in0=rows[:, 0, :], scalar=-1.0, in1=rows[:, 0, :], op0=ALU.mult, op1=ALU.max).then_inc(s.ready, 1)
                dve.wait_ge(s.lned, 1)
                order(dve.scalar_tensor_tensor(out=rows[:, 0, :], in0=rows[:, 0, :], scalar=0.0, in1=tmp[:, :], op0=ALU.max, op1=ALU.add))
                order(dve.tensor_scalar(rows[:, 0, :], rows[:, 0, :], ea[:, 0:1], -1.0, ALU.mult, ALU.mult))
                for t0, n in TILES2:
                    last = dve.tensor_tensor_scan(rows[:, 2, t0:t0 + n], k.ones[0:NH, 0:1].broadcast_to([NH, n]),
                                                  rows[:, 0, t0:t0 + n], 0.0, ALU.mult, ALU.add)
                order(last)
                order(dve.tensor_scalar(rows[:, 3, :], rows[:, 2, :], -1.0, None, ALU.mult))

            @block.scalar
            def _(act):
                act.activation(ea[:, :], k.gdn_ab[:, 0:1], ACT.Exp)
                act.wait_ge(s.ready, 1)
                act.activation(tmp[:, :], tmp[:, :], ACT.Exp, scale=-1.0).then_inc(s.expd, 1)
                act.wait_ge(s.expd, 1)
                act.activation(tmp[:, :], tmp[:, :], ACT.Ln, bias=k.one[0:NH, 0:1]).then_inc(s.lned, 1)
                act.activation(rows[:, 1, :], rows[:, 1, :], ACT.Sigmoid)
                act.activation(gate[:, :, :], gate[:, :, :], ACT.Silu)

        with ExitStack() as es3:
            state = sbuf(k, es3, "state", [P, NH, P])
            for i in range(3):
                gdn_tile(k, i, qkv, rows, state, o)
        head_norms(k, "o_norm", o, range(NH), k.ones, P, gain=lambda c: k.small("gdn_o_gain_2")[:, 0:1])
        with stage(k, "gdn_gate", "order") as (block, s):
            @block.vector
            def _(dve):
                dve.tensor_tensor(H[:, :, 0:T2], o[:, :, :], gate[:, :, :], ALU.mult)
    project_residual_2(k, "gdn_out", H[:, :, 0:T2])


def gdn_conv(k, raw, out):
    with stage(k, "gdn_conv", "convolved order") as (block, s):
        w = k.small("gdn_conv_w_2").rearrange("p (tap c) -> p tap c", tap=4)

        @block.vector
        def _(dve):
            order = Order(dve, s.order)
            for g in range(6):
                cs = range(4 * g, 4 * g + 4)
                for c in cs:
                    last = dve.tensor_scalar(out[:, c, :], raw[:, c, :], w[:, 3, c:c + 1], None, ALU.mult)
                order(last)
                for back in (1, 2, 3):
                    for c in cs:
                        last = dve.scalar_tensor_tensor(out=out[:, c, back:T2], in0=raw[:, c, 0:T2 - back], scalar=w[:, 3 - back, c:c + 1],
                                                        in1=out[:, c, back:T2], op0=ALU.mult, op1=ALU.add)
                    if back < 3:
                        order(last)
                last.then_inc(s.convolved, 1)

        @block.scalar
        def _(act):
            for g in range(6):
                act.wait_ge(s.convolved, g + 1)
                act.activation(out[:, 4 * g:4 * g + 4, :], out[:, 4 * g:4 * g + 4, :], ACT.Silu)


def gdn_tile(k, i, qkv, rows, state, o):
    NH = GDN_HEADS
    t0, n = TILES2[i]
    levels = LEVELS if n == P else 4
    cols = slice(t0, t0 + n)
    q, kk, v = (qkv[:, c * NH:(c + 1) * NH, cols] for c in range(3))
    G = 2

    with ExitStack() as es:
        kb = sbuf(k, es, "kb", [P, NH, P])
        kg = sbuf(k, es, "kg", [P, NH, P])
        qg = sbuf(k, es, "qg", [P, NH, P])
        last_decay = sbuf(k, es, "last_decay", [P, NH])
        kT = sbuf(k, es, "kT", [P, NH, P])
        vT = sbuf(k, es, "vT", [P, NH, P])
        A = sbuf(k, es, "A", [P, NH, P])
        U = sbuf(k, es, "U", [P, NH, P])
        X = sbuf(k, es, "X", [P, NH, P])
        XT = sbuf(k, es, "XT", [P, NH, P])
        four = lambda ap, g: ap[:, 4 * g:4 * g + 4, :]
        bank4 = lambda n_bank, m: k.bank[n_bank][0:m, :].rearrange("p (h t) -> p h t", h=4)

        with ExitStack() as es1, stage(k, "gdn_a", "spread beta grown apart faded order made products turned done") as (block, s):
            EB = sbuf(k, es1, "EB", [P, NH, P])
            BB = sbuf(k, es1, "BB", [P, NH, P])
            kd = sbuf(k, es1, "kd", [P, NH, P])
            vb = sbuf(k, es1, "vb", [P, NH, P])
            fade = sbuf(k, es1, "fade", [P, NH, P])
            bl = sbuf(k, es1, "bl", [P, NH])

            @block.tensor
            def _(pe):
                for h in range(NH):
                    pick = k.ident[0:NH, h:h + 1]
                    at = slice((h % 4) * P, (h % 4) * P + n)
                    g = h // 4
                    pe.matmul(k.bank[g][:, at], pick.broadcast_to([NH, P]), rows[:, 2, cols], start=True, stop=True)
                    pe.matmul(k.bank[2 + g][:, at], pick.broadcast_to([NH, P]), rows[:, 1, cols], start=True, stop=True)
                    pe.matmul(k.bank[4 + g][0:n, at], pick.broadcast_to([NH, n]), rows[:, 2, cols], start=True, stop=False)
                    last = pe.matmul(k.bank[4 + g][0:n, at], rows[:, 3, cols], pick.broadcast_to([NH, n]), start=False, stop=True)
                last.then_inc(s.spread, 1)
                pe.wait_ge(s.made, 1)
                for h in range(NH):
                    at = slice((h % 4) * P, (h % 4) * P + n)
                    pe.matmul(k.bank[6 + h // 4][0:n, at], kk[:, h, :], kb[:, h, 0:n], start=True, stop=True)
                    last = pe.matmul(k.bank[2 + h // 4][0:n, at], kk[:, h, :], q[:, h, :], start=True, stop=True)
                last.then_inc(s.products, 1)
                pe.wait_ge(s.made, 2)
                for h in range(NH):
                    at = slice((h % 4) * P, (h % 4 + 1) * P)
                    pe.transpose(k.bank[0 + h // 4][0:n, at], kd[:, h, 0:n], k.ident)
                    last = pe.transpose(k.bank[4 + h // 4][0:n, at], vb[:, h, 0:n], k.ident)
                last.then_inc(s.turned, 1)

            @block.scalar
            def _(act):
                act.wait_ge(s.spread, 1)
                for g in range(G):
                    act.activation(four(EB, g)[:, :, 0:n], bank4(g, P)[:, :, 0:n], ACT.Exp)
                    last = act.copy(four(BB, g)[:, :, 0:n], bank4(2 + g, P)[:, :, 0:n])
                last.then_inc(s.grown, 1)
                act.wait_ge(s.apart, 1)
                act.activation(fade[0:n, :, 0:n], fade[0:n, :, 0:n], ACT.Exp).then_inc(s.faded, 1)
                act.wait_ge(s.apart, 2)
                act.activation(kd[:, :, 0:n], kd[:, :, 0:n], ACT.Exp).then_inc(s.faded, 1)
                act.activation(last_decay[:, :], bl[:, :], ACT.Exp)

            @block.vector
            def _(dve):
                order = Order(dve, s.order)
                dve.wait_ge(s.spread, 1)
                incl = k.const("decay_incl")[0:n, 0:n].unsqueeze(1).broadcast_to([n, 4, n])
                for g in range(G):
                    last = dve.tensor_tensor(fade[0:n, 4 * g:4 * g + 4, 0:n], bank4(4 + g, n)[:, :, 0:n], incl, ALU.add)
                last.then_inc(s.apart, 1)
                dve.wait_ge(s.grown, 1)
                for g in range(G):
                    last = dve.tensor_copy(bl[:, 4 * g:4 * g + 4], bank4(g, P)[:, :, n - 1])
                order(last)
                for g in range(G):
                    last = dve.tensor_tensor(four(kd, g)[:, :, 0:n], bl[:, 4 * g:4 * g + 4].unsqueeze(2).broadcast_to([P, 4, n]),
                                             bank4(g, P)[:, :, 0:n], ALU.subtract)
                last.then_inc(s.apart, 1)
                order(dve.tensor_tensor(kb[:, :, 0:n], kk, BB[:, :, 0:n], ALU.mult))
                dve.tensor_tensor(vb[:, :, 0:n], v, BB[:, :, 0:n], ALU.mult).then_inc(s.made, 1)
                dve.tensor_tensor(qg[:, :, 0:n], q, EB[:, :, 0:n], ALU.mult)
                dve.tensor_tensor(kg[:, :, 0:n], kb[:, :, 0:n], EB[:, :, 0:n], ALU.mult)
                dve.wait_ge(s.faded, 2)
                dve.tensor_tensor(kd[:, :, 0:n], kd[:, :, 0:n], kk, ALU.mult).then_inc(s.made, 1)
                dve.wait_ge(s.products, 1)
                strict = k.const("decay_strict")[0:n, 0:n].unsqueeze(1).broadcast_to([n, 4, n])
                for g in range(G):
                    f4 = fade[0:n, 4 * g:4 * g + 4, 0:n]
                    dve.tensor_tensor(A[0:n, 4 * g:4 * g + 4, 0:n], bank4(2 + g, n)[:, :, 0:n], f4, ALU.mult)
                    last = dve.tensor_tensor(U[0:n, 4 * g:4 * g + 4, 0:n], bank4(6 + g, n)[:, :, 0:n], f4, ALU.mult)
                order(last)
                for g in range(G):
                    u4 = U[0:n, 4 * g:4 * g + 4, 0:n]
                    dve.tensor_tensor(u4, u4, strict, ALU.mult)
                dve.wait_ge(s.turned, 1)
                for g in range(G):
                    dve.tensor_copy(kT[0:n, 4 * g:4 * g + 4, :], bank4(g, n))
                    dve.tensor_copy(vT[0:n, 4 * g:4 * g + 4, :], bank4(4 + g, n))
                eye = k.ident[0:n, 0:n].unsqueeze(1).broadcast_to([n, NH, n])
                dve.tensor_copy(X[0:n, :, 0:n], eye)
                dve.tensor_copy(XT[0:n, :, 0:n], eye)

        with ExitStack() as es1, stage(k, "gdn_inverse", "masked lower copied twice took") as (block, s):
            UM = sbuf(k, es1, "UM", [P, NH, P])
            Z = sbuf(k, es1, "Z", [P, NH, P])
            steps = [(l, g) for l in range(levels) for g in range(G)]
            grp = lambda ap, g: ap[0:n, 4 * g:4 * g + 4, 0:n]

            @block.gpsimd
            def _(pool):
                for j, (l, g) in enumerate(steps):
                    if j >= G:
                        pool.wait_ge(s.lower, j - G + 1)
                    mask = k.fwd[0:n, l, 0:n].unsqueeze(1).broadcast_to([n, 4, n])
                    pool.tensor_tensor(grp(UM, g), grp(U, g), mask, ALU.mult).then_inc(s.masked, 1)

            @block.tensor
            def _(pe):
                def lower(j):
                    l, g = steps[j]
                    pe.wait_ge(s.masked, j + 1)
                    if j >= G:
                        pe.wait_ge(s.took, j - G + 1)
                    for h in range(4):
                        last = pe.matmul(k.bank[g][0:n, h * P:h * P + n], UM[0:n, 4 * g + h, 0:n], X[0:n, 4 * g + h, 0:n],
                                         start=True, stop=True)
                    last.then_inc(s.lower, 1)

                def twice(j):
                    l, g = steps[j]
                    pe.wait_ge(s.copied, j + 1)
                    for h in range(4):
                        hh = 4 * g + h
                        pe.matmul(k.bank[2 + g][0:n, h * P:h * P + n], XT[0:n, hh, 0:n], Z[0:n, hh, 0:n], start=True, stop=True)
                        last = pe.matmul(k.bank[4 + g][0:n, h * P:h * P + n], Z[0:n, hh, 0:n], XT[0:n, hh, 0:n], start=True, stop=True)
                    last.then_inc(s.twice, 1)

                for j in range(0, len(steps), G):
                    for g in range(G):
                        lower(j + g)
                    for g in range(G):
                        twice(j + g)

            @block.scalar
            def _(act):
                for j, (l, g) in enumerate(steps):
                    act.wait_ge(s.lower, j + 1)
                    if j >= G:
                        act.wait_ge(s.twice, j - G + 1)
                    act.copy(grp(Z, g), bank4(g, n)[:, :, 0:n]).then_inc(s.copied, 1)

            @block.vector
            def _(dve):
                for j, (l, g) in enumerate(steps):
                    dve.wait_ge(s.twice, j + 1)
                    dve.tensor_tensor(grp(X, g), grp(X, g), bank4(2 + g, n)[:, :, 0:n], ALU.subtract)
                    dve.tensor_tensor(grp(XT, g), grp(XT, g), bank4(4 + g, n)[:, :, 0:n], ALU.subtract).then_inc(s.took, 1)
                    dve.wait_ge(s.took, j + 1)

        with ExitStack() as es1, stage(k, "gdn_step", "read rest solved new mixed updated order") as (block, s):
            R = sbuf(k, es1, "R", [P, NH, P])
            new = sbuf(k, es1, "new", [P, NH, P])

            @block.tensor
            def _(pe):
                if i > 0:
                    for h in range(NH):
                        last = pe.matmul(k.bank[h // 4][0:n, (h % 4) * P:(h % 4 + 1) * P], kg[:, h, 0:n], state[:, h, :], start=True, stop=True)
                    last.then_inc(s.read, 1)
                pe.wait_ge(s.rest, 1)
                for h in range(NH):
                    last = pe.matmul(k.bank[2 + h // 4][0:n, (h % 4) * P:(h % 4 + 1) * P], XT[0:n, h, 0:n], R[0:n, h, :], start=True, stop=True)
                last.then_inc(s.solved, 1)
                pe.wait_ge(s.new, 1)
                for h in range(NH):
                    out = k.bank[4 + h // 4][:, (h % 4) * P:(h % 4) * P + n]
                    last = pe.matmul(out, new[0:n, h, :], A[0:n, h, 0:n], start=True, stop=(i == 0))
                    if i > 0:
                        last = pe.matmul(out, state[:, h, :], qg[:, h, 0:n], start=False, stop=True)
                last.then_inc(s.mixed, 1)
                if i < 2:
                    for h in range(NH):
                        last = pe.matmul(k.bank[6 + h // 4][:, (h % 4) * P:(h % 4 + 1) * P], kT[0:n, h, :], new[0:n, h, :], start=True, stop=True)
                    last.then_inc(s.updated, 1)

            @block.vector
            def _(dve):
                order = Order(dve, s.order)
                if i > 0:
                    dve.wait_ge(s.read, 1)
                for g in range(G):
                    r4, v4 = R[0:n, 4 * g:4 * g + 4, :], vT[0:n, 4 * g:4 * g + 4, :]
                    if i > 0:
                        last = dve.tensor_tensor(r4, v4, bank4(g, n), ALU.subtract)
                    else:
                        last = dve.tensor_copy(r4, v4)
                last.then_inc(s.rest, 1)
                dve.wait_ge(s.solved, 1)
                for g in range(G):
                    last = dve.tensor_copy(new[0:n, 4 * g:4 * g + 4, :], bank4(2 + g, n))
                last.then_inc(s.new, 1)
                dve.wait_ge(s.mixed, 1)
                for g in range(G):
                    dve.tensor_copy(o[:, 4 * g:4 * g + 4, cols], bank4(4 + g, P)[:, :, 0:n])
                if i == 0:
                    dve.wait_ge(s.updated, 1)
                    for g in range(G):
                        dve.tensor_copy(state[:, 4 * g:4 * g + 4, :], bank4(6 + g, P))
                if i == 1:
                    dve.wait_ge(s.updated, 1)
                    order(dve.tensor_tensor(state[:, :, :], state[:, :, :], last_decay[:, :].unsqueeze(2).broadcast_to([P, NH, P]), ALU.mult))
                    for g in range(G):
                        dve.tensor_tensor(state[:, 4 * g:4 * g + 4, :], state[:, 4 * g:4 * g + 4, :], bank4(6 + g, P), ALU.add)


def swiglu(k):
    H = k.H
    with ExitStack() as es:
        hidden = sbuf(k, es, "hidden", [P, KF, T2])
        gate = sbuf(k, es, "gate", [P, 2, T2])
        x = lambda t: H[:, t, 0:T2]

        def evict(eng, c, bank, s):
            j = c // 2
            if c % 2 == 0:
                if j >= 2:
                    eng.wait_ge(s.dve_took, j - 1)
                return eng.activation(gate[:, j % 2, :], bank[:, 0:T2], ACT.Silu)
            eng.wait_ge(s.act_took, j + 1)
            return eng.tensor_tensor(hidden[:, j, :], gate[:, j % 2, :], bank[:, 0:T2], ALU.mult)

        project(k, "gate_up", [fm_out(x, T2) for _ in range(2 * KF)], None, evict)
        project_residual_2(k, "down", hidden[:, :, :], 3, KF)


def join_blocks(k, a):
    with stage(k, "meta", "loaded") as (block, s):
        @block.sync
        def _(sp):
            sp.dma_start(k.Y[:, :, 0:META], a.meta).then_inc(s.loaded, 16)
            sp.wait_ge(s.loaded, 16)
    g = k.small("final_g")
    rms_norm(k, "final", k.X[:, :, SEQ:TWO], SEQ, lambda c: [(0, SEQ, g[:, c:c + 1])], None, k.Y[:, :, META:T2])


def second_block(k, a):
    for i in range(4):
        g = k.small("norm_mix_2")[:, i * KD:(i + 1) * KD]
        rms_norm(k, "mix_norm", k.Y[:, :, :], T2, lambda c: [(0, T2, g[:, c:c + 1])], None, k.H[:, :, 0:T2])
        (lambda: fox(k, a, i // 3), lambda: gla(k, a), lambda: gdn(k, a))[i % 3]()
        g2 = k.small("norm_ffn_2")[:, i * KD:(i + 1) * KD]
        rms_norm(k, "ffn_norm", k.Y[:, :, :], T2, lambda c: [(0, T2, g2[:, c:c + 1])], None, k.H[:, :, 0:T2])
        swiglu(k)



def build(nc, a, out, debug=None):
    k = Program(nc)
    with ExitStack() as es:
        k.small_sb = sbuf(k, es, "small", [P, N_SMALL])
        k.const_sb = sbuf(k, es, "const", [P, N_CONST])
        both = sbuf(k, es, "both", [P, LEVELS + 1, P], I32)
        k.fox_b = sbuf(k, es, "fox_b", [FOX_HEADS, 2])
        k.gdn_ab = sbuf(k, es, "gdn_ab", [GDN_HEADS, 2])
        k.X = sbuf(k, es, "X", [P, KD, TWO])
        k.H = sbuf(k, es, "H", [P, KD, TWO])
        k.ring = sbuf(k, es, "ring", [P, RING, D])
        k.mods = sbuf(k, es, "mods", [P, DEPTH, 48, 2])
        k.gain = sbuf(k, es, "gain", [P, DEPTH, 2, KD, 2])
        k.lower = sbuf(k, es, "lower", [P, DEPTH, 8])
        k.upper = sbuf(k, es, "upper", [P, DEPTH, 8])
        k.back_total = sbuf(k, es, "back_total", [P, HG_HEADS])
        k.qgain = sbuf(k, es, "qgain", [P, 1])
        k.eps = sbuf(k, es, "eps", [P, 1])
        k.one = sbuf(k, es, "one", [P, 1])
        k.bank = [es.enter_context(nc.psum_tensor(f"bank{i}", [P, 512], F32)) for i in range(BANKS)]
        k.small = lambda name: k.small_sb[:, SMALL[name][0]:SMALL[name][0] + SMALL[name][1]]
        k.const = lambda name: k.const_sb[:, CONST[name][0]:CONST[name][0] + CONST[name][1]]
        k.ident, k.ones, k.ones64, k.causal = (k.const(n) for n in ("ident", "ones", "ones64", "causal"))
        k.fwd = k.const("fwd").rearrange("p (l n) -> p l n", l=LEVELS)
        k.both = both
        k.landed = [nc.alloc_semaphore(f"landed{i}") for i in range(RING)]
        k.unit_done = nc.alloc_semaphore("unit_done")
        k.stored = nc.alloc_semaphore("stored")
        k.units = plan_weights(a)

        with stage(k, "load", "loaded") as (block, s):
            @block.sync
            def _(sp):
                for dst, src in ((k.small_sb[:, :], a.small), (k.const_sb[:, :], a.const), (both[:, :, :], a.both),
                                 (k.fox_b[:, :], a.fox_b), (k.gdn_ab[:, :], a.gdn_ab), (k.X[:, :, :], a.tokens)):
                    sp.dma_start(dst, src).then_inc(s.loaded, 16)
                for u in range(RING):
                    load_unit(k, sp, u)
                sp.wait_ge(s.loaded, 16 * 6)

            @block.vector
            def _(dve):
                dve.memset(k.eps[:, :], EPS)
                dve.memset(k.one[:, :], 1.0)

        if debug is not None:
            debug(k, a, out)
            return
        first_block(k, a)
        k.Y = sbuf(k, es, "Y", [P, KD, T2])
        join_blocks(k, a)
        second_block(k, a)
        store(k, k.Y[:, :, META:T2], out)


def store(k, src, out):
    with stage(k, "store", "") as (block, s):
        @block.sync
        def _(sp):
            sp.dma_start(out, src).then_inc(k.stored, 16)
            sp.wait_ge(k.stored, 16)


def features(v):
    return np.asarray(v).reshape(-1, P).T


def weights(w, cols=None):
    w = np.asarray(w)
    *lead, K, N = w.shape
    w = w.reshape(*lead, K // P, P, N // P, P)
    n = len(lead)
    return np.ascontiguousarray(w.transpose(*range(n), n + 2, n + 1, n, n + 3).reshape(*lead, N // P, P, K))


def narrow(w):
    w = np.asarray(w)
    *lead, K, n = w.shape
    d = len(lead)
    return np.ascontiguousarray(w.reshape(*lead, K // P, P, n).transpose(*range(d), d + 1, d, d + 2).reshape(*lead, P, K // P * n))


def lay_out(i):
    A = {}
    i = {n: np.asarray(v) for n, v in i.items()}
    small = np.empty((P, N_SMALL), np.float32)
    twice = lambda v: np.concatenate([v, v], axis=-1)
    for name, (at, n) in SMALL.items():
        v = twice(i[name]) if name.startswith("fox_") else i[name]
        small[:, at:at + n] = features(v)
    A["small"] = small
    const, both, _ = constants()
    A["const"], A["both"] = const, both.reshape(P, LEVELS + 1, P)
    A["fox_b"] = np.ascontiguousarray(i["fox_b_f_2"].T)
    A["gdn_ab"] = np.ascontiguousarray(np.concatenate([i["gdn_a_log_2"], i["gdn_dt_bias_2"]]).T)
    fm = lambda x: np.ascontiguousarray(x.T.reshape(KD, P, -1).transpose(1, 0, 2))
    A["tokens"] = fm(np.concatenate([i["ctx"][0], i["x"][0]]))
    A["meta"] = fm(i["meta_tokens_2"])
    for name in ("w_mod", "w_in", "w_out", "peer_wq", "w_gate_up_2", "w_down_2", "fox_w_out_2", "gla_w_out_2", "gdn_w_out_2"):
        A[name] = weights(i[name])
    for name, n, extra in (("fox_w_in_2", 4 * D, "fox_w_f"), ("gla_w_in_2", 3 * D, "gla_w_a"), ("gdn_w_in_2", 4 * D, "gdn_w_ab")):
        A[name] = weights(i[name][:, :, :n])
        over = i[name][:, :, n:]
        A[extra] = np.stack([narrow(over[:, :, c:c + 8]) for c in (0, 8)], 1) if extra == "gdn_w_ab" else narrow(over)[:, None]
    A["gla_w_alpha2_2"] = np.ascontiguousarray(i["gla_w_alpha2_2"])
    sk = i["peer_subkeys"]
    A["peer_subkeys"] = np.ascontiguousarray(sk.reshape(DEPTH, 2 * PEER_HEADS, N_KEYS, P).transpose(0, 3, 1, 2))
    for l in range(DEPTH):
        A[f"peer_u{l}"], A[f"peer_v{l}"] = np.ascontiguousarray(i["peer_u"][l]), np.ascontiguousarray(i["peer_v"][l])
    return A


def declare(nc, A):
    aps = {n: nc.dram_tensor(f"in_{n}", v.shape, mybir.dt.from_np(v.dtype), kind="ExternalInput").ap() for n, v in A.items()}
    aps["peer_u"] = [aps[f"peer_u{l}"] for l in range(DEPTH)]
    aps["peer_v"] = [aps[f"peer_v{l}"] for l in range(DEPTH)]
    return namedtuple("Inputs", list(aps))(**aps)


def kernel(**inputs):
    import concourse.bacc as bacc
    from concourse.bass_utils import run_bass_kernel_spmd as run

    nc = bacc.Bacc("TRN2", target_bir_lowering=False, num_devices=1)
    A = lay_out(inputs)
    a = declare(nc, A)
    out = nc.dram_tensor("out", (P, KD, SEQ), F32, kind="ExternalOutput").ap()
    build(nc, a, out)
    r = run(nc, [{f"in_{n}": v for n, v in A.items()}], core_ids=[0])
    y = np.asarray(r.results[0]["out"])
    return np.ascontiguousarray(y.transpose(2, 1, 0).reshape(1, SEQ, D))
```

```python
import numpy as np
from collections import namedtuple
from contextlib import ExitStack, contextmanager

import concourse.bass as bass
from concourse import mybir
from concourse.alu_op_type import AluOpType as ALU

F32 = mybir.dt.float32
F32R = mybir.dt.float32r
I32 = mybir.dt.int32
U32 = mybir.dt.uint32
ACT = mybir.ActivationFunctionType
AX = mybir.AxisListType.X

P = 128
D = 1024
KD = D // P
EPS = 1e-6
LN2 = float(np.log(2.0))

SEQ = 256
TWO = 2 * SEQ
DEPTH = 2
N_MOD = 6
HG_HEADS = 4
GRID_W = 64
PEER_HEADS = 8
TOPK = 16
N_KEYS = 128
SEL = PEER_HEADS * TOPK
LEVELS = 7

META = 16
T2 = META + SEQ
TILES2 = ((0, 128), (128, 128), (256, 16))
FOX_HEADS = 16
DK_FOX = 64
GDN_HEADS = 8
D_FF = 2816
KF = D_FF // P

RING = 6
SPLIT = 3
BANKS = 8
NEG = -1e30

SMALL = {}


def small_columns():
    at = 0
    for name, n in (("c_ctx", KD), ("c", KD), ("b_mod", DEPTH * 48), ("norm1_g", DEPTH * KD),
                    ("norm2_g", DEPTH * KD), ("conv_w", DEPTH * 12), ("lb_logits", DEPTH * 8),
                    ("final_g", KD), ("norm_mix_2", 4 * KD), ("norm_ffn_2", 4 * KD),
                    ("fox_q_gain_2", 2), ("fox_k_gain_2", 2), ("gla_b_alpha_2", 4),
                    ("gla_o_gain_2", 2), ("gdn_conv_w_2", 96), ("gdn_o_gain_2", 1)):
        SMALL[name] = (at, n)
        at += n
    return at


N_SMALL = small_columns()

CONST = {}


def const_columns():
    at = 0
    for name, n in (("ident", P), ("ones", P), ("ones64", P), ("causal", 3 * P), ("decay_incl", P),
                    ("decay_strict", P), ("fwd", LEVELS * P), ("iota", TOPK)):
        CONST[name] = (at, n)
        at += n
    return at


N_CONST = const_columns()


def constants():
    c = np.zeros((P, N_CONST), np.float32)

    def put(name, value):
        a, n = CONST[name]
        c[:, a:a + n] = value

    i = np.arange(P)
    put("ident", np.eye(P))
    put("ones", 1.0)
    put("ones64", (i[:, None] // 64) == (i[None, :] // 64))
    put("causal", np.concatenate([np.zeros((P, 2 * P)), np.where(i[None, :] > i[:, None], NEG, 0.0)], 1))
    put("decay_incl", np.where(i[:, None] > i[None, :], NEG, 0.0))
    put("decay_strict", np.where(i[:, None] < i[None, :], 1.0, 0.0))
    both = np.zeros((P, LEVELS + 1, P), np.int32)
    fwd = np.zeros((P, LEVELS, P), np.float32)
    for l in range(LEVELS):
        m = 1 << l
        same = (i[:, None] // (2 * m)) == (i[None, :] // (2 * m))
        left = (i // m) % 2 == 0
        fwd[:, l] = same & left[:, None] & ~left[None, :]
        both[:, l] = same & (left[:, None] != left[None, :])
    both[:, LEVELS] = np.eye(P)
    put("fwd", fwd.reshape(P, -1))
    put("iota", np.arange(TOPK)[None, :])
    scan = np.ones((P, 2, HG_HEADS, SEQ), np.float32)
    scan[:, :, :, 0] = 0.0
    return c, both.reshape(P, -1), scan.reshape(P, -1)


class Program:

    def __init__(self, nc):
        self.nc, self.stages, self.used = nc, 0, 0


@contextmanager
def stage(k, name, signals):
    k.stages += 1
    sems = [k.nc.alloc_semaphore(f"{name}_{s}_{k.stages}") for s in signals.split()]
    with k.nc.Block(no_gpsimd_drain=True) as block:
        yield block, namedtuple("Signals", signals)(*sems)
    if sems:
        k.nc.clear_and_free_semaphores(sems)
    k.nc.all_engine_barrier()


def sbuf(k, es, name, shape, dtype=F32):
    k.stages += 1
    return es.enter_context(k.nc.sbuf_tensor(f"{name}_{k.stages}", shape, dtype))


class Order:

    def __init__(self, eng, sem):
        self.eng, self.sem, self.n = eng, sem, 0

    def __call__(self, ins):
        self.n += 1
        ins.then_inc(self.sem, 1)
        self.eng.wait_ge(self.sem, self.n)



def plan_weights(a):
    units = []

    def chunks(w, order):
        for c in order:
            units.append((w[c], w.shape[-1]))

    for l in range(DEPTH):
        chunks(a.w_mod[l], range(48))
    for l in range(DEPTH):
        chunks(a.w_in[l], range(32))
        chunks(a.w_out[l], range(8))
        chunks(a.peer_wq[l], range(16))
    for i in range(4):
        kind, j = i % 3, i // 3
        w_in, extra, w_out = {0: (a.fox_w_in_2, a.fox_w_f, a.fox_w_out_2), 1: (a.gla_w_in_2, a.gla_w_a, a.gla_w_out_2),
                              2: (a.gdn_w_in_2, a.gdn_w_ab, a.gdn_w_out_2)}[kind]
        chunks(w_in[j], range(w_in.shape[1]))
        chunks(extra[j], range(extra.shape[1]))
        chunks(w_out[j], range(8))
        gate_up = a.w_gate_up_2[i]
        for c in range(KF):
            chunks(gate_up, (c, KF + c))
        for c in range(KD):
            for k0 in range(0, KF, KD):
                n = min(KD, KF - k0) * P
                units.append((a.w_down_2[i][c][:, k0 * P:k0 * P + n], n))
    return units


def load_unit(k, sp, u):
    if u < len(k.units):
        src, n = k.units[u]
        sp.dma_start(k.ring[:, u % RING, 0:n], src).then_inc(k.landed[u % RING], 16)


def project(k, name, outs, x, evict, by=None, extra="", finish=None, split_x=None):
    by = by or (lambda c: c % 2)
    first, n_units = k.used, sum(o[0] for o in outs)
    k.used += n_units
    KT, T = x.shape[1], x.shape[2]
    unit_of = []
    for c, o in enumerate(outs):
        unit_of += [(c, j) for j in range(o[0])]
    with ExitStack() as es, stage(k, name, "act_took dve_took x_high x_low w_high w_low " + extra) as (block, s):
        if split_x is None:
            high, low = (sbuf(k, es, n, [P, KT, T], F32R) for n in ("x_high", "x_low"))
        else:
            high, low = split_x
        w_high, w_low = (sbuf(k, es, n, [P, SPLIT, D], F32R) for n in ("w_high", "w_low"))
        took = (s.act_took, s.dve_took)

        def width(u):
            return k.units[first + u][1]

        @block.sync
        def _(sp):
            for u in range(n_units):
                sp.wait_ge(s.w_low, u + 1)
                load_unit(k, sp, first + u + RING)

        @block.tensor
        def _(pe):
            for u, (c, j) in enumerate(unit_of):
                n, m, t0, nt = outs[c]
                if j == 0 and c >= BANKS:
                    old = c - BANKS
                    pe.wait_ge(took[by(old)], sum(by(i) == by(old) for i in range(old + 1)))
                pe.wait_ge(s.w_low, u + 1)
                slot = u % SPLIT
                for i in range(min(KD, KT - j * KD)):
                    t = j * KD + i
                    if u == 0 and split_x is None:
                        pe.wait_ge(s.x_low, t + 1)
                    cols = slice(i * m, i * m + P)
                    for n_pass, (w, xx) in enumerate(((w_high, high), (w_high, low), (w_low, high))):
                        last = pe.matmul(k.bank[c % BANKS][:, 0:nt], w[:, slot, cols], xx[:, t, t0:t0 + nt],
                                         start=(t == 0 and n_pass == 0), stop=(t == KT - 1 and n_pass == 2))
                last.then_inc(k.unit_done, 1)

        def each(eng, mine, make, make_x, sem):
            made = 0
            for u, (c, j) in enumerate(unit_of):
                while made < min(n_units, u + SPLIT):
                    if made >= SPLIT:
                        eng.wait_ge(k.unit_done, first + made - SPLIT + 1)
                    make(made).then_inc(sem, 1)
                    made += 1
                    if made == 1 and split_x is None:
                        for t in range(KT):
                            make_x(t)
                if j == outs[c][0] - 1 and by(c) == mine:
                    eng.wait_ge(k.unit_done, first + u + 1)
                    evict(eng, c, k.bank[c % BANKS], s).then_inc(took[mine], 1)
            if finish is not None:
                finish(eng, s)

        @block.scalar
        def _(act):
            def make(u):
                act.wait_ge(k.landed[(first + u) % RING], 16 * ((first + u) // RING + 1))
                return act.copy(w_high[:, u % SPLIT, 0:width(u)], k.ring[:, (first + u) % RING, 0:width(u)])

            each(act, 0, make, lambda t: act.copy(high[:, t, :], x[:, t, :]).then_inc(s.x_high, 1), s.w_high)

        @block.vector
        def _(dve):
            def make(u):
                dve.wait_ge(s.w_high, u + 1)
                n = width(u)
                return dve.tensor_tensor(w_low[:, u % SPLIT, 0:n], k.ring[:, (first + u) % RING, 0:n],
                                         w_high[:, u % SPLIT, 0:n].bitcast(F32), ALU.subtract)

            def make_x(t):
                dve.wait_ge(s.x_high, t + 1)
                dve.tensor_tensor(low[:, t, :], x[:, t, :], high[:, t, :].bitcast(F32), ALU.subtract).then_inc(s.x_low, 1)

            each(dve, 1, make, make_x, s.w_low)


def copy(k, eng, out, in_):
    if eng is k.nc.scalar:
        return eng.copy(out, in_)
    return eng.tensor_copy(out, in_)



def rms_norm(k, name, x, T, gain, shift, out, kd=KD):
    with ExitStack() as es, stage(k, name, "squares sum logged root scaled done") as (block, s):
        sq = sbuf(k, es, "sq", [P, kd, T])
        rstd = sbuf(k, es, "rstd", [P, T])
        bank = k.bank[0]

        @block.scalar
        def _(act):
            for c in range(kd):
                act.activation(sq[:, c, :], x[:, c, :], ACT.Square).then_inc(s.squares, 1)
            act.wait_ge(s.sum, 1)
            act.activation(rstd[:, :], bank[:, 0:T], ACT.Ln, scale=1.0 / (kd * P), bias=k.eps[:, 0:1]).then_inc(s.logged, 1)
            act.wait_ge(s.logged, 1)
            act.activation(rstd[:, :], rstd[:, :], ACT.Exp, scale=-0.5).then_inc(s.root, 1)
            if shift is not None:
                for c in range(kd):
                    act.wait_ge(s.scaled, c + 1)
                    for t0, n, b in shift(c):
                        last = act.activation(out[:, c, t0:t0 + n], out[:, c, t0:t0 + n], ACT.Identity, bias=b)
                last.then_inc(s.done, 1)

        @block.tensor
        def _(pe):
            for c in range(kd):
                pe.wait_ge(s.squares, c + 1)
                last = pe.matmul(bank[:, 0:T], k.ones, sq[:, c, :], start=(c == 0), stop=(c == kd - 1))
            last.then_inc(s.sum, 1)

        @block.vector
        def _(dve):
            dve.wait_ge(s.root, 1)
            for c in range(kd):
                for t0, n, g in gain(c):
                    last = dve.scalar_tensor_tensor(out=out[:, c, t0:t0 + n], in0=x[:, c, t0:t0 + n], scalar=g,
                                                    in1=rstd[:, t0:t0 + n], op0=ALU.mult, op1=ALU.mult)
                last.then_inc(s.scaled, 1)


def transpose_chunks(k, name, jobs):
    groups = [jobs[i:i + 4] for i in range(0, len(jobs), 4)]
    with stage(k, name, "turned act_took dve_took") as (block, s):

        @block.tensor
        def _(pe):
            for g, group in enumerate(groups):
                if g >= BANKS:
                    pe.wait_ge((s.act_took, s.dve_took)[g % 2], (g - BANKS) // 2 + 1)
                for i, (out, in_) in enumerate(group):
                    m, n = in_.shape
                    last = pe.transpose(k.bank[g % BANKS][0:n, i * P:i * P + m], in_, k.ident[0:m, 0:m])
                last.then_inc(s.turned, 1)

        def take(eng, mine, took):
            for g, group in enumerate(groups):
                if g % 2 == mine:
                    eng.wait_ge(s.turned, g + 1)
                    for i, (out, in_) in enumerate(group):
                        m, n = in_.shape
                        last = copy(k, eng, out, k.bank[g % BANKS][0:n, i * P:i * P + m])
                    last.then_inc(took, 1)

        @block.scalar
        def _(act):
            take(act, 0, s.act_took)

        @block.vector
        def _(dve):
            take(dve, 1, s.dve_took)



def modulation(k):
    with ExitStack() as es:
        cond = sbuf(k, es, "cond", [P, KD, 2])
        with stage(k, "cond", "done") as (block, s):
            @block.scalar
            def _(act):
                act.activation(cond[:, :, 0], k.small("c_ctx"), ACT.Silu)
                act.activation(cond[:, :, 1], k.small("c"), ACT.Silu).then_inc(s.done, 1)

        n_units, first = DEPTH * 48, k.used
        k.used += n_units
        with stage(k, "modulate", "took turned added") as (block, s):
            rows = sbuf(k, es, "rows", [2, 4, 4 * P])

            @block.sync
            def _(sp):
                for u in range(n_units):
                    sp.wait_ge(k.unit_done, u + 1)
                    load_unit(k, sp, u + RING)

            @block.tensor
            def _(pe):
                def turn(g):
                    pe.wait_ge(s.took, g + 1)
                    if g >= 2:
                        pe.wait_ge(s.added, g - 1)
                    for i in range(4):
                        last = pe.transpose(k.bank[4 + g % 2][:, 2 * i:2 * i + 2], rows[:, g % 4, i * P:(i + 1) * P], k.ident[0:2, 0:2])
                    last.then_inc(s.turned, 1)

                for g in range(n_units // 4):
                    if g >= 4:
                        pe.wait_ge(s.took, g - 3)
                    for i in range(4):
                        u = 4 * g + i
                        pe.wait_ge(k.landed[u % RING], 16 * (u // RING + 1))
                        for t in range(KD):
                            last = pe.matmul(k.bank[g % 4][0:2, i * P:(i + 1) * P], cond[:, t, :], k.ring[:, u % RING, t * P:(t + 1) * P],
                                             start=(t == 0), stop=(t == KD - 1))
                        last.then_inc(k.unit_done, 1)
                    if g >= 1:
                        turn(g - 1)
                turn(n_units // 4 - 1)

            @block.scalar
            def _(act):
                for g in range(n_units // 4):
                    act.wait_ge(k.unit_done, 4 * g + 4)
                    if g >= 4:
                        act.wait_ge(s.turned, g - 3)
                    act.copy(rows[:, g % 4, :], k.bank[g % 4][0:2, :]).then_inc(s.took, 1)

            @block.vector
            def _(dve):
                for g in range(n_units // 4):
                    dve.wait_ge(s.turned, g + 1)
                    l, c = divmod(4 * g, 48)
                    bias = k.small("b_mod")[:, 4 * g:4 * g + 4].unsqueeze(2).broadcast_to([P, 4, 2])
                    dve.tensor_tensor(k.mods[:, l, c:c + 4, :], k.bank[4 + g % 2][:, 0:8].rearrange("p (c q) -> p c q", q=2),
                                      bias, ALU.add).then_inc(s.added, 1)

    with ExitStack() as es, stage(k, "bounds", "order exps subs") as (block, s):
        lb = k.small("lb_logits").rearrange("p (l n) -> p l n", l=DEPTH)
        top = sbuf(k, es, "top", [P, 8])
        e = sbuf(k, es, "e", [P, DEPTH, 8])
        total = sbuf(k, es, "total", [P, 8])

        @block.vector
        def _(dve):
            order = Order(dve, s.order)
            for l in range(DEPTH):
                for n, (scale0, name) in enumerate(((8, "norm1_g"), (32, "norm2_g"))):
                    g = k.small(name)[:, l * KD:(l + 1) * KD].unsqueeze(2).broadcast_to([P, KD, 2])
                    dve.scalar_tensor_tensor(out=k.gain[:, l, n, :, :], in0=k.mods[:, l, scale0:scale0 + KD, :],
                                             scalar=1.0, in1=g, op0=ALU.add, op1=ALU.mult)
            order(dve.tensor_tensor(top[:, :], lb[:, 0, :], lb[:, 1, :], ALU.max))
            for l in range(DEPTH):
                dve.tensor_tensor(e[:, l, :], lb[:, l, :], top[:, :], ALU.subtract).then_inc(s.subs, 1)
            dve.wait_ge(s.exps, 1)
            order(dve.tensor_tensor(total[:, :], e[:, 0, :], e[:, 1, :], ALU.add))
            order(dve.reciprocal(total[:, :], total[:, :]))
            for l in range(DEPTH):
                order(dve.tensor_tensor(e[:, l, :], e[:, l, :], total[:, :], ALU.mult))
            order(dve.tensor_tensor(total[:, :], e[:, 0, :], e[:, 1, :], ALU.add))
            order(dve.tensor_tensor(k.lower[:, 0, :], e[:, 0, :], e[:, 0, :], ALU.subtract))
            order(dve.tensor_tensor(k.lower[:, 1, :], total[:, :], e[:, 0, :], ALU.subtract))
            order(dve.tensor_scalar(k.upper[:, :, :], k.lower[:, :, :], -1.0, 1.0, ALU.mult, ALU.add))

        @block.scalar
        def _(act):
            act.wait_ge(s.subs, 2)
            act.activation(e[:, :, :], e[:, :, :], ACT.Exp).then_inc(s.exps, 1)


def both_ways(gain):
    return lambda c: [(0, SEQ, gain(c)[:, 0:1]), (SEQ, SEQ, gain(c)[:, 1:2])]


def halves(ap, m, side):
    return ap.rearrange("p h (n two m) -> p h n two m", two=2, m=m)[:, :, :, side, :]


def hgrn_gates(k, l, z, bc, key):
    n = 2 * HG_HEADS
    with ExitStack() as es, stage(k, "gates", "sig logs order fed") as (block, s):
        low = sbuf(k, es, "low", [P, n, SEQ])
        high = sbuf(k, es, "high", [P, n, SEQ])
        b = bc[:, :, :, :].rearrange("p d h t -> p (d h) t")
        keys = key[:, :, :, :].rearrange("p d h t -> p (d h) t")

        @block.scalar
        def _(act):
            act.activation(high[:, :, :], z, ACT.Sigmoid).then_inc(s.sig, 1)
            act.activation(keys, z, ACT.Sigmoid, scale=-1.0).then_inc(s.sig, 1)
            act.wait_ge(s.fed, 1)
            act.activation(low[:, :, :], low[:, :, :], ACT.Ln).then_inc(s.logs, 1)
            act.activation(high[:, :, :], high[:, :, :], ACT.Ln).then_inc(s.logs, 1)

        @block.vector
        def _(dve):
            order = Order(dve, s.order)
            dve.wait_ge(s.sig, 2)
            for i in range(n):
                up, lo = k.upper[:, l, i:i + 1], k.lower[:, l, i:i + 1]
                dve.tensor_scalar(high[:, i, :], high[:, i, :], up, lo, ALU.mult, ALU.add)
                last = dve.tensor_scalar(keys[:, i, :], keys[:, i, :], up, None, ALU.mult)
            order(last)
            order(dve.tensor_scalar(low[:, :, :], high[:, :, :], 1e-20, 2.0 ** 60, ALU.max, ALU.mult))
            order(dve.tensor_scalar(low[:, :, :], low[:, :, :], 1.0, None, ALU.min))
            dve.tensor_scalar(high[:, :, :], high[:, :, :], 2.0 ** -60, None, ALU.max).then_inc(s.fed, 1)
            dve.wait_ge(s.logs, 2)
            order(dve.tensor_tensor(high[:, :, :], high[:, :, :], low[:, :, :], ALU.add))
            one = k.ones[:, 0:1].broadcast_to([P, SEQ])
            for i in range(n):
                last = dve.tensor_tensor_scan(b[:, i, :], one, high[:, i, :], 0.0, ALU.mult, ALU.add)
            order(last)
            back = high[:, HG_HEADS:n, :]
            order(dve.tensor_tensor(bc[:, 1, :, :], back, bc[:, 1, :, :], ALU.subtract))
            last_gate = high[:, HG_HEADS:n, SEQ - 1]
            order(dve.tensor_tensor(k.back_total[:, :], last_gate, bc[:, 1, :, SEQ - 1], ALU.subtract))


def hgrn_attention(k, q, key, bc, att):
    with ExitStack() as es, stage(k, "attend", "apart decayed scaled scored took order") as (block, s):
        dif = sbuf(k, es, "dif", [P, 2, 2, HG_HEADS, SEQ])
        kh = sbuf(k, es, "kh", [P, 2, HG_HEADS, SEQ])
        qh = sbuf(k, es, "qh", [P, 2, HG_HEADS, SEQ])
        steps = LEVELS + 2
        shape = lambda m: [P, HG_HEADS, SEQ // (2 * m), m]

        @block.gpsimd
        def _(pool):
            for j in range(1, steps):
                m = 1 << (j - 1)
                if j >= 3:
                    pool.wait_ge(s.scaled, j - 1)
                for d in range(2):
                    b = bc[:, d, :, :]
                    out = dif[:, j % 2, d, :, :]
                    mid = (halves(b, m, 0)[:, :, :, m - 1:m] if d == 0 else halves(b, m, 1)[:, :, :, 0:1]).broadcast_to(shape(m))
                    near, far = (0, 1) if d == 0 else (1, 0)
                    pool.tensor_tensor(halves(out, m, near), mid, halves(b, m, near), ALU.subtract)
                    last = pool.tensor_tensor(halves(out, m, far), halves(b, m, far), mid, ALU.subtract)
                last.then_inc(s.apart, 1)

        @block.scalar
        def _(act):
            for j in range(1, steps):
                act.wait_ge(s.apart, j)
                act.activation(dif[:, j % 2, :, :, :], dif[:, j % 2, :, :, :], ACT.Exp).then_inc(s.decayed, 1)

        @block.vector
        def _(dve):
            order = Order(dve, s.order)

            def factors(j):
                if j >= 2:
                    dve.wait_ge(s.scored, j - 1)
                ks, qs = kh[:, j % 2, :, :], qh[:, j % 2, :, :]
                if j == 0:
                    dve.tensor_tensor(ks, key[:, 0, :, :], key[:, 1, :, :], ALU.add)
                    dve.tensor_copy(qs, q).then_inc(s.scaled, 1)
                    return
                m = 1 << (j - 1)
                dve.wait_ge(s.decayed, j)
                fwd, back = dif[:, j % 2, 0, :, :], dif[:, j % 2, 1, :, :]
                dve.tensor_tensor(halves(ks, m, 0), halves(key[:, 0, :, :], m, 0), halves(fwd, m, 0), ALU.mult)
                dve.tensor_tensor(halves(ks, m, 1), halves(key[:, 1, :, :], m, 1), halves(back, m, 1), ALU.mult)
                dve.tensor_tensor(halves(qs, m, 1), halves(q, m, 1), halves(fwd, m, 1), ALU.mult)
                dve.tensor_tensor(halves(qs, m, 0), halves(q, m, 0), halves(back, m, 0), ALU.mult).then_inc(s.scaled, 1)

            def take(j):
                dve.wait_ge(s.scored, j + 1)
                for i in range(2):
                    data = k.bank[2 * (j % 2) + i][:, :].rearrange("p (h t) -> p h t", h=HG_HEADS)
                    own = att[:, i, :, i * P:(i + 1) * P]
                    if j == 0:
                        last = dve.tensor_copy(own, data)
                    elif j == steps - 1:
                        last = dve.tensor_copy(att[:, i, :, (1 - i) * P:(2 - i) * P], data)
                    else:
                        mask = k.both[:, j - 1, :].unsqueeze(1).broadcast_to([P, HG_HEADS, P])
                        last = dve.copy_predicated(own, mask, data)
                last.then_inc(s.took, 1)
                dve.wait_ge(s.took, j + 1)

            factors(0)
            for j in range(1, steps):
                factors(j)
                take(j - 1)
            take(steps - 1)

        @block.tensor
        def _(pe):
            for j in range(steps):
                pe.wait_ge(s.scaled, j + 1)
                if j >= 2:
                    pe.wait_ge(s.took, j - 1)
                for i in range(2):
                    t = i if j < steps - 1 else 1 - i
                    for h in range(HG_HEADS):
                        last = pe.matmul(k.bank[2 * (j % 2) + i][:, h * P:(h + 1) * P],
                                         kh[:, j % 2, h, i * P:(i + 1) * P], qh[:, j % 2, h, t * P:(t + 1) * P],
                                         start=True, stop=True)
                last.then_inc(s.scored, 1)


def hgrn_outputs(k, s0, q, gate, key, bc, att, from_state, out):
    with ExitStack() as es, stage(k, "outputs", "shifted grown fed mixed squares sums logged root order gated") as (block, s):
        grow = sbuf(k, es, "grow", [P, 2, HG_HEADS, SEQ])
        sq = sbuf(k, es, "sq", [P, HG_HEADS * SEQ])
        rstd = sbuf(k, es, "rstd", [P, HG_HEADS * SEQ])

        @block.vector
        def _(dve):
            order = Order(dve, s.order)
            if from_state:
                for h in range(HG_HEADS):
                    last = dve.tensor_scalar(grow[:, 1, h, :], bc[:, 1, h, :], k.back_total[:, h:h + 1], None, ALU.add)
                last.then_inc(s.shifted, 1)
                dve.wait_ge(s.grown, 2)
                for d in range(2):
                    last = dve.tensor_tensor(grow[:, d, :, :], grow[:, d, :, :], q, ALU.mult)
                last.then_inc(s.fed, 1)
            dve.wait_ge(s.root, 1)
            for n in range(2):
                half = slice(512 * n, 512 * (n + 1))
                last = dve.tensor_tensor(rstd[:, half], rstd[:, half], k.bank[n][:, :], ALU.mult)
            order(last)
            dve.wait_ge(s.gated, 1)
            dve.tensor_tensor(out, rstd[:, :].rearrange("p (h t) -> p h t", h=HG_HEADS), gate, ALU.mult)

        @block.scalar
        def _(act):
            if from_state:
                act.activation(grow[:, 0, :, :], bc[:, 0, :, :], ACT.Exp).then_inc(s.grown, 1)
                act.wait_ge(s.shifted, 1)
                act.activation(grow[:, 1, :, :], grow[:, 1, :, :], ACT.Exp).then_inc(s.grown, 1)
            act.wait_ge(s.mixed, 1)
            for n in range(2):
                last = act.activation(sq[:, 512 * n:512 * (n + 1)], k.bank[n][:, :], ACT.Square)
            last.then_inc(s.squares, 1)
            act.activation(gate, gate, ACT.Silu).then_inc(s.gated, 1)
            act.wait_ge(s.sums, 1)
            for n in range(2):
                last = act.activation(rstd[:, 512 * n:512 * (n + 1)], k.bank[2 + n][:, :], ACT.Ln, scale=1.0 / P, bias=k.eps[:, 0:1])
            last.then_inc(s.logged, 1)
            act.wait_ge(s.logged, 1)
            act.activation(rstd[:, :], rstd[:, :], ACT.Exp, scale=-0.5).then_inc(s.root, 1)

        @block.tensor
        def _(pe):
            if from_state:
                pe.wait_ge(s.fed, 1)
            for h in range(HG_HEADS):
                o = k.bank[h // 2][:, (h % 2) * SEQ:(h % 2 + 1) * SEQ]
                parts = [(k.v[:, s0 // P + i, h * P:(h + 1) * P], att[:, i, h, :]) for i in range(2)]
                if from_state:
                    parts += [(k.state[:, d, h, :], grow[:, d, h, :]) for d in range(2)]
                for i, (lhsT, rhs) in enumerate(parts):
                    last = pe.matmul(o, lhsT, rhs, start=(i == 0), stop=(i == len(parts) - 1))
            last.then_inc(s.mixed, 1)
            pe.wait_ge(s.squares, 1)
            for n in range(2):
                last = pe.matmul(k.bank[2 + n][:, :], k.ones, sq[:, 512 * n:512 * (n + 1)], start=True, stop=True)
            last.then_inc(s.sums, 1)


def hgrn_states(k, s0, key, bc):
    with ExitStack() as es, stage(k, "states", "shifted grown fed turned took summed order") as (block, s):
        dec = sbuf(k, es, "dec", [P, 2, HG_HEADS, SEQ])
        turned = sbuf(k, es, "turned", [P, 2, 2, HG_HEADS, P])

        @block.scalar
        def _(act):
            for h in range(HG_HEADS):
                act.activation(dec[:, 0, h, :], bc[:, 0, h, :], ACT.Exp, scale=-1.0, bias=bc[:, 0, h, SEQ - 1:SEQ])
            act.activation(dec[:, 1, :, :], bc[:, 1, :, :], ACT.Exp, scale=-1.0).then_inc(s.grown, 1)

        @block.vector
        def _(dve):
            dve.wait_ge(s.grown, 1)
            dve.tensor_tensor(dec[:, :, :, :], dec[:, :, :, :], key[:, :, :, :], ALU.mult).then_inc(s.fed, 1)
            for n in range(4):
                dve.wait_ge(s.turned, n + 1)
                dve.tensor_copy(turned[:, n // 2, n % 2, :, :],
                                k.bank[n][:, :].rearrange("p (h d) -> p h d", h=HG_HEADS)).then_inc(s.took, 1)
            dve.wait_ge(s.summed, 1)
            for d in range(2):
                dve.tensor_copy(k.state[:, d, :, :], k.bank[4 + d][:, :].rearrange("p (h d) -> p h d", h=HG_HEADS))

        @block.tensor
        def _(pe):
            pe.wait_ge(s.fed, 1)
            for n in range(4):
                for h in range(HG_HEADS):
                    i, d = n // 2, n % 2
                    last = pe.transpose(k.bank[n][:, h * P:(h + 1) * P], dec[:, d, h, i * P:(i + 1) * P], k.ident)
                last.then_inc(s.turned, 1)
            pe.wait_ge(s.took, 4)
            for d in range(2):
                for h in range(HG_HEADS):
                    for i in range(2):
                        last = pe.matmul(k.bank[4 + d][:, h * P:(h + 1) * P], turned[:, i, d, h, :],
                                         k.v[:, s0 // P + i, h * P:(h + 1) * P], start=(i == 0), stop=(i == 1))
            last.then_inc(s.summed, 1)


def short_conv(k, l, s0, grid, cg, bg, hv, out):
    with ExitStack() as es, stage(k, "conv", "order") as (block, s):
        u = sbuf(k, es, "u", [P, 4, SEQ])
        y = sbuf(k, es, "y", [P, 4, SEQ])

        @block.vector
        def _(dve):
            order = Order(dve, s.order)
            order(dve.tensor_tensor(u[:, :, :], cg, hv, ALU.mult))
            w = k.small("conv_w").rearrange("p (l tap c) -> p l tap c", l=DEPTH, tap=3)
            for c in range(4):
                last = dve.tensor_scalar(y[:, c, :], u[:, c, :], w[:, l, 1, c:c + 1], None, ALU.mult)
            order(last)
            for tap in (0, 2):
                for c in range(4):
                    step = GRID_W if grid and c >= 2 else 1
                    rows = SEQ // GRID_W if grid and c < 2 else 1
                    uu = u[:, c, :].rearrange("p (r w) -> p r w", r=rows)
                    yy = y[:, c, :].rearrange("p (r w) -> p r w", r=rows)
                    width = SEQ // rows
                    near, far = slice(0, width - step), slice(step, width)
                    src, dst = (near, far) if tap == 0 else (far, near)
                    last = dve.scalar_tensor_tensor(out=yy[:, :, dst], in0=uu[:, :, src], scalar=w[:, l, tap, c:c + 1],
                                                    in1=yy[:, :, dst], op0=ALU.mult, op1=ALU.add)
                order(last)
            dve.tensor_tensor(out, y[:, :, :], bg, ALU.mult)


def residual_project(k, name, x, gate, seqs):
    t0, t1 = seqs[0] * SEQ, (seqs[-1] + 1) * SEQ

    def evict(dve, c, bank, s):
        for q in seqs:
            half = slice(q * SEQ, (q + 1) * SEQ)
            last = dve.scalar_tensor_tensor(out=k.X[:, c, half], in0=bank[:, q * SEQ - t0:(q + 1) * SEQ - t0],
                                            scalar=gate[:, c, q:q + 1], in1=k.X[:, c, half], op0=ALU.mult, op1=ALU.add)
        return last

    project(k, name, [(1, P, 0, t1 - t0)] * KD, x[:, :, t0:t1], evict, by=lambda c: 1)


def token_mixer_1(k, l):
    with ExitStack() as es:
        proj = sbuf(k, es, "proj", [P, 28, TWO])
        H = k.H
        last_layer = l == DEPTH - 1
        outs = [(1, P, 0, TWO)] * 12 + [(1, P, SEQ, SEQ) if last_layer else (1, P, 0, TWO)] * 20
        with ExitStack() as inner:
            values = sbuf(k, inner, "values", [P, HG_HEADS, TWO])

            def evict(eng, c, bank, s):
                t0, n = outs[c][2:]
                return copy(k, eng, values[:, c, :] if c < 4 else proj[:, c - 4, t0:t0 + n], bank[:, 0:n])

            project(k, "w_in", outs, H[:, :, :], evict)
            transpose_chunks(k, "values", [(k.v[:, i, c * P:(c + 1) * P], values[:, c, i * P:(i + 1) * P])
                                           for i in range(4) for c in range(4)])
        bc = sbuf(k, es, "bc", [P, 2, HG_HEADS, SEQ])
        key = sbuf(k, es, "key", [P, 2, HG_HEADS, SEQ])
        for n, s0 in enumerate((0, SEQ)):
            part = lambda c: proj[:, c:c + 4, s0:s0 + SEQ]
            hgrn_gates(k, l, proj[:, 0:8, s0:s0 + SEQ], bc, key)
            if n == 1 or not last_layer:
                with ExitStack() as inner:
                    att = sbuf(k, inner, "att", [P, 2, HG_HEADS, SEQ])
                    hgrn_attention(k, part(8), key, bc, att)
                    hgrn_outputs(k, s0, part(8), part(12), key, bc, att, n == 1, H[:, 0:4, s0:s0 + SEQ])
                short_conv(k, l, s0, n == 1, part(16), part(20), part(24), H[:, 4:8, s0:s0 + SEQ])
            if n == 0:
                hgrn_states(k, s0, key, bc)
    residual_project(k, "w_out", k.H, k.mods[:, l, 16:24, :], (1,) if last_layer else (0, 1))



GATHER = 8


def peer(k, a, l, tiles):
    H = k.H
    with ExitStack() as es:
        T0, T = tiles[0] * P, len(tiles) * P
        qr = sbuf(k, es, "qr", [P, 2 * PEER_HEADS, T])
        project(k, "peer_wq", [(1, P, 0, T)] * (2 * PEER_HEADS), H[:, :, T0:T0 + T],
                lambda eng, c, bank, s: copy(k, eng, qr[:, c, :], bank[:, 0:T]))
        hT = sbuf(k, es, "hT", [P, len(tiles), D])
        transpose_chunks(k, "h_rows", [(hT[:, i, c * P:(c + 1) * P], H[:, c, t * P:(t + 1) * P])
                                       for i, t in enumerate(tiles) for c in range(KD)])
        peer_experts(k, a, l, tiles, qr, hT)


def peer_experts(k, a, l, tiles, qr, hT):
    NH = 2 * PEER_HEADS
    NT = len(tiles)
    slots = " ".join(f"landed{n}" for n in range(GATHER))
    with ExitStack() as es, stage(k, "experts", slots + " keys scored took order chosen spread grown dotted "
                                  "gelu weighed diag summed out_rows turned") as (block, s):
        landed = [s.landed0, s.landed1, s.landed2, s.landed3, s.landed4, s.landed5, s.landed6, s.landed7]
        keys = sbuf(k, es, "subkeys", [P, NH, N_KEYS])
        scores = sbuf(k, es, "scores", [P, NH, N_KEYS])
        rows = sbuf(k, es, "rows", [P, GATHER, D])
        junk = sbuf(k, es, "junk", [P, D])
        out_rows = sbuf(k, es, "out_rows", [P, D])
        expert = sbuf(k, es, "expert", [P, 2, SEL], U32)
        best = sbuf(k, es, "best", [P, NH, TOPK])
        where = sbuf(k, es, "where", [P, NH, TOPK], U32)
        where_f = sbuf(k, es, "where_f", [P, NH, TOPK])
        cand = sbuf(k, es, "cand", [P, PEER_HEADS, TOPK, TOPK])
        top = sbuf(k, es, "top", [P, PEER_HEADS, TOPK])
        largest = sbuf(k, es, "largest", [P, PEER_HEADS])
        pos = sbuf(k, es, "pos", [P, PEER_HEADS, TOPK], U32)
        part = sbuf(k, es, "part", [P, 2, PEER_HEADS, TOPK], U32)
        part_f = sbuf(k, es, "part_f", [P, 2, PEER_HEADS, TOPK])
        hot = sbuf(k, es, "hot", [P, PEER_HEADS, TOPK, TOPK])
        index = sbuf(k, es, "index", [P, 2, PEER_HEADS, TOPK])
        total = sbuf(k, es, "total", [P, PEER_HEADS])
        products = sbuf(k, es, "products", [P, SEL])
        weight = sbuf(k, es, "weight", [P, SEL])
        diag = sbuf(k, es, "diag", [P, 4, P])
        table = (a.peer_u[l], a.peer_v[l])

        @block.sync
        def _(sp):
            sp.dma_start(keys[:, :, :], a.peer_subkeys[l]).then_inc(s.keys, 16)

        @block.gpsimd
        def _(pool):
            for n in range(2 * SEL * NT):
                i, e = n // (2 * SEL), n % SEL
                is_v = n % (2 * SEL) >= SEL
                if n % (2 * SEL) == 0:
                    pool.wait_ge(s.chosen, i + 1)
                if n >= GATHER:
                    old = n - GATHER
                    done = SEL * (old // (2 * SEL)) + old % SEL + 1
                    pool.wait_ge(s.summed if old % (2 * SEL) >= SEL else s.dotted, done)
                pool.indirect_dma_start(rows[:, n % GATHER, :], None, table[is_v],
                                        bass.IndirectOffsetOnAxis(ap=expert[:, i % 2, e:e + 1], axis=0)
                                        ).then_inc(landed[n % GATHER], 16)

        @block.tensor
        def _(pe):
            def score(i):
                if i > 0:
                    pe.wait_ge(s.took, 4 * i)
                for c in range(NH):
                    last = pe.matmul(k.bank[2 + c // 4][:, (c % 4) * P:(c % 4 + 1) * P], qr[:, c, i * P:(i + 1) * P],
                                     keys[:, c, :], start=True, stop=True)
                    if c % 4 == 3:
                        last.then_inc(s.scored, 1)

            pe.wait_ge(s.keys, 16)
            score(0)
            for i in range(NT):
                if i + 1 < NT:
                    score(i + 1)
                if i > 0:
                    pe.wait_ge(s.out_rows, i)
                for e in range(SEL):
                    n = (2 * i + 1) * SEL + e
                    pe.wait_ge(s.diag, SEL * i + e + 1)
                    pe.wait_ge(landed[n % GATHER], 16 * (n // GATHER + 1))
                    for half in range(2):
                        last = pe.matmul(k.bank[half][:, :], diag[:, e % 4, :], rows[:, n % GATHER, half * 512:(half + 1) * 512],
                                         start=(e == 0), stop=(e == SEL - 1))
                    last.then_inc(s.summed, 1)
                pe.wait_ge(s.out_rows, i + 1)
                for c in range(KD):
                    last = pe.transpose(k.bank[6 + c // 4][:, (c % 4) * P:(c % 4 + 1) * P], out_rows[:, c * P:(c + 1) * P], k.ident)
                last.then_inc(s.turned, 1)

        @block.scalar
        def _(act):
            def take_scores(i):
                if i > 0:
                    act.wait_ge(s.chosen, i)
                for n in range(4):
                    act.wait_ge(s.scored, 4 * i + n + 1)
                    act.copy(scores[:, 4 * n:4 * n + 4, :], k.bank[2 + n][:, :].rearrange("p (c n) -> p c n", c=4)).then_inc(s.took, 1)

            def exps(i):
                act.wait_ge(s.spread, i + 1)
                act.activation(top[:, :, :], top[:, :, :], ACT.Exp).then_inc(s.grown, 1)

            take_scores(0)
            exps(0)
            for i in range(NT):
                if i + 1 < NT:
                    take_scores(i + 1)
                act.wait_ge(s.dotted, SEL * (i + 1))
                act.activation(products[:, :], products[:, :], ACT.Gelu).then_inc(s.gelu, 1)
                act.wait_ge(s.weighed, i + 1)
                for e in range(SEL):
                    n = SEL * i + e
                    if n >= 4:
                        act.wait_ge(s.summed, n - 3)
                    act.mul(diag[:, e % 4, :], k.ident, products[:, e:e + 1]).then_inc(s.diag, 1)
                if i + 1 < NT:
                    exps(i + 1)
                act.wait_ge(s.summed, SEL * (i + 1))
                if i > 0:
                    act.wait_ge(s.turned, i)
                act.copy(out_rows[:, 0:512], k.bank[0][:, :])
                act.copy(out_rows[:, 512:1024], k.bank[1][:, :]).then_inc(s.out_rows, 1)

        @block.vector
        def _(dve):
            order = Order(dve, s.order)

            def top16(values, best, where):
                order(dve.max(best[:, 0:8], values))
                order(dve.max_index(where[:, 0:8], best[:, 0:8], values))
                order(dve.match_replace(values, best[:, 0:8], values, -3e38))
                order(dve.max(best[:, 8:16], values))
                order(dve.max_index(where[:, 8:16], best[:, 8:16], values))

            full = [P, PEER_HEADS, TOPK, TOPK]

            def choose(i):
                for c in range(NH):
                    if c % 4 == 0:
                        dve.wait_ge(s.took, 4 * i + c // 4 + 1)
                    top16(scores[:, c, :], best[:, c, :], where[:, c, :])
                order(dve.tensor_copy(where_f[:, :, :], where[:, :, :]))
                pairs = best[:, :, :].rearrange("p (h two) n -> p h two n", two=2)
                order(dve.tensor_tensor(cand[:, :, :, :], pairs[:, :, 0, :].unsqueeze(3).broadcast_to(full),
                                        pairs[:, :, 1, :].unsqueeze(2).broadcast_to(full), ALU.add))
                for h in range(PEER_HEADS):
                    top16(cand[:, h, :, :].rearrange("p a b -> p (a b)"), top[:, h, :], pos[:, h, :])
                dve.tensor_scalar(part[:, 0, :, :], pos[:, :, :], 4, None, ALU.logical_shift_right)
                order(dve.tensor_scalar(part[:, 1, :, :], pos[:, :, :], TOPK - 1, None, ALU.bitwise_and))
                order(dve.tensor_copy(part_f[:, :, :, :], part[:, :, :, :]))
                places = where_f[:, :, :].rearrange("p (h two) n -> p h two n", two=2)
                iota = k.const("iota").unsqueeze(1).broadcast_to([P, PEER_HEADS * TOPK, TOPK]).rearrange("p (h j) n -> p h j n", h=PEER_HEADS)
                for half in range(2):
                    order(dve.tensor_tensor(hot[:, :, :, :], part_f[:, half, :, :].unsqueeze(3).broadcast_to(full), iota, ALU.is_equal))
                    order(dve.tensor_tensor(hot[:, :, :, :], hot[:, :, :, :],
                                            places[:, :, half, :].unsqueeze(2).broadcast_to(full), ALU.mult))
                    order(dve.tensor_reduce(index[:, half, :, :], hot[:, :, :, :], AX, ALU.add))
                if i >= 2:
                    dve.wait_ge(s.summed, SEL * (i - 1))
                dve.scalar_tensor_tensor(out=expert[:, i % 2, :], in0=index[:, 0, :, :].rearrange("p h j -> p (h j)"), scalar=float(N_KEYS),
                                         in1=index[:, 1, :, :].rearrange("p h j -> p (h j)"), op0=ALU.mult, op1=ALU.add).then_inc(s.chosen, 1)
                order(dve.tensor_copy(largest[:, :], top[:, :, 0]))
                dve.tensor_tensor(top[:, :, :], top[:, :, :],
                                  largest[:, :].unsqueeze(2).broadcast_to([P, PEER_HEADS, TOPK]), ALU.subtract).then_inc(s.spread, 1)

            def add_out(i):
                t = tiles[i]
                dve.wait_ge(s.turned, i + 1)
                cols = slice(t * P, (t + 1) * P)
                for c in range(KD):
                    dve.scalar_tensor_tensor(out=k.X[:, c, cols], in0=k.bank[6 + c // 4][:, (c % 4) * P:(c % 4 + 1) * P],
                                             scalar=k.mods[:, l, 40 + c, t // 2:t // 2 + 1], in1=k.X[:, c, cols],
                                             op0=ALU.mult, op1=ALU.add)

            choose(0)
            for i in range(NT):
                for e in range(SEL):
                    n = 2 * i * SEL + e
                    dve.wait_ge(landed[n % GATHER], 16 * (n // GATHER + 1))
                    if i > 0 and e == 0:
                        dve.wait_ge(s.diag, SEL * i)
                    if n > 0:
                        dve.wait_ge(s.dotted, SEL * i + e)
                    dve.tensor_tensor_reduce(junk[:, :], rows[:, n % GATHER, :], hT[:, i, :], 1.0, 0.0, ALU.mult, ALU.add,
                                             products[:, e:e + 1]).then_inc(s.dotted, 1)
                    if i > 0 and e == 2:
                        add_out(i - 1)
                dve.wait_ge(s.grown, i + 1)
                order(dve.tensor_reduce(total[:, :], top[:, :, :], AX, ALU.add))
                order(dve.reciprocal(total[:, :], total[:, :]))
                order(dve.tensor_tensor(weight[:, :].rearrange("p (h j) -> p h j", h=PEER_HEADS), top[:, :, :],
                                        total[:, :].unsqueeze(2).broadcast_to([P, PEER_HEADS, TOPK]), ALU.mult))
                dve.wait_ge(s.gelu, i + 1)
                dve.tensor_tensor(products[:, :], products[:, :], weight[:, :], ALU.mult).then_inc(s.weighed, 1)
                if i + 1 < NT:
                    choose(i + 1)
            add_out(NT - 1)


def first_block(k, a):
    modulation(k)
    for l in range(DEPTH):
        gain = lambda n: both_ways(lambda c: k.gain[:, l, n, c, :])
        shift = lambda c0: both_ways(lambda c: k.mods[:, l, c0 + c, :])
        rms_norm(k, "norm1", k.X[:, :, :], TWO, gain(0), shift(0), k.H)
        with ExitStack() as es:
            k.v = sbuf(k, es, "values", [P, 4, HG_HEADS * P])
            k.state = sbuf(k, es, "states", [P, 2, HG_HEADS, P])
            token_mixer_1(k, l)
        rms_norm(k, "norm2", k.X[:, :, :], TWO, gain(1), shift(24), k.H)
        peer(k, a, l, (0, 1, 2, 3) if l < DEPTH - 1 else (2, 3))



def project_residual_2(k, name, x, n_units=1, split_x=None):
    project(k, name, [(n_units, P, 0, T2)] * KD, x,
            lambda dve, c, bank, s: dve.tensor_tensor(k.Y[:, c, :], bank[:, 0:T2], k.Y[:, c, :], ALU.add),
            by=lambda c: 1, split_x=split_x)


def turn_values(k, name, values, v):
    transpose_chunks(k, name, [(v[0:n, i, c * P:(c + 1) * P], values[:, c, t0:t0 + n])
                               for i, (t0, n) in enumerate(TILES2) for c in range(KD)])


def head_norms(k, name, x, chunks, ones, width, eps_chunks=None, gain=None, factor=1.0, mean=True):
    with ExitStack() as es, stage(k, name, "squares summed logged root taken") as (block, s):
        n = len(chunks)
        sq = sbuf(k, es, "sq", [P, 2, T2])
        rstd = sbuf(k, es, "rstd", [P, 2, T2])

        @block.scalar
        def _(act):
            for i, c in enumerate(chunks):
                if i >= 2:
                    act.wait_ge(s.summed, i - 1)
                act.activation(sq[:, i % 2, :], x[:, c, :], ACT.Square).then_inc(s.squares, 1)
                act.wait_ge(s.summed, i + 1)
                if i >= 2:
                    act.wait_ge(s.taken, i - 1)
                act.activation(rstd[:, i % 2, :], k.bank[i % 4][:, 0:T2], ACT.Ln, scale=1.0 / width if mean else 1.0,
                               bias=k.eps[:, 0:1]).then_inc(s.logged, 1)
                act.wait_ge(s.logged, i + 1)
                act.activation(rstd[:, i % 2, :], rstd[:, i % 2, :], ACT.Exp, scale=-0.5).then_inc(s.root, 1)

        @block.tensor
        def _(pe):
            for i, c in enumerate(chunks):
                pe.wait_ge(s.squares, i + 1)
                if i >= 4:
                    pe.wait_ge(s.root, i - 3)
                pe.matmul(k.bank[i % 4][:, 0:T2], ones, sq[:, i % 2, :], start=True, stop=True).then_inc(s.summed, 1)

        @block.vector
        def _(dve):
            for i, c in enumerate(chunks):
                dve.wait_ge(s.root, i + 1)
                g = factor if gain is None else gain(c)
                dve.scalar_tensor_tensor(out=x[:, c, :], in0=x[:, c, :], scalar=g, in1=rstd[:, i % 2, :],
                                         op0=ALU.mult, op1=ALU.mult).then_inc(s.taken, 1)




def fox(k, a, j):
    H = k.H
    with ExitStack() as es:
        q = sbuf(k, es, "q", [P, KD, T2])
        kk = sbuf(k, es, "k", [P, KD, T2])
        v = sbuf(k, es, "v", [P, 3, D])
        gate = sbuf(k, es, "gate", [P, KD, T2])
        f = sbuf(k, es, "f", [FOX_HEADS, 3, T2])
        with ExitStack() as inner:
            values = sbuf(k, inner, "values", [P, KD, T2])

            def evict(eng, c, bank, s):
                if c == 32:
                    return copy(k, eng, f[:, 0, :], bank[0:FOX_HEADS, 0:T2])
                return copy(k, eng, (q, kk, values, gate)[c // 8][:, c % 8, :], bank[:, 0:T2])

            project(k, "fox_in", [(1, P, 0, T2)] * 32 + [(1, FOX_HEADS, 0, T2)], H[:, :, 0:T2], evict)
            turn_values(k, "fox_values", values, v)
        gq, gk = k.small("fox_q_gain_2")[:, j:j + 1], k.small("fox_k_gain_2")[:, j:j + 1]
        with ExitStack() as es2, stage(k, "fox_gates", "order ready absd expd lned scaled") as (block, s):
            tmp = sbuf(k, es2, "tmp", [FOX_HEADS, T2])

            @block.vector
            def _(dve):
                order = Order(dve, s.order)
                order(dve.tensor_scalar(k.qgain[:, 0:1], gq, DK_FOX ** -0.5, None, ALU.mult))
                order(dve.tensor_scalar(f[:, 0, :], f[:, 0, :], k.fox_b[:, j:j + 1], None, ALU.add))
                dve.scalar_tensor_tensor(out=tmp[:, :], in0=f[:, 0, :], scalar=-1.0, in1=f[:, 0, :], op0=ALU.mult, op1=ALU.max).then_inc(s.absd, 1)
                dve.wait_ge(s.lned, 1)
                order(dve.scalar_tensor_tensor(out=f[:, 0, :], in0=f[:, 0, :], scalar=0.0, in1=tmp[:, :], op0=ALU.min, op1=ALU.subtract))
                order(dve.tensor_tensor_scan(f[:, 1, :], k.ones[0:FOX_HEADS, 0:1].broadcast_to([FOX_HEADS, T2]), f[:, 0, :], 0.0, ALU.mult, ALU.add))
                order(dve.tensor_scalar(f[:, 2, :], f[:, 1, :], -1.0, None, ALU.mult))

            @block.scalar
            def _(act):
                act.wait_ge(s.absd, 1)
                act.activation(tmp[:, :], tmp[:, :], ACT.Exp, scale=-1.0).then_inc(s.expd, 1)
                act.wait_ge(s.expd, 1)
                act.activation(tmp[:, :], tmp[:, :], ACT.Ln, bias=k.one[0:FOX_HEADS, 0:1]).then_inc(s.lned, 1)
                act.activation(gate[:, :, :], gate[:, :, :], ACT.Sigmoid)

        head_norms(k, "q_norm", q, range(KD), k.ones64, DK_FOX, gain=lambda c: k.qgain[:, 0:1])
        head_norms(k, "k_norm", kk, range(KD), k.ones64, DK_FOX, gain=lambda c: gk)
        fox_attention(k, q, kk, v, gate, f)
    project_residual_2(k, "fox_out", H[:, :, 0:T2])


def fox_attention(k, q, kk, v, gate, f):
    H = k.H
    steps = [(h, i) for h in range(FOX_HEADS) for i in range(3)]
    with ExitStack() as es, stage(k, "attention", "scored maxed negated exped summed rcp normed turned copied mixed gated") as (block, s):
        sc = sbuf(k, es, "sc", [P, 2, T2])
        pr = sbuf(k, es, "pr", [P, 2, T2])
        pT = sbuf(k, es, "pT", [P, 2, 3, P])
        mx = sbuf(k, es, "mx", [P, 2])
        nmx = sbuf(k, es, "nmx", [P, 2])
        total = sbuf(k, es, "total", [P, 2])
        inv = sbuf(k, es, "inv", [P, 2])

        def score(pe, n):
            h, i = steps[n]
            t0, nq = TILES2[i]
            nk = t0 + nq
            lo = (h % 2) * DK_FOX
            if n >= 2:
                pe.wait_ge(s.maxed, n - 1)
            bank = k.bank[n % 2][0:nq, 0:nk]
            pe.matmul(bank, q[lo:lo + DK_FOX, h // 2, t0:t0 + nq], kk[lo:lo + DK_FOX, h // 2, 0:nk], start=True, stop=False)
            pick = k.ident[0:FOX_HEADS, h:h + 1]
            pe.matmul(bank, f[:, 1, t0:t0 + nq], pick.broadcast_to([FOX_HEADS, nk]), start=False, stop=False)
            pe.matmul(bank, pick.broadcast_to([FOX_HEADS, nq]), f[:, 2, 0:nk], start=False, stop=True).then_inc(s.scored, 1)

        def turn(pe, n):
            h, i = steps[n]
            t0, nq = TILES2[i]
            pe.wait_ge(s.normed, n + 1)
            if n >= 2:
                pe.wait_ge(s.copied, n - 1)
            for j in range(i + 1):
                k0, nk = TILES2[j]
                last = pe.transpose(k.bank[2 + n % 2][0:nk, j * P:j * P + nq], pr[0:nq, n % 2, k0:k0 + nk], k.ident[0:nq, 0:nq])
            last.then_inc(s.turned, 1)

        def mix(pe, n):
            h, i = steps[n]
            t0, nq = TILES2[i]
            pe.wait_ge(s.copied, n + 1)
            if i == 0 and h % 2 == 0 and h >= 4:
                pe.wait_ge(s.gated, h // 2 - 1)
            lo = (h % 2) * DK_FOX
            for j in range(i + 1):
                nk = TILES2[j][1]
                last = pe.matmul(k.bank[4 + (h // 2) % 2][lo:lo + DK_FOX, t0:t0 + nq], v[0:nk, j, h * DK_FOX:(h + 1) * DK_FOX],
                                 pT[0:nk, n % 2, j, 0:nq], start=(j == 0), stop=(j == i))
            last.then_inc(s.mixed, 1)

        @block.tensor
        def _(pe):
            for n in range(len(steps) + 2):
                if n < len(steps):
                    score(pe, n)
                if 1 <= n <= len(steps):
                    turn(pe, n - 1)
                if n >= 2:
                    mix(pe, n - 2)

        @block.vector
        def _(dve):
            for n in range(len(steps) + 2):
                if n < len(steps):
                    h, i = steps[n]
                    t0, nq = TILES2[i]
                    nk = t0 + nq
                    b = n % 2
                    dve.wait_ge(s.scored, n + 1)
                    if n >= 2:
                        dve.wait_ge(s.summed, n - 1)
                    dve.tensor_tensor_reduce(sc[0:nq, b, 0:nk], k.bank[n % 2][0:nq, 0:nk],
                                             k.causal[0:nq, 2 * P - t0:2 * P - t0 + nk], 1.0, NEG, ALU.add, ALU.max,
                                             mx[0:nq, b:b + 1]).then_inc(s.maxed, 1)
                    dve.wait_ge(s.maxed, n + 1)
                    dve.tensor_scalar(nmx[0:nq, b:b + 1], mx[0:nq, b:b + 1], -1.0, None, ALU.mult).then_inc(s.negated, 1)
                if 1 <= n <= len(steps):
                    m = n - 1
                    h, i = steps[m]
                    t0, nq = TILES2[i]
                    nk = t0 + nq
                    b = m % 2
                    dve.wait_ge(s.summed, m + 1)
                    dve.reciprocal(inv[0:nq, b:b + 1], total[0:nq, b:b + 1]).then_inc(s.rcp, 1)
                    dve.wait_ge(s.rcp, m + 1)
                    dve.tensor_scalar(pr[0:nq, b, 0:nk], pr[0:nq, b, 0:nk], inv[0:nq, b:b + 1], None, ALU.mult).then_inc(s.normed, 1)
                if n >= 2 and steps[n - 2][1] == 2 and steps[n - 2][0] % 2 == 1:
                    pair = steps[n - 2][0] // 2
                    dve.wait_ge(s.mixed, n - 1)
                    dve.tensor_tensor(H[:, pair, 0:T2], k.bank[4 + pair % 2][:, 0:T2], gate[:, pair, :], ALU.mult).then_inc(s.gated, 1)

        @block.scalar
        def _(act):
            for n in range(len(steps) + 1):
                if n < len(steps):
                    h, i = steps[n]
                    t0, nq = TILES2[i]
                    nk = t0 + nq
                    b = n % 2
                    act.wait_ge(s.negated, n + 1)
                    if n >= 2:
                        act.wait_ge(s.turned, n - 1)
                    act.activation(pr[0:nq, b, 0:nk], sc[0:nq, b, 0:nk], ACT.Exp, bias=nmx[0:nq, b:b + 1],
                                   accum_out=total[0:nq, b:b + 1]).then_inc(s.summed, 1)
                if n >= 1:
                    m = n - 1
                    h, i = steps[m]
                    t0, nq = TILES2[i]
                    act.wait_ge(s.turned, m + 1)
                    if m >= 2:
                        act.wait_ge(s.mixed, m - 1)
                    for j in range(i + 1):
                        nk = TILES2[j][1]
                        last = act.copy(pT[0:nk, m % 2, j, 0:nq], k.bank[2 + m % 2][0:nk, j * P:j * P + nq])
                    last.then_inc(s.copied, 1)


def gla(k, a):
    H = k.H
    NH = 4
    with ExitStack() as es:
        q = sbuf(k, es, "q", [P, NH, T2])
        kk = sbuf(k, es, "k", [P, NH, T2])
        v = sbuf(k, es, "v", [P, 3, D])
        r = sbuf(k, es, "r", [P, KD, T2])
        low = sbuf(k, es, "low", [16, T2])
        b = sbuf(k, es, "b", [P, NH, T2])
        att = sbuf(k, es, "att", [P, 3, NH, T2])
        o = sbuf(k, es, "o", [P, KD, T2])
        alpha = sbuf(k, es, "alpha", [16, NH * P])
        with ExitStack() as inner:
            values = sbuf(k, inner, "values", [P, KD, T2])

            def evict(eng, c, bank, s):
                if c == 24:
                    return copy(k, eng, low[:, :], bank[0:16, 0:T2])
                if c >= NH:
                    out = kk[:, c - NH, :] if c < 8 else values[:, c - 8, :] if c < 16 else r[:, c - 16, :]
                    return copy(k, eng, out, bank[:, 0:T2])
                if eng is k.nc.scalar:
                    return eng.mul(q[:, c, :], bank[:, 0:T2], float(P) ** -0.5)
                return eng.tensor_scalar(q[:, c, :], bank[:, 0:T2], float(P) ** -0.5, None, ALU.mult)

            project(k, "gla_in", [(1, P, 0, T2)] * 24 + [(1, 16, 0, T2)], H[:, :, 0:T2], evict)
            turn_values(k, "gla_values", values, v)

        with ExitStack() as es2, stage(k, "gla_gates", "alpha made order ready expd lned") as (block, s):
            tmp = sbuf(k, es2, "tmp", [P, NH, T2])
            z = sbuf(k, es2, "z", [P, NH, T2])

            @block.sync
            def _(sp):
                sp.dma_start(alpha[:, :], a.gla_w_alpha2_2[0]).then_inc(s.alpha, 16)

            @block.tensor
            def _(pe):
                pe.wait_ge(s.alpha, 16)
                for h in range(NH):
                    last = pe.matmul(k.bank[h][:, 0:T2], alpha[:, h * P:(h + 1) * P], low[:, :], start=True, stop=True)
                last.then_inc(s.made, 1)

            @block.vector
            def _(dve):
                order = Order(dve, s.order)
                bias = k.small("gla_b_alpha_2")
                dve.wait_ge(s.made, 1)
                for h in range(NH):
                    last = dve.tensor_scalar(z[:, h, :], k.bank[h][:, 0:T2], bias[:, h:h + 1], None, ALU.add)
                order(last)
                dve.scalar_tensor_tensor(out=tmp[:, :, :], in0=z[:, :, :], scalar=-1.0, in1=z[:, :, :], op0=ALU.mult, op1=ALU.max).then_inc(s.ready, 1)
                dve.wait_ge(s.lned, 1)
                order(dve.tensor_scalar(z[:, :, :], z[:, :, :], 0.0, None, ALU.min))
                order(dve.tensor_tensor(z[:, :, :], z[:, :, :], tmp[:, :, :], ALU.subtract))
                order(dve.tensor_scalar(z[:, :, :], z[:, :, :], 1.0 / 16.0, None, ALU.mult))
                one = k.ones[:, 0:1].broadcast_to([P, T2])
                for h in range(NH):
                    last = dve.tensor_tensor_scan(b[:, h, :], one, z[:, h, :], 0.0, ALU.mult, ALU.add)
                order(last)

            @block.scalar
            def _(act):
                act.wait_ge(s.ready, 1)
                act.activation(tmp[:, :, :], tmp[:, :, :], ACT.Exp, scale=-1.0).then_inc(s.expd, 1)
                act.wait_ge(s.expd, 1)
                act.activation(tmp[:, :, :], tmp[:, :, :], ACT.Ln, bias=k.one[:, 0:1]).then_inc(s.lned, 1)
                act.activation(r[:, :, :], r[:, :, :], ACT.Silu)

        gla_attention(k, q, kk, b, att)

        with ExitStack() as es2, stage(k, "gla_mix", "mixed dve_took squares summed logged root") as (block, s):
            sq = sbuf(k, es2, "sq", [P, KD, T2])
            rstd = sbuf(k, es2, "rstd", [P, NH, T2])

            @block.tensor
            def _(pe):
                for c in range(KD):
                    h = c // 2
                    for i, (s0, n) in enumerate(TILES2):
                        last = pe.matmul(k.bank[c][:, s0:T2], v[0:n, i, c * P:(c + 1) * P], att[0:n, i, h, s0:T2],
                                         start=(i == 0), stop=(i == 2))
                    last.then_inc(s.mixed, 1)
                pe.wait_ge(s.squares, KD)
                pe.wait_ge(s.dve_took, KD)
                for h in range(NH):
                    for c in range(2):
                        last = pe.matmul(k.bank[h][:, 0:T2], k.ones, sq[:, 2 * h + c, :], start=(c == 0), stop=(c == 1))
                last.then_inc(s.summed, 1)

            @block.scalar
            def _(act):
                for c in range(KD):
                    act.wait_ge(s.mixed, c + 1)
                    act.activation(sq[:, c, :], k.bank[c][:, 0:T2], ACT.Square).then_inc(s.squares, 1)
                act.wait_ge(s.summed, 1)
                for h in range(NH):
                    last = act.activation(rstd[:, h, :], k.bank[h][:, 0:T2], ACT.Ln, scale=1.0 / (2 * P), bias=k.eps[:, 0:1])
                last.then_inc(s.logged, 1)
                act.wait_ge(s.logged, 1)
                act.activation(rstd[:, :, :], rstd[:, :, :], ACT.Exp, scale=-0.5).then_inc(s.root, 1)

            @block.vector
            def _(dve):
                gain = k.small("gla_o_gain_2")
                for c in range(KD):
                    dve.wait_ge(s.squares, c + 1)
                    dve.scalar_tensor_tensor(out=o[:, c, :], in0=k.bank[c][:, 0:T2], scalar=gain[:, c % 2:c % 2 + 1],
                                             in1=r[:, c, :], op0=ALU.mult, op1=ALU.mult).then_inc(s.dve_took, 1)
                dve.wait_ge(s.dve_took, KD)
                dve.wait_ge(s.root, 1)
                for c in range(KD):
                    dve.tensor_tensor(H[:, c, 0:T2], o[:, c, :], rstd[:, c // 2, :], ALU.mult)
    project_residual_2(k, "gla_out", H[:, :, 0:T2])


def gla_attention(k, q, kk, b, att):
    NH = 4
    whole, full_tiles = T2, 2 * P
    steps = [("diag", 0)] + [("level", l) for l in range(LEVELS)] + [("cross", 0), ("cross", 1)]
    with ExitStack() as es, stage(k, "gla_attend", "apart decayed scaled scored took order") as (block, s):
        dif = sbuf(k, es, "dif", [P, 2, NH, T2])
        kh = sbuf(k, es, "kh", [P, 2, NH, T2])
        qh = sbuf(k, es, "qh", [P, 2, NH, T2])

        def spans(kind, l):
            if kind == "level":
                m = 1 << l
                n = whole if 2 * m <= META else full_tiles
                view = lambda ap, side: halves(ap[:, :, 0:n], m, side)
                return view, (lambda ap: view(ap, 0)[:, :, :, m - 1:m]), [P, NH, n // (2 * m), m], [P, NH, n // (2 * m), m]
            e = (l + 1) * P
            view = lambda ap, side: ap[:, :, l * P:e] if side == 0 else ap[:, :, e:T2]
            return view, (lambda ap: ap[:, :, e - 1:e]), [P, NH, P], [P, NH, T2 - e]

        def blocks(j):
            kind, l = steps[j]
            if kind == "cross":
                return [(0, P, 2 * P, P), (0, 2 * P, T2, P)] if l == 0 else [(1, 2 * P, T2, P)]
            tiles = TILES2 if kind == "diag" or (2 << l) <= META else TILES2[:2]
            return [(i, t0, t0 + n, n) for i, (t0, n) in enumerate(tiles)]

        def banks(j):
            return [k.bank[4 * (j % 2) + n] for n in range(3)]

        @block.gpsimd
        def _(pool):
            for j in range(1, len(steps)):
                view, middle, near, far = spans(*steps[j])
                if j >= 3:
                    pool.wait_ge(s.scaled, j - 1)
                out = dif[:, j % 2, :, :]
                pool.tensor_tensor(view(out, 0), middle(b[:, :, :]).broadcast_to(near), view(b[:, :, :], 0), ALU.subtract)
                pool.tensor_tensor(view(out, 1), view(b[:, :, :], 1), middle(b[:, :, :]).broadcast_to(far), ALU.subtract).then_inc(s.apart, 1)

        @block.scalar
        def _(act):
            for j in range(1, len(steps)):
                view, *_ = spans(*steps[j])
                act.wait_ge(s.apart, j)
                d = dif[:, j % 2, :, :]
                for side in range(2):
                    last = act.activation(view(d, side), view(d, side), ACT.Exp)
                last.then_inc(s.decayed, 1)

        @block.vector
        def _(dve):
            order = Order(dve, s.order)

            def factors(j):
                if j >= 2:
                    dve.wait_ge(s.scored, j - 1)
                ks, qs = kh[:, j % 2, :, :], qh[:, j % 2, :, :]
                if j == 0:
                    dve.tensor_copy(ks, kk[:, :, :])
                    dve.tensor_copy(qs, q[:, :, :]).then_inc(s.scaled, 1)
                    return
                view, *_ = spans(*steps[j])
                dve.wait_ge(s.decayed, j)
                d = dif[:, j % 2, :, :]
                dve.tensor_tensor(view(ks, 0), view(kk[:, :, :], 0), view(d, 0), ALU.mult)
                dve.tensor_tensor(view(qs, 1), view(q[:, :, :], 1), view(d, 1), ALU.mult).then_inc(s.scaled, 1)

            def take(j):
                kind, l = steps[j]
                dve.wait_ge(s.scored, j + 1)
                for n, (i, t0, t1, m) in enumerate(blocks(j)):
                    data = banks(j)[n][0:m, :].rearrange("p (h t) -> p h t", h=NH)[:, :, 0:t1 - t0]
                    out = att[0:m, i, :, t0:t1]
                    if kind == "level":
                        mask = k.fwd[0:m, l, 0:t1 - t0].bitcast(I32).unsqueeze(1).broadcast_to([m, NH, t1 - t0])
                        last = dve.copy_predicated(out, mask, data)
                    else:
                        last = dve.tensor_copy(out, data)
                last.then_inc(s.took, 1)
                dve.wait_ge(s.took, j + 1)

            def take_diag():
                dve.wait_ge(s.scored, 1)
                for n, (i, t0, t1, m) in enumerate(blocks(0)):
                    data = banks(0)[n][0:m, :].rearrange("p (h t) -> p h t", h=NH)[:, :, 0:t1 - t0]
                    mask = k.both[0:m, LEVELS, 0:t1 - t0].unsqueeze(1).broadcast_to([m, NH, t1 - t0])
                    last = dve.copy_predicated(att[0:m, i, :, t0:t1], mask, data)
                last.then_inc(s.took, 1)
                dve.wait_ge(s.took, 1)

            order(dve.memset(att[:, :, :, :], 0.0))
            order(dve.memset(kh[:, 1, :, :], 0.0))
            order(dve.memset(qh[:, 1, :, :], 0.0))
            factors(0)
            for j in range(1, len(steps)):
                factors(j)
                take_diag() if j - 1 == 0 else take(j - 1)
            take(len(steps) - 1)

        @block.tensor
        def _(pe):
            for j in range(len(steps)):
                pe.wait_ge(s.scaled, j + 1)
                if j >= 2:
                    pe.wait_ge(s.took, j - 1)
                for n, (i, t0, t1, m) in enumerate(blocks(j)):
                    s0 = TILES2[i][0]
                    for h in range(NH):
                        last = pe.matmul(banks(j)[n][0:m, h * P:h * P + t1 - t0], kh[:, j % 2, h, s0:s0 + m],
                                         qh[:, j % 2, h, t0:t1], start=True, stop=True)
                last.then_inc(s.scored, 1)


def gdn(k, a):
    H = k.H
    NH = GDN_HEADS
    with ExitStack() as es:
        qkv = sbuf(k, es, "qkv", [P, 24, T2])
        gate = sbuf(k, es, "gate", [P, NH, T2])
        rows = sbuf(k, es, "rows", [NH, 6, T2])
        o = sbuf(k, es, "o", [P, NH, T2])
        with ExitStack() as es1:
            raw = sbuf(k, es1, "raw", [P, 24, T2])

            def evict(eng, c, bank, s):
                if c >= 32:
                    return copy(k, eng, rows[:, c - 32, :], bank[0:NH, 0:T2])
                return copy(k, eng, raw[:, c, :] if c < 24 else gate[:, c - 24, :], bank[:, 0:T2])

            project(k, "gdn_in", [(1, P, 0, T2)] * 32 + [(1, NH, 0, T2)] * 2, H[:, :, 0:T2], evict)
            gdn_conv(k, raw, qkv)
        head_norms(k, "q_norm", qkv, range(0, NH), k.ones, P, factor=float(P) ** -0.5, mean=False)
        head_norms(k, "k_norm", qkv, range(NH, 2 * NH), k.ones, P, mean=False)

        with ExitStack() as es2, stage(k, "gdn_gates", "ready lned expd order done") as (block, s):
            tmp = sbuf(k, es2, "tmp", [NH, T2])
            ea = sbuf(k, es2, "ea", [NH, 1])

            @block.vector
            def _(dve):
                order = Order(dve, s.order)
                order(dve.tensor_scalar(rows[:, 0, :], rows[:, 0, :], k.gdn_ab[:, 1:2], None, ALU.add))
                dve.scalar_tensor_tensor(out=tmp[:, :], in0=rows[:, 0, :], scalar=-1.0, in1=rows[:, 0, :], op0=ALU.mult, op1=ALU.max).then_inc(s.ready, 1)
                dve.wait_ge(s.lned, 1)
                order(dve.scalar_tensor_tensor(out=rows[:, 0, :], in0=rows[:, 0, :], scalar=0.0, in1=tmp[:, :], op0=ALU.max, op1=ALU.add))
                order(dve.tensor_scalar(rows[:, 0, :], rows[:, 0, :], ea[:, 0:1], -1.0, ALU.mult, ALU.mult))
                for t0, n in TILES2:
                    last = dve.tensor_tensor_scan(rows[:, 2, t0:t0 + n], k.ones[0:NH, 0:1].broadcast_to([NH, n]),
                                                  rows[:, 0, t0:t0 + n], 0.0, ALU.mult, ALU.add)
                order(last)
                order(dve.tensor_scalar(rows[:, 3, :], rows[:, 2, :], -1.0, None, ALU.mult))

            @block.scalar
            def _(act):
                act.activation(ea[:, :], k.gdn_ab[:, 0:1], ACT.Exp)
                act.wait_ge(s.ready, 1)
                act.activation(tmp[:, :], tmp[:, :], ACT.Exp, scale=-1.0).then_inc(s.expd, 1)
                act.wait_ge(s.expd, 1)
                act.activation(tmp[:, :], tmp[:, :], ACT.Ln, bias=k.one[0:NH, 0:1]).then_inc(s.lned, 1)
                act.activation(rows[:, 1, :], rows[:, 1, :], ACT.Sigmoid)
                act.activation(gate[:, :, :], gate[:, :, :], ACT.Silu)

        with ExitStack() as es3:
            state = sbuf(k, es3, "state", [P, NH, P])
            for i in range(3):
                gdn_tile(k, i, qkv, rows, state, o)
        head_norms(k, "o_norm", o, range(NH), k.ones, P, gain=lambda c: k.small("gdn_o_gain_2")[:, 0:1])
        with stage(k, "gdn_gate", "order") as (block, s):
            @block.vector
            def _(dve):
                dve.tensor_tensor(H[:, :, 0:T2], o[:, :, :], gate[:, :, :], ALU.mult)
    project_residual_2(k, "gdn_out", H[:, :, 0:T2])


def gdn_conv(k, raw, out):
    with stage(k, "gdn_conv", "convolved order") as (block, s):
        w = k.small("gdn_conv_w_2").rearrange("p (tap c) -> p tap c", tap=4)

        @block.vector
        def _(dve):
            order = Order(dve, s.order)
            for g in range(6):
                cs = range(4 * g, 4 * g + 4)
                for c in cs:
                    last = dve.tensor_scalar(out[:, c, :], raw[:, c, :], w[:, 3, c:c + 1], None, ALU.mult)
                order(last)
                for back in (1, 2, 3):
                    for c in cs:
                        last = dve.scalar_tensor_tensor(out=out[:, c, back:T2], in0=raw[:, c, 0:T2 - back], scalar=w[:, 3 - back, c:c + 1],
                                                        in1=out[:, c, back:T2], op0=ALU.mult, op1=ALU.add)
                    if back < 3:
                        order(last)
                last.then_inc(s.convolved, 1)

        @block.scalar
        def _(act):
            for g in range(6):
                act.wait_ge(s.convolved, g + 1)
                act.activation(out[:, 4 * g:4 * g + 4, :], out[:, 4 * g:4 * g + 4, :], ACT.Silu)


def gdn_tile(k, i, qkv, rows, state, o):
    NH = GDN_HEADS
    t0, n = TILES2[i]
    levels = LEVELS if n == P else 4
    cols = slice(t0, t0 + n)
    q, kk, v = (qkv[:, c * NH:(c + 1) * NH, cols] for c in range(3))
    G = 2

    with ExitStack() as es:
        kb = sbuf(k, es, "kb", [P, NH, P])
        kg = sbuf(k, es, "kg", [P, NH, P])
        qg = sbuf(k, es, "qg", [P, NH, P])
        last_decay = sbuf(k, es, "last_decay", [P, NH])
        kT = sbuf(k, es, "kT", [P, NH, P])
        vT = sbuf(k, es, "vT", [P, NH, P])
        A = sbuf(k, es, "A", [P, NH, P])
        U = sbuf(k, es, "U", [P, NH, P])
        X = sbuf(k, es, "X", [P, NH, P])
        XT = sbuf(k, es, "XT", [P, NH, P])
        four = lambda ap, g: ap[:, 4 * g:4 * g + 4, :]
        bank4 = lambda n_bank, m: k.bank[n_bank][0:m, :].rearrange("p (h t) -> p h t", h=4)

        with ExitStack() as es1, stage(k, "gdn_a", "spread beta grown apart faded order made products turned done") as (block, s):
            EB = sbuf(k, es1, "EB", [P, NH, P])
            BB = sbuf(k, es1, "BB", [P, NH, P])
            kd = sbuf(k, es1, "kd", [P, NH, P])
            vb = sbuf(k, es1, "vb", [P, NH, P])
            fade = sbuf(k, es1, "fade", [P, NH, P])
            bl = sbuf(k, es1, "bl", [P, NH])

            @block.tensor
            def _(pe):
                for h in range(NH):
                    pick = k.ident[0:NH, h:h + 1]
                    at = slice((h % 4) * P, (h % 4) * P + n)
                    g = h // 4
                    pe.matmul(k.bank[g][:, at], pick.broadcast_to([NH, P]), rows[:, 2, cols], start=True, stop=True)
                    pe.matmul(k.bank[2 + g][:, at], pick.broadcast_to([NH, P]), rows[:, 1, cols], start=True, stop=True)
                    pe.matmul(k.bank[4 + g][0:n, at], pick.broadcast_to([NH, n]), rows[:, 2, cols], start=True, stop=False)
                    last = pe.matmul(k.bank[4 + g][0:n, at], rows[:, 3, cols], pick.broadcast_to([NH, n]), start=False, stop=True)
                last.then_inc(s.spread, 1)
                pe.wait_ge(s.made, 1)
                for h in range(NH):
                    at = slice((h % 4) * P, (h % 4) * P + n)
                    pe.matmul(k.bank[6 + h // 4][0:n, at], kk[:, h, :], kb[:, h, 0:n], start=True, stop=True)
                    last = pe.matmul(k.bank[2 + h // 4][0:n, at], kk[:, h, :], q[:, h, :], start=True, stop=True)
                last.then_inc(s.products, 1)
                pe.wait_ge(s.made, 2)
                for h in range(NH):
                    at = slice((h % 4) * P, (h % 4 + 1) * P)
                    pe.transpose(k.bank[0 + h // 4][0:n, at], kd[:, h, 0:n], k.ident)
                    last = pe.transpose(k.bank[4 + h // 4][0:n, at], vb[:, h, 0:n], k.ident)
                last.then_inc(s.turned, 1)

            @block.scalar
            def _(act):
                act.wait_ge(s.spread, 1)
                for g in range(G):
                    act.activation(four(EB, g)[:, :, 0:n], bank4(g, P)[:, :, 0:n], ACT.Exp)
                    last = act.copy(four(BB, g)[:, :, 0:n], bank4(2 + g, P)[:, :, 0:n])
                last.then_inc(s.grown, 1)
                act.wait_ge(s.apart, 1)
                act.activation(fade[0:n, :, 0:n], fade[0:n, :, 0:n], ACT.Exp).then_inc(s.faded, 1)
                act.wait_ge(s.apart, 2)
                act.activation(kd[:, :, 0:n], kd[:, :, 0:n], ACT.Exp).then_inc(s.faded, 1)
                act.activation(last_decay[:, :], bl[:, :], ACT.Exp)

            @block.vector
            def _(dve):
                order = Order(dve, s.order)
                dve.wait_ge(s.spread, 1)
                incl = k.const("decay_incl")[0:n, 0:n].unsqueeze(1).broadcast_to([n, 4, n])
                for g in range(G):
                    last = dve.tensor_tensor(fade[0:n, 4 * g:4 * g + 4, 0:n], bank4(4 + g, n)[:, :, 0:n], incl, ALU.add)
                last.then_inc(s.apart, 1)
                dve.wait_ge(s.grown, 1)
                for g in range(G):
                    last = dve.tensor_copy(bl[:, 4 * g:4 * g + 4], bank4(g, P)[:, :, n - 1])
                order(last)
                for g in range(G):
                    last = dve.tensor_tensor(four(kd, g)[:, :, 0:n], bl[:, 4 * g:4 * g + 4].unsqueeze(2).broadcast_to([P, 4, n]),
                                             bank4(g, P)[:, :, 0:n], ALU.subtract)
                last.then_inc(s.apart, 1)
                order(dve.tensor_tensor(kb[:, :, 0:n], kk, BB[:, :, 0:n], ALU.mult))
                dve.tensor_tensor(vb[:, :, 0:n], v, BB[:, :, 0:n], ALU.mult).then_inc(s.made, 1)
                dve.tensor_tensor(qg[:, :, 0:n], q, EB[:, :, 0:n], ALU.mult)
                dve.tensor_tensor(kg[:, :, 0:n], kb[:, :, 0:n], EB[:, :, 0:n], ALU.mult)
                dve.wait_ge(s.faded, 2)
                dve.tensor_tensor(kd[:, :, 0:n], kd[:, :, 0:n], kk, ALU.mult).then_inc(s.made, 1)
                dve.wait_ge(s.products, 1)
                strict = k.const("decay_strict")[0:n, 0:n].unsqueeze(1).broadcast_to([n, 4, n])
                for g in range(G):
                    f4 = fade[0:n, 4 * g:4 * g + 4, 0:n]
                    dve.tensor_tensor(A[0:n, 4 * g:4 * g + 4, 0:n], bank4(2 + g, n)[:, :, 0:n], f4, ALU.mult)
                    last = dve.tensor_tensor(U[0:n, 4 * g:4 * g + 4, 0:n], bank4(6 + g, n)[:, :, 0:n], f4, ALU.mult)
                order(last)
                for g in range(G):
                    u4 = U[0:n, 4 * g:4 * g + 4, 0:n]
                    dve.tensor_tensor(u4, u4, strict, ALU.mult)
                dve.wait_ge(s.turned, 1)
                for g in range(G):
                    dve.tensor_copy(kT[0:n, 4 * g:4 * g + 4, :], bank4(g, n))
                    dve.tensor_copy(vT[0:n, 4 * g:4 * g + 4, :], bank4(4 + g, n))
                eye = k.ident[0:n, 0:n].unsqueeze(1).broadcast_to([n, NH, n])
                dve.tensor_copy(X[0:n, :, 0:n], eye)
                dve.tensor_copy(XT[0:n, :, 0:n], eye)

        with ExitStack() as es1, stage(k, "gdn_inverse", "masked lower copied twice took") as (block, s):
            UM = sbuf(k, es1, "UM", [P, NH, P])
            Z = sbuf(k, es1, "Z", [P, NH, P])
            steps = [(l, g) for l in range(levels) for g in range(G)]
            grp = lambda ap, g: ap[0:n, 4 * g:4 * g + 4, 0:n]

            @block.gpsimd
            def _(pool):
                for j, (l, g) in enumerate(steps):
                    if j >= G:
                        pool.wait_ge(s.lower, j - G + 1)
                    mask = k.fwd[0:n, l, 0:n].unsqueeze(1).broadcast_to([n, 4, n])
                    pool.tensor_tensor(grp(UM, g), grp(U, g), mask, ALU.mult).then_inc(s.masked, 1)

            @block.tensor
            def _(pe):
                def lower(j):
                    l, g = steps[j]
                    pe.wait_ge(s.masked, j + 1)
                    if j >= G:
                        pe.wait_ge(s.took, j - G + 1)
                    for h in range(4):
                        last = pe.matmul(k.bank[g][0:n, h * P:h * P + n], UM[0:n, 4 * g + h, 0:n], X[0:n, 4 * g + h, 0:n],
                                         start=True, stop=True)
                    last.then_inc(s.lower, 1)

                def twice(j):
                    l, g = steps[j]
                    pe.wait_ge(s.copied, j + 1)
                    for h in range(4):
                        hh = 4 * g + h
                        pe.matmul(k.bank[2 + g][0:n, h * P:h * P + n], XT[0:n, hh, 0:n], Z[0:n, hh, 0:n], start=True, stop=True)
                        last = pe.matmul(k.bank[4 + g][0:n, h * P:h * P + n], Z[0:n, hh, 0:n], XT[0:n, hh, 0:n], start=True, stop=True)
                    last.then_inc(s.twice, 1)

                for j in range(0, len(steps), G):
                    for g in range(G):
                        lower(j + g)
                    for g in range(G):
                        twice(j + g)

            @block.scalar
            def _(act):
                for j, (l, g) in enumerate(steps):
                    act.wait_ge(s.lower, j + 1)
                    if j >= G:
                        act.wait_ge(s.twice, j - G + 1)
                    act.copy(grp(Z, g), bank4(g, n)[:, :, 0:n]).then_inc(s.copied, 1)

            @block.vector
            def _(dve):
                for j, (l, g) in enumerate(steps):
                    dve.wait_ge(s.twice, j + 1)
                    dve.tensor_tensor(grp(X, g), grp(X, g), bank4(2 + g, n)[:, :, 0:n], ALU.subtract)
                    dve.tensor_tensor(grp(XT, g), grp(XT, g), bank4(4 + g, n)[:, :, 0:n], ALU.subtract).then_inc(s.took, 1)
                    dve.wait_ge(s.took, j + 1)

        with ExitStack() as es1, stage(k, "gdn_step", "read rest solved new mixed updated order") as (block, s):
            R = sbuf(k, es1, "R", [P, NH, P])
            new = sbuf(k, es1, "new", [P, NH, P])

            @block.tensor
            def _(pe):
                if i > 0:
                    for h in range(NH):
                        last = pe.matmul(k.bank[h // 4][0:n, (h % 4) * P:(h % 4 + 1) * P], kg[:, h, 0:n], state[:, h, :], start=True, stop=True)
                    last.then_inc(s.read, 1)
                pe.wait_ge(s.rest, 1)
                for h in range(NH):
                    last = pe.matmul(k.bank[2 + h // 4][0:n, (h % 4) * P:(h % 4 + 1) * P], XT[0:n, h, 0:n], R[0:n, h, :], start=True, stop=True)
                last.then_inc(s.solved, 1)
                pe.wait_ge(s.new, 1)
                for h in range(NH):
                    out = k.bank[4 + h // 4][:, (h % 4) * P:(h % 4) * P + n]
                    last = pe.matmul(out, new[0:n, h, :], A[0:n, h, 0:n], start=True, stop=(i == 0))
                    if i > 0:
                        last = pe.matmul(out, state[:, h, :], qg[:, h, 0:n], start=False, stop=True)
                last.then_inc(s.mixed, 1)
                if i < 2:
                    for h in range(NH):
                        last = pe.matmul(k.bank[6 + h // 4][:, (h % 4) * P:(h % 4 + 1) * P], kT[0:n, h, :], new[0:n, h, :], start=True, stop=True)
                    last.then_inc(s.updated, 1)

            @block.vector
            def _(dve):
                order = Order(dve, s.order)
                if i > 0:
                    dve.wait_ge(s.read, 1)
                for g in range(G):
                    r4, v4 = R[0:n, 4 * g:4 * g + 4, :], vT[0:n, 4 * g:4 * g + 4, :]
                    if i > 0:
                        last = dve.tensor_tensor(r4, v4, bank4(g, n), ALU.subtract)
                    else:
                        last = dve.tensor_copy(r4, v4)
                last.then_inc(s.rest, 1)
                dve.wait_ge(s.solved, 1)
                for g in range(G):
                    last = dve.tensor_copy(new[0:n, 4 * g:4 * g + 4, :], bank4(2 + g, n))
                last.then_inc(s.new, 1)
                dve.wait_ge(s.mixed, 1)
                for g in range(G):
                    dve.tensor_copy(o[:, 4 * g:4 * g + 4, cols], bank4(4 + g, P)[:, :, 0:n])
                if i == 0:
                    dve.wait_ge(s.updated, 1)
                    for g in range(G):
                        dve.tensor_copy(state[:, 4 * g:4 * g + 4, :], bank4(6 + g, P))
                if i == 1:
                    dve.wait_ge(s.updated, 1)
                    order(dve.tensor_tensor(state[:, :, :], state[:, :, :], last_decay[:, :].unsqueeze(2).broadcast_to([P, NH, P]), ALU.mult))
                    for g in range(G):
                        dve.tensor_tensor(state[:, 4 * g:4 * g + 4, :], state[:, 4 * g:4 * g + 4, :], bank4(6 + g, P), ALU.add)


def swiglu(k):
    with ExitStack() as es:
        high, low = (sbuf(k, es, n, [P, KF, T2], F32R) for n in ("hidden_high", "hidden_low"))
        gate = sbuf(k, es, "gate", [P, 2, T2])
        hidden = sbuf(k, es, "hidden", [P, 2, T2])

        def make_high(act, j, s):
            act.wait_ge(s.dve_took, j + 1)
            act.copy(high[:, j, :], hidden[:, j % 2, :]).then_inc(s.high, 1)

        def make_low(dve, j, s):
            dve.wait_ge(s.high, j + 1)
            dve.tensor_tensor(low[:, j, :], hidden[:, j % 2, :], high[:, j, :].bitcast(F32), ALU.subtract).then_inc(s.low, 1)

        def evict(eng, c, bank, s):
            j = c // 2
            if c % 2 == 0:
                if j >= 1:
                    make_high(eng, j - 1, s)
                return eng.activation(gate[:, j % 2, :], bank[:, 0:T2], ACT.Silu)
            if j >= 1:
                make_low(eng, j - 1, s)
            if j >= 2:
                eng.wait_ge(s.low, j - 1)
            eng.wait_ge(s.act_took, j + 1)
            return eng.tensor_tensor(hidden[:, j % 2, :], gate[:, j % 2, :], bank[:, 0:T2], ALU.mult)

        def finish(eng, s):
            if eng is k.nc.scalar:
                make_high(eng, KF - 1, s)
            else:
                make_low(eng, KF - 1, s)

        project(k, "gate_up", [(1, P, 0, T2)] * (2 * KF), k.H[:, :, 0:T2], evict, extra="high low", finish=finish)
        project_residual_2(k, "down", high[:, :, :], 3, split_x=(high, low))


def join_blocks(k, a):
    with stage(k, "meta", "loaded") as (block, s):
        @block.sync
        def _(sp):
            sp.dma_start(k.Y[:, :, 0:META], a.meta).then_inc(s.loaded, 16)
            sp.wait_ge(s.loaded, 16)
    g = k.small("final_g")
    rms_norm(k, "final", k.X[:, :, SEQ:TWO], SEQ, lambda c: [(0, SEQ, g[:, c:c + 1])], None, k.Y[:, :, META:T2])


def second_block(k, a):
    for i in range(4):
        g = k.small("norm_mix_2")[:, i * KD:(i + 1) * KD]
        rms_norm(k, "mix_norm", k.Y[:, :, :], T2, lambda c: [(0, T2, g[:, c:c + 1])], None, k.H[:, :, 0:T2])
        (lambda: fox(k, a, i // 3), lambda: gla(k, a), lambda: gdn(k, a))[i % 3]()
        g2 = k.small("norm_ffn_2")[:, i * KD:(i + 1) * KD]
        rms_norm(k, "ffn_norm", k.Y[:, :, :], T2, lambda c: [(0, T2, g2[:, c:c + 1])], None, k.H[:, :, 0:T2])
        swiglu(k)



def build(nc, a, out, debug=None):
    k = Program(nc)
    with ExitStack() as es:
        k.small_sb = sbuf(k, es, "small", [P, N_SMALL])
        k.const_sb = sbuf(k, es, "const", [P, N_CONST])
        both = sbuf(k, es, "both", [P, LEVELS + 1, P], I32)
        k.fox_b = sbuf(k, es, "fox_b", [FOX_HEADS, 2])
        k.gdn_ab = sbuf(k, es, "gdn_ab", [GDN_HEADS, 2])
        k.X = sbuf(k, es, "X", [P, KD, TWO])
        k.H = sbuf(k, es, "H", [P, KD, TWO])
        k.ring = sbuf(k, es, "ring", [P, RING, D])
        k.mods = sbuf(k, es, "mods", [P, DEPTH, 48, 2])
        k.gain = sbuf(k, es, "gain", [P, DEPTH, 2, KD, 2])
        k.lower = sbuf(k, es, "lower", [P, DEPTH, 8])
        k.upper = sbuf(k, es, "upper", [P, DEPTH, 8])
        k.back_total = sbuf(k, es, "back_total", [P, HG_HEADS])
        k.qgain = sbuf(k, es, "qgain", [P, 1])
        k.eps = sbuf(k, es, "eps", [P, 1])
        k.one = sbuf(k, es, "one", [P, 1])
        k.bank = [es.enter_context(nc.psum_tensor(f"bank{i}", [P, 512], F32)) for i in range(BANKS)]
        k.small = lambda name: k.small_sb[:, SMALL[name][0]:SMALL[name][0] + SMALL[name][1]]
        k.const = lambda name: k.const_sb[:, CONST[name][0]:CONST[name][0] + CONST[name][1]]
        k.ident, k.ones, k.ones64, k.causal = (k.const(n) for n in ("ident", "ones", "ones64", "causal"))
        k.fwd = k.const("fwd").rearrange("p (l n) -> p l n", l=LEVELS)
        k.both = both
        k.landed = [nc.alloc_semaphore(f"landed{i}") for i in range(RING)]
        k.unit_done = nc.alloc_semaphore("unit_done")
        k.stored = nc.alloc_semaphore("stored")
        k.units = plan_weights(a)

        with stage(k, "load", "loaded") as (block, s):
            @block.sync
            def _(sp):
                for dst, src in ((k.small_sb[:, :], a.small), (k.const_sb[:, :], a.const), (both[:, :, :], a.both),
                                 (k.fox_b[:, :], a.fox_b), (k.gdn_ab[:, :], a.gdn_ab), (k.X[:, :, :], a.tokens)):
                    sp.dma_start(dst, src).then_inc(s.loaded, 16)
                for u in range(RING):
                    load_unit(k, sp, u)
                sp.wait_ge(s.loaded, 16 * 6)

            @block.vector
            def _(dve):
                dve.memset(k.eps[:, :], EPS)
                dve.memset(k.one[:, :], 1.0)

        if debug is not None:
            debug(k, a, out)
            return
        first_block(k, a)
        k.Y = sbuf(k, es, "Y", [P, KD, T2])
        join_blocks(k, a)
        second_block(k, a)
        store(k, k.Y[:, :, META:T2], out)


def store(k, src, out):
    with stage(k, "store", "") as (block, s):
        @block.sync
        def _(sp):
            sp.dma_start(out, src).then_inc(k.stored, 16)
            sp.wait_ge(k.stored, 16)


def features(v):
    return np.asarray(v).reshape(-1, P).T


def weights(w, cols=None):
    w = np.asarray(w)
    *lead, K, N = w.shape
    w = w.reshape(*lead, K // P, P, N // P, P)
    n = len(lead)
    return np.ascontiguousarray(w.transpose(*range(n), n + 2, n + 1, n, n + 3).reshape(*lead, N // P, P, K))


def narrow(w):
    w = np.asarray(w)
    *lead, K, n = w.shape
    d = len(lead)
    return np.ascontiguousarray(w.reshape(*lead, K // P, P, n).transpose(*range(d), d + 1, d, d + 2).reshape(*lead, P, K // P * n))


def lay_out(i):
    A = {}
    i = {n: np.asarray(v) for n, v in i.items()}
    small = np.empty((P, N_SMALL), np.float32)
    twice = lambda v: np.concatenate([v, v], axis=-1)
    for name, (at, n) in SMALL.items():
        v = twice(i[name]) if name.startswith("fox_") else i[name]
        small[:, at:at + n] = features(v)
    A["small"] = small
    const, both, _ = constants()
    A["const"], A["both"] = const, both.reshape(P, LEVELS + 1, P)
    A["fox_b"] = np.ascontiguousarray(i["fox_b_f_2"].T)
    A["gdn_ab"] = np.ascontiguousarray(np.concatenate([i["gdn_a_log_2"], i["gdn_dt_bias_2"]]).T)
    fm = lambda x: np.ascontiguousarray(x.T.reshape(KD, P, -1).transpose(1, 0, 2))
    A["tokens"] = fm(np.concatenate([i["ctx"][0], i["x"][0]]))
    A["meta"] = fm(i["meta_tokens_2"])
    for name in ("w_mod", "w_in", "w_out", "peer_wq", "w_gate_up_2", "w_down_2", "fox_w_out_2", "gla_w_out_2", "gdn_w_out_2"):
        A[name] = weights(i[name])
    for name, n, extra in (("fox_w_in_2", 4 * D, "fox_w_f"), ("gla_w_in_2", 3 * D, "gla_w_a"), ("gdn_w_in_2", 4 * D, "gdn_w_ab")):
        A[name] = weights(i[name][:, :, :n])
        over = i[name][:, :, n:]
        A[extra] = np.stack([narrow(over[:, :, c:c + 8]) for c in (0, 8)], 1) if extra == "gdn_w_ab" else narrow(over)[:, None]
    A["gla_w_alpha2_2"] = np.ascontiguousarray(i["gla_w_alpha2_2"])
    sk = i["peer_subkeys"]
    A["peer_subkeys"] = np.ascontiguousarray(sk.reshape(DEPTH, 2 * PEER_HEADS, N_KEYS, P).transpose(0, 3, 1, 2))
    for l in range(DEPTH):
        A[f"peer_u{l}"], A[f"peer_v{l}"] = np.ascontiguousarray(i["peer_u"][l]), np.ascontiguousarray(i["peer_v"][l])
    return A


def declare(nc, A):
    aps = {n: nc.dram_tensor(f"in_{n}", v.shape, mybir.dt.from_np(v.dtype), kind="ExternalInput").ap() for n, v in A.items()}
    aps["peer_u"] = [aps[f"peer_u{l}"] for l in range(DEPTH)]
    aps["peer_v"] = [aps[f"peer_v{l}"] for l in range(DEPTH)]
    return namedtuple("Inputs", list(aps))(**aps)


def kernel(**inputs):
    import concourse.bacc as bacc
    from concourse.bass_utils import run_bass_kernel_spmd as run

    nc = bacc.Bacc("TRN2", target_bir_lowering=False, num_devices=1)
    A = lay_out(inputs)
    a = declare(nc, A)
    out = nc.dram_tensor("out", (P, KD, SEQ), F32, kind="ExternalOutput").ap()
    build(nc, a, out)
    r = run(nc, [{f"in_{n}": v for n, v in A.items()}], core_ids=[0])
    y = np.asarray(r.results[0]["out"])
    return np.ascontiguousarray(y.transpose(2, 1, 0).reshape(1, SEQ, D))
```

```python
import numpy as np
from collections import namedtuple
from contextlib import ExitStack, contextmanager

import concourse.bass as bass
from concourse import mybir
from concourse.alu_op_type import AluOpType as ALU

F32 = mybir.dt.float32
F32R = mybir.dt.float32r
I32 = mybir.dt.int32
U32 = mybir.dt.uint32
ACT = mybir.ActivationFunctionType
AX = mybir.AxisListType.X

P = 128
D = 1024
KD = D // P
EPS = 1e-6

SEQ = 256
TWO = 2 * SEQ
DEPTH = 2
HG_HEADS = 4
GRID_W = 64
PEER_HEADS = 8
TOPK = 16
N_KEYS = 128
SEL = PEER_HEADS * TOPK
LEVELS = 7

META = 16
T2 = META + SEQ
TILES2 = ((0, 128), (128, 128), (256, 16))
FOX_HEADS = 16
DK_FOX = 64
GDN_HEADS = 8
D_FF = 2816
KF = D_FF // P

RING = 6
SPLIT = 3
BANKS = 8
NEG = -1e30

SMALL = {}


def small_columns():
    at = 0
    for name, n in (("c_ctx", KD), ("c", KD), ("b_mod", DEPTH * 48), ("norm1_g", DEPTH * KD),
                    ("norm2_g", DEPTH * KD), ("conv_w", DEPTH * 12), ("lb_logits", DEPTH * 8),
                    ("final_g", KD), ("norm_mix_2", 4 * KD), ("norm_ffn_2", 4 * KD),
                    ("fox_q_gain_2", 2), ("fox_k_gain_2", 2), ("gla_b_alpha_2", 4),
                    ("gla_o_gain_2", 2), ("gdn_conv_w_2", 96), ("gdn_o_gain_2", 1)):
        SMALL[name] = (at, n)
        at += n
    return at


N_SMALL = small_columns()

CONST = {}


def const_columns():
    at = 0
    for name, n in (("ident", P), ("ones", P), ("ones64", P), ("causal", 3 * P), ("decay_incl", P),
                    ("decay_strict", P), ("fwd", LEVELS * P), ("iota", TOPK), ("pick", FOX_HEADS), ("fold", 2)):
        CONST[name] = (at, n)
        at += n
    return at


N_CONST = const_columns()


def constants():
    c = np.zeros((P, N_CONST), np.float32)

    def put(name, value):
        a, n = CONST[name]
        c[:, a:a + n] = value

    i = np.arange(P)
    put("ident", np.eye(P))
    put("ones", 1.0)
    put("ones64", (i[:, None] // 64) == (i[None, :] // 64))
    put("causal", np.concatenate([np.zeros((P, 2 * P)), np.where(i[None, :] > i[:, None], NEG, 0.0)], 1))
    put("decay_incl", np.where(i[:, None] > i[None, :], NEG, 0.0))
    put("decay_strict", np.where(i[:, None] < i[None, :], 1.0, 0.0))
    both = np.zeros((P, LEVELS + 1, P), np.int32)
    fwd = np.zeros((P, LEVELS, P), np.float32)
    for l in range(LEVELS):
        m = 1 << l
        same = (i[:, None] // (2 * m)) == (i[None, :] // (2 * m))
        left = (i // m) % 2 == 0
        fwd[:, l] = same & left[:, None] & ~left[None, :]
        both[:, l] = same & (left[:, None] != left[None, :])
    both[:, LEVELS] = np.eye(P)
    put("fwd", fwd.reshape(P, -1))
    put("iota", np.arange(TOPK)[None, :])
    put("pick", sum((i[:, None] == np.arange(FOX_HEADS)[None, :] + r) for r in (0, 64)))
    put("fold", (i[:, None] % 2) == np.arange(2)[None, :])
    return c, both.reshape(P, -1)


class Program:

    def __init__(self, nc):
        self.nc, self.stages, self.used, self.done = nc, 0, 0, 0


@contextmanager
def stage(k, name, signals):
    k.stages += 1
    sems = [k.nc.alloc_semaphore(f"{name}_{s}_{k.stages}") for s in signals.split()]
    with k.nc.Block(no_gpsimd_drain=True) as block:
        yield block, namedtuple("Signals", signals)(*sems)
    if sems:
        k.nc.clear_and_free_semaphores(sems)
    k.nc.all_engine_barrier()


def sbuf(k, es, name, shape, dtype=F32):
    k.stages += 1
    return es.enter_context(k.nc.sbuf_tensor(f"{name}_{k.stages}", shape, dtype))


class Order:

    def __init__(self, eng, sem):
        self.eng, self.sem, self.n = eng, sem, 0

    def __call__(self, ins):
        self.n += 1
        ins.then_inc(self.sem, 1)
        self.eng.wait_ge(self.sem, self.n)


def load_tables(act):
    act.preload_act_table_set("natural_log_exp_and_others")



def plan_weights(a):
    units = []

    def chunks(w, order):
        for c in order:
            units.append((w[c], w.shape[-1]))

    for l in range(DEPTH):
        chunks(a.w_mod[l], range(48))
    for l in range(DEPTH):
        chunks(a.w_in[l], range(32))
        chunks(a.w_out[l], range(8))
        chunks(a.peer_wq[l], range(16))
    for i in range(4):
        kind, j = i % 3, i // 3
        w_in, extra, w_out = {0: (a.fox_w_in_2, a.fox_w_f, a.fox_w_out_2), 1: (a.gla_w_in_2, a.gla_w_a, a.gla_w_out_2),
                              2: (a.gdn_w_in_2, a.gdn_w_ab, a.gdn_w_out_2)}[kind]
        chunks(w_in[j], range(w_in.shape[1]))
        chunks(extra[j], range(extra.shape[1]))
        chunks(w_out[j], range(8))
        gate_up = a.w_gate_up_2[i]
        for c in range(KF):
            chunks(gate_up, (c, KF + c))
        for c in range(KD):
            for k0 in range(0, KF, KD):
                n = min(KD, KF - k0) * P
                units.append((a.w_down_2[i][c][:, k0 * P:k0 * P + n], n))
    return units


def load_unit(k, sp, u):
    if u < len(k.units):
        src, n = k.units[u]
        sp.dma_start(k.ring[:, u % RING, 0:n], src).then_inc(k.landed[u % RING], 16)


class Norm:
    signals = "squares added sum logged root scaled shifted"

    def __init__(self, k, x, T, gain, shift, out):
        self.k, self.x, self.T, self.gain, self.shift, self.out = k, x, T, gain, shift, out

    def place(self, es):
        k, T = self.k, self.T
        self.sq = self.out
        self.total = sbuf(k, es, "total", [P, T])
        self.rstd = self.total
        self.bank = k.bank[BANKS - 1][:, 0:T]

    def done(self, s):
        return s.scaled if self.shift is None else s.shifted

    def act_squares(self, act, s):
        for c in range(KD):
            act.activation(self.sq[:, c, :], self.x[:, c, :], ACT.Square).then_inc(s.squares, 1)

    def act_root(self, act, s):
        act.wait_ge(s.sum, 1)
        act.activation(self.rstd[:, :], self.bank, ACT.Ln, scale=1.0 / D, bias=self.k.eps[:, 0:1]).then_inc(s.logged, 1)
        act.wait_ge(s.logged, 1)
        act.activation(self.rstd[:, :], self.rstd[:, :], ACT.Exp, scale=-0.5).then_inc(s.root, 1)

    def act_shift(self, act, s, c):
        if self.shift is not None:
            act.wait_ge(s.scaled, c + 1)
            for (t0, n, g), (_, _, b) in zip(self.gain(c), self.shift(c)):
                part = self.out[:, c, t0:t0 + n]
                last = act.activation(part, part, ACT.Identity, bias=b, scale=g)
            last.then_inc(s.shifted, 1)

    def pe_sum(self, pe, s):
        pe.wait_ge(s.added, KD - 1)
        pe.matmul(self.bank, self.k.ones, self.total[:, :], start=True, stop=True).then_inc(s.sum, 1)

    def dve_add(self, dve, s):
        for c in range(1, KD):
            dve.wait_ge(s.squares, c + 1)
            if c > 1:
                dve.wait_ge(s.added, c - 1)
            dve.tensor_tensor(self.total[:, :], self.sq[:, 0, :] if c == 1 else self.total[:, :], self.sq[:, c, :],
                              ALU.add).then_inc(s.added, 1)

    def dve_scale(self, dve, s, c):
        if c == 0:
            dve.wait_ge(s.root, 1)
        if self.shift is not None:
            last = dve.tensor_tensor(self.out[:, c, :], self.x[:, c, :], self.rstd[:, :], ALU.mult)
        else:
            for t0, n, g in self.gain(c):
                last = dve.scalar_tensor_tensor(out=self.out[:, c, t0:t0 + n], in0=self.x[:, c, t0:t0 + n], scalar=g,
                                                in1=self.rstd[:, t0:t0 + n], op0=ALU.mult, op1=ALU.mult)
        last.then_inc(s.scaled, 1)


def rms_norm(k, name, x, T, gain, out):
    norm = Norm(k, x, T, gain, None, out)
    with ExitStack() as es, stage(k, name, norm.signals) as (block, s):
        norm.place(es)

        @block.scalar
        def _(act):
            norm.act_squares(act, s)
            norm.act_root(act, s)

        @block.tensor
        def _(pe):
            norm.pe_sum(pe, s)

        @block.vector
        def _(dve):
            norm.dve_add(dve, s)
            for c in range(KD):
                norm.dve_scale(dve, s, c)


def project(k, name, outs, x, evict, by=None, extra="", finish=None, split_x=None, norm=None, tables=False):
    by = by or (lambda c: c % 2)
    first, n_units = k.used, sum(o[0] for o in outs)
    k.used += n_units
    before = k.done
    k.done += n_units
    KT, T = x.shape[1], x.shape[2]
    unit_of = []
    for c, o in enumerate(outs):
        unit_of += [(c, j) for j in range(o[0])]
    signals = " ".join(["act_took dve_took x_high x_low w_high w_low", extra] + ([norm.signals] if norm else []))
    with ExitStack() as es, stage(k, name, signals) as (block, s):
        if split_x is None:
            high, low = (sbuf(k, es, n, [P, KT, T], F32R) for n in ("x_high", "x_low"))
        else:
            high, low = split_x
        w_high, w_low = (sbuf(k, es, n, [P, SPLIT, D], F32R) for n in ("w_high", "w_low"))
        took = (s.act_took, s.dve_took)
        if norm is not None:
            norm.place(es)

        at_once = 1 if norm is None else SPLIT

        def width(u):
            return k.units[first + u][1]

        @block.sync
        def _(sp):
            for u in range(n_units):
                sp.wait_ge(s.w_low, u + 1)
                load_unit(k, sp, first + u + RING)

        @block.tensor
        def _(pe):
            if norm is not None:
                norm.pe_sum(pe, s)
            for u, (c, j) in enumerate(unit_of):
                n, m, t0, nt = outs[c]
                if j == 0 and c >= BANKS:
                    old = c - BANKS
                    pe.wait_ge(took[by(old)], sum(by(i) == by(old) for i in range(old + 1)))
                pe.wait_ge(s.w_low, u + 1)
                slot = u % SPLIT
                for i in range(min(KD, KT - j * KD)):
                    t = j * KD + i
                    if u == 0 and split_x is None:
                        pe.wait_ge(s.x_low, t + 1)
                    cols = slice(i * m, i * m + P)
                    for n_pass, (w, xx) in enumerate(((w_high, high), (w_high, low), (w_low, high))):
                        last = pe.matmul(k.bank[c % BANKS][:, 0:nt], w[:, slot, cols], xx[:, t, t0:t0 + nt],
                                         start=(t == 0 and n_pass == 0), stop=(t == KT - 1 and n_pass == 2))
                last.then_inc(k.unit_done, 1)

        def each(eng, mine, make, begin, sem):
            begin(lambda u0, u1: [make(u).then_inc(sem, 1) for u in range(u0, min(u1, n_units))])
            made = min(SPLIT, n_units)
            for u, (c, j) in enumerate(unit_of):
                while made < min(n_units, u + SPLIT):
                    eng.wait_ge(k.unit_done, before + made - SPLIT + 1)
                    make(made).then_inc(sem, 1)
                    made += 1
                if j == outs[c][0] - 1 and by(c) == mine:
                    eng.wait_ge(k.unit_done, before + u + 1)
                    evict(eng, c, k.bank[c % BANKS], s).then_inc(took[mine], 1)
            if finish is not None:
                finish(eng, s)

        @block.scalar
        def _(act):
            def make(u):
                act.wait_ge(k.landed[(first + u) % RING], 16 * ((first + u) // RING + 1))
                return act.copy(w_high[:, u % SPLIT, 0:width(u)], k.ring[:, (first + u) % RING, 0:width(u)])

            def begin(first_units):
                if norm is not None:
                    norm.act_squares(act, s)
                first_units(0, at_once)
                if norm is not None:
                    norm.act_root(act, s)
                if split_x is None:
                    for t in range(KT):
                        if norm is not None:
                            norm.act_shift(act, s, t)
                            act.wait_ge(norm.done(s), t + 1)
                        act.copy(high[:, t, :], x[:, t, :]).then_inc(s.x_high, 1)
                first_units(at_once, SPLIT)

            each(act, 0, make, begin, s.w_high)
            if tables:
                load_tables(act)

        @block.vector
        def _(dve):
            def make(u):
                dve.wait_ge(s.w_high, u + 1)
                n = width(u)
                return dve.tensor_tensor(w_low[:, u % SPLIT, 0:n], k.ring[:, (first + u) % RING, 0:n],
                                         w_high[:, u % SPLIT, 0:n].bitcast(F32), ALU.subtract)

            def begin(first_units):
                if norm is not None:
                    norm.dve_add(dve, s)
                first_units(0, at_once)
                if norm is not None:
                    norm.dve_scale(dve, s, 0)
                if split_x is None:
                    for t in range(KT):
                        if norm is not None and t + 1 < KT:
                            norm.dve_scale(dve, s, t + 1)
                        dve.wait_ge(s.x_high, t + 1)
                        dve.tensor_tensor(low[:, t, :], x[:, t, :], high[:, t, :].bitcast(F32), ALU.subtract).then_inc(s.x_low, 1)
                first_units(at_once, SPLIT)

            each(dve, 1, make, begin, s.w_low)


def copy(k, eng, out, in_):
    if eng is k.nc.scalar:
        return eng.copy(out, in_)
    return eng.tensor_copy(out, in_)



def transpose_chunks(k, name, jobs):
    groups = [jobs[i:i + 4] for i in range(0, len(jobs), 4)]
    with stage(k, name, "turned act_took dve_took") as (block, s):

        @block.tensor
        def _(pe):
            for g, group in enumerate(groups):
                if g >= BANKS:
                    pe.wait_ge((s.act_took, s.dve_took)[g % 2], (g - BANKS) // 2 + 1)
                for i, (out, in_) in enumerate(group):
                    m, n = in_.shape
                    last = pe.transpose(k.bank[g % BANKS][0:n, i * P:i * P + m], in_, k.ident[0:m, 0:m])
                last.then_inc(s.turned, 1)

        def take(eng, mine, took):
            for g, group in enumerate(groups):
                if g % 2 == mine:
                    eng.wait_ge(s.turned, g + 1)
                    for i, (out, in_) in enumerate(group):
                        m, n = in_.shape
                        last = copy(k, eng, out, k.bank[g % BANKS][0:n, i * P:i * P + m])
                    last.then_inc(took, 1)

        @block.scalar
        def _(act):
            take(act, 0, s.act_took)

        @block.vector
        def _(dve):
            take(dve, 1, s.dve_took)



def modulation(k):
    with ExitStack() as es:
        cond = sbuf(k, es, "cond", [P, KD, 2])
        parts = sbuf(k, es, "parts", [P, KD, 2, 2], F32R)
        with stage(k, "cond", "done high") as (block, s):
            @block.scalar
            def _(act):
                act.activation(cond[:, :, 0], k.small("c_ctx"), ACT.Silu)
                act.activation(cond[:, :, 1], k.small("c"), ACT.Silu).then_inc(s.done, 1)
                act.wait_ge(s.done, 1)
                act.copy(parts[:, :, 0, :], cond[:, :, :]).then_inc(s.high, 1)

            @block.vector
            def _(dve):
                dve.wait_ge(s.high, 1)
                dve.tensor_tensor(parts[:, :, 1, :], cond[:, :, :], parts[:, :, 0, :].bitcast(F32), ALU.subtract)

        n_units, first = DEPTH * 48, k.used
        n_groups = n_units // 4
        k.used += n_units
        with stage(k, "modulate", "w_high w_low took turned added multiplied") as (block, s):
            rows = sbuf(k, es, "rows", [4, 2, 4 * P])
            w_high, w_low = (sbuf(k, es, n, [P, 2, 4, D], F32R) for n in ("w_high", "w_low"))
            fold = k.const("fold")[0:4, :]

            @block.sync
            def _(sp):
                for u in range(n_units):
                    sp.wait_ge(s.w_low, u + 1)
                    load_unit(k, sp, u + RING)

            @block.tensor
            def _(pe):
                def turn(g):
                    pe.wait_ge(s.took, g + 1)
                    if g >= 2:
                        pe.wait_ge(s.added, g - 1)
                    for i in range(4):
                        last = pe.matmul(k.bank[4 + g % 2][:, 2 * i:2 * i + 2], rows[:, g % 2, i * P:(i + 1) * P], fold,
                                         start=True, stop=True)
                    last.then_inc(s.turned, 1)

                for g in range(n_groups):
                    if g >= 4:
                        pe.wait_ge(s.took, g - 3)
                    pe.wait_ge(s.w_low, 4 * g + 4)
                    for t in range(KD):
                        for n_pass, w in enumerate((w_high, w_low)):
                            last = pe.matmul(k.bank[g % 4][0:4, :], parts[:, t, :, :].rearrange("p a b -> p (a b)"),
                                             w[:, g % 2, :, t * P:(t + 1) * P], start=(t == 0 and n_pass == 0), stop=(t == KD - 1 and n_pass == 1))
                    last.then_inc(s.multiplied, 1)
                    if g >= 1:
                        turn(g - 1)
                turn(n_groups - 1)

            @block.scalar
            def _(act):
                for g in range(n_groups + 1):
                    for u in range(4 * g, min(4 * g + 4, n_units)):
                        if g >= 2:
                            act.wait_ge(s.multiplied, g - 1)
                        act.wait_ge(k.landed[u % RING], 16 * (u // RING + 1))
                        act.copy(w_high[:, g % 2, u % 4, :], k.ring[:, u % RING, :]).then_inc(s.w_high, 1)
                    if g >= 1:
                        act.wait_ge(s.multiplied, g)
                        if g >= 3:
                            act.wait_ge(s.turned, g - 2)
                        act.copy(rows[:, (g - 1) % 2, :], k.bank[(g - 1) % 4][0:4, :]).then_inc(s.took, 1)

            @block.vector
            def _(dve):
                def take(g):
                    dve.wait_ge(s.turned, g + 1)
                    l, c = divmod(4 * g, 48)
                    bias = k.small("b_mod")[:, 4 * g:4 * g + 4].unsqueeze(2).broadcast_to([P, 4, 2])
                    dve.tensor_tensor(k.mods[:, l, c:c + 4, :], k.bank[4 + g % 2][:, 0:8].rearrange("p (c q) -> p c q", q=2),
                                      bias, ALU.add).then_inc(s.added, 1)

                for g in range(n_groups):
                    for u in range(4 * g, 4 * g + 4):
                        dve.wait_ge(s.w_high, u + 1)
                        dve.tensor_tensor(w_low[:, g % 2, u % 4, :], k.ring[:, u % RING, :], w_high[:, g % 2, u % 4, :].bitcast(F32),
                                          ALU.subtract).then_inc(s.w_low, 1)
                    if g >= 2:
                        take(g - 2)
                take(n_groups - 2)
                take(n_groups - 1)

    with ExitStack() as es, stage(k, "bounds", "order exps subs") as (block, s):
        lb = k.small("lb_logits").rearrange("p (l n) -> p l n", l=DEPTH)
        top = sbuf(k, es, "top", [P, 8])
        e = sbuf(k, es, "e", [P, DEPTH, 8])
        total = sbuf(k, es, "total", [P, 8])

        @block.vector
        def _(dve):
            order = Order(dve, s.order)
            for l in range(DEPTH):
                for n, (scale0, name) in enumerate(((8, "norm1_g"), (32, "norm2_g"))):
                    g = k.small(name)[:, l * KD:(l + 1) * KD].unsqueeze(2).broadcast_to([P, KD, 2])
                    dve.scalar_tensor_tensor(out=k.gain[:, l, n, :, :], in0=k.mods[:, l, scale0:scale0 + KD, :],
                                             scalar=1.0, in1=g, op0=ALU.add, op1=ALU.mult)
            order(dve.tensor_tensor(top[:, :], lb[:, 0, :], lb[:, 1, :], ALU.max))
            for l in range(DEPTH):
                dve.tensor_tensor(e[:, l, :], lb[:, l, :], top[:, :], ALU.subtract).then_inc(s.subs, 1)
            dve.wait_ge(s.exps, 1)
            order(dve.tensor_tensor(total[:, :], e[:, 0, :], e[:, 1, :], ALU.add))
            order(dve.reciprocal(total[:, :], total[:, :]))
            for l in range(DEPTH):
                order(dve.tensor_tensor(e[:, l, :], e[:, l, :], total[:, :], ALU.mult))
            order(dve.tensor_tensor(total[:, :], e[:, 0, :], e[:, 1, :], ALU.add))
            order(dve.tensor_tensor(k.lower[:, 0, :], e[:, 0, :], e[:, 0, :], ALU.subtract))
            order(dve.tensor_tensor(k.lower[:, 1, :], total[:, :], e[:, 0, :], ALU.subtract))
            order(dve.tensor_scalar(k.upper[:, :, :], k.lower[:, :, :], -1.0, 1.0, ALU.mult, ALU.add))

        @block.scalar
        def _(act):
            load_tables(act)
            act.wait_ge(s.subs, 2)
            act.activation(e[:, :, :], e[:, :, :], ACT.Exp).then_inc(s.exps, 1)


def both_ways(gain):
    return lambda c: [(0, SEQ, gain(c)[:, 0:1]), (SEQ, SEQ, gain(c)[:, 1:2])]


def halves(ap, m, side):
    return ap.rearrange("p h (n two m) -> p h n two m", two=2, m=m)[:, :, :, side, :]


def hgrn_gates(k, l, z, bc, key):
    with ExitStack() as es, stage(k, "gates", "sig keyed logs order fed") as (block, s):
        low = sbuf(k, es, "low", [P, 2, HG_HEADS, SEQ])
        high = sbuf(k, es, "high", [P, 2, HG_HEADS, SEQ])

        @block.scalar
        def _(act):
            for d in range(2):
                act.activation(high[:, d, :, :], z[:, d * HG_HEADS:(d + 1) * HG_HEADS, :], ACT.Sigmoid).then_inc(s.sig, 1)
            for d in range(2):
                act.activation(key[:, d, :, :], z[:, d * HG_HEADS:(d + 1) * HG_HEADS, :], ACT.Sigmoid, scale=-1.0).then_inc(s.keyed, 1)
            load_tables(act)
            for d in range(2):
                act.wait_ge(s.fed, d + 1)
                act.activation(low[:, d, :, :], low[:, d, :, :], ACT.Ln).then_inc(s.logs, 1)
                act.activation(high[:, d, :, :], high[:, d, :, :], ACT.Ln).then_inc(s.logs, 1)

        @block.gpsimd
        def _(pool):
            for d in range(2):
                pool.wait_ge(s.keyed, d + 1)
                up = k.upper[:, l, d * HG_HEADS:(d + 1) * HG_HEADS].unsqueeze(2).broadcast_to([P, HG_HEADS, SEQ])
                pool.tensor_tensor(key[:, d, :, :], key[:, d, :, :], up, ALU.mult)

        @block.vector
        def _(dve):
            order = Order(dve, s.order)
            for d in range(2):
                dve.wait_ge(s.sig, d + 1)
                for h in range(HG_HEADS):
                    i = d * HG_HEADS + h
                    last = dve.tensor_scalar(high[:, d, h, :], high[:, d, h, :], k.upper[:, l, i:i + 1], k.lower[:, l, i:i + 1], ALU.mult, ALU.add)
                order(last)
                order(dve.tensor_scalar(low[:, d, :, :], high[:, d, :, :], 1e-20, 2.0 ** 60, ALU.max, ALU.mult))
                dve.tensor_scalar(low[:, d, :, :], low[:, d, :, :], 1.0, None, ALU.min)
                dve.tensor_scalar(high[:, d, :, :], high[:, d, :, :], 2.0 ** -60, None, ALU.max).then_inc(s.fed, 1)
            one = k.ones[:, 0:1].broadcast_to([P, SEQ])
            for d in range(2):
                dve.wait_ge(s.logs, 2 * d + 2)
                order(dve.tensor_tensor(high[:, d, :, :], high[:, d, :, :], low[:, d, :, :], ALU.add))
                for h in range(HG_HEADS):
                    last = dve.tensor_tensor_scan(bc[:, d, h, :], one, high[:, d, h, :], 0.0, ALU.mult, ALU.add)
                order(last)
            order(dve.tensor_tensor(bc[:, 1, :, :], high[:, 1, :, :], bc[:, 1, :, :], ALU.subtract))
            order(dve.tensor_tensor(k.back_total[:, :], high[:, 1, :, SEQ - 1], bc[:, 1, :, SEQ - 1], ALU.subtract))


def hgrn_attention(k, q, key, bc, att, gate):
    with ExitStack() as es, stage(k, "attend", "first_apart apart decayed scaled scored took") as (block, s):
        dif = sbuf(k, es, "dif", [P, 3, 2, HG_HEADS, SEQ])
        kh = sbuf(k, es, "kh", [P, 2, HG_HEADS, SEQ])
        qh = sbuf(k, es, "qh", [P, 2, HG_HEADS, SEQ])
        steps = LEVELS + 2
        shape = lambda m: [P, HG_HEADS, SEQ // (2 * m), m]

        def differences(eng, j):
            m = 1 << (j - 1)
            for d in range(2):
                b = bc[:, d, :, :]
                out = dif[:, j % 3, d, :, :]
                mid = (halves(b, m, 0)[:, :, :, m - 1:m] if d == 0 else halves(b, m, 1)[:, :, :, 0:1]).broadcast_to(shape(m))
                near, far = (0, 1) if d == 0 else (1, 0)
                eng.tensor_tensor(halves(out, m, near), mid, halves(b, m, near), ALU.subtract)
                last = eng.tensor_tensor(halves(out, m, far), halves(b, m, far), mid, ALU.subtract)
            return last

        @block.gpsimd
        def _(pool):
            for j in range(2, steps):
                if j >= 4:
                    pool.wait_ge(s.scaled, j - 2)
                differences(pool, j).then_inc(s.apart, 1)

        @block.scalar
        def _(act):
            act.activation(gate, gate, ACT.Silu)
            load_tables(act)
            for j in range(1, steps):
                if j == 1:
                    act.wait_ge(s.first_apart, 1)
                else:
                    act.wait_ge(s.apart, j - 1)
                act.activation(dif[:, j % 3, :, :, :], dif[:, j % 3, :, :, :], ACT.Exp).then_inc(s.decayed, 1)

        @block.vector
        def _(dve):
            def factors(j):
                if j >= 2:
                    dve.wait_ge(s.scored, j - 1)
                ks, qs = kh[:, j % 2, :, :], qh[:, j % 2, :, :]
                if j == 0:
                    dve.tensor_tensor(ks, key[:, 0, :, :], key[:, 1, :, :], ALU.add)
                    dve.tensor_copy(qs, q).then_inc(s.scaled, 1)
                    return
                m = 1 << (j - 1)
                dve.wait_ge(s.decayed, j)
                fwd, back = dif[:, j % 3, 0, :, :], dif[:, j % 3, 1, :, :]
                dve.tensor_tensor(halves(ks, m, 0), halves(key[:, 0, :, :], m, 0), halves(fwd, m, 0), ALU.mult)
                dve.tensor_tensor(halves(ks, m, 1), halves(key[:, 1, :, :], m, 1), halves(back, m, 1), ALU.mult)
                dve.tensor_tensor(halves(qs, m, 1), halves(q, m, 1), halves(fwd, m, 1), ALU.mult)
                dve.tensor_tensor(halves(qs, m, 0), halves(q, m, 0), halves(back, m, 0), ALU.mult).then_inc(s.scaled, 1)

            def take(j):
                dve.wait_ge(s.scored, j + 1)
                for i in range(2):
                    data = k.bank[2 * (j % 2) + i][:, :].rearrange("p (h t) -> p h t", h=HG_HEADS)
                    own = att[:, i, :, i * P:(i + 1) * P]
                    if j == 0:
                        last = dve.tensor_copy(own, data)
                    elif j == steps - 1:
                        last = dve.tensor_copy(att[:, i, :, (1 - i) * P:(2 - i) * P], data)
                    else:
                        mask = k.both[:, j - 1, :].unsqueeze(1).broadcast_to([P, HG_HEADS, P])
                        last = dve.copy_predicated(own, mask, data)
                last.then_inc(s.took, 1)
                dve.wait_ge(s.took, j + 1)

            differences(dve, 1).then_inc(s.first_apart, 1)
            factors(0)
            for j in range(1, steps):
                factors(j)
                take(j - 1)
            take(steps - 1)

        @block.tensor
        def _(pe):
            for j in range(steps):
                pe.wait_ge(s.scaled, j + 1)
                if j >= 2:
                    pe.wait_ge(s.took, j - 1)
                for i in range(2):
                    t = i if j < steps - 1 else 1 - i
                    for h in range(HG_HEADS):
                        last = pe.matmul(k.bank[2 * (j % 2) + i][:, h * P:(h + 1) * P],
                                         kh[:, j % 2, h, i * P:(i + 1) * P], qh[:, j % 2, h, t * P:(t + 1) * P],
                                         start=True, stop=True)
                last.then_inc(s.scored, 1)


def hgrn_outputs(k, s0, q, gate, key, bc, att, from_state, out, conv):
    with ExitStack() as es, stage(k, "outputs", "shifted grown fed mixed squares sums logged root order conv") as (block, s):
        conv.place(es)
        grow = sbuf(k, es, "grow", [P, 2, HG_HEADS, SEQ])
        sq = sbuf(k, es, "sq", [P, HG_HEADS * SEQ])
        rstd = sbuf(k, es, "rstd", [P, HG_HEADS * SEQ])

        @block.gpsimd
        def _(pool):
            conv.run(pool, s)

        @block.vector
        def _(dve):
            order = Order(dve, s.order)
            if from_state:
                for h in range(HG_HEADS):
                    last = dve.tensor_scalar(grow[:, 1, h, :], bc[:, 1, h, :], k.back_total[:, h:h + 1], None, ALU.add)
                last.then_inc(s.shifted, 1)
                dve.wait_ge(s.grown, 2)
                for d in range(2):
                    last = dve.tensor_tensor(grow[:, d, :, :], grow[:, d, :, :], q, ALU.mult)
                last.then_inc(s.fed, 1)
            dve.wait_ge(s.root, 1)
            for n in range(2):
                half = slice(512 * n, 512 * (n + 1))
                last = dve.tensor_tensor(rstd[:, half], rstd[:, half], k.bank[n][:, :], ALU.mult)
            order(last)
            dve.tensor_tensor(out, rstd[:, :].rearrange("p (h t) -> p h t", h=HG_HEADS), gate, ALU.mult)

        @block.scalar
        def _(act):
            if from_state:
                act.activation(grow[:, 0, :, :], bc[:, 0, :, :], ACT.Exp).then_inc(s.grown, 1)
                act.wait_ge(s.shifted, 1)
                act.activation(grow[:, 1, :, :], grow[:, 1, :, :], ACT.Exp).then_inc(s.grown, 1)
            act.wait_ge(s.mixed, 1)
            for n in range(2):
                last = act.activation(sq[:, 512 * n:512 * (n + 1)], k.bank[n][:, :], ACT.Square)
            last.then_inc(s.squares, 1)
            act.wait_ge(s.sums, 1)
            for n in range(2):
                last = act.activation(rstd[:, 512 * n:512 * (n + 1)], k.bank[2 + n][:, :], ACT.Ln, scale=1.0 / P, bias=k.eps[:, 0:1])
            last.then_inc(s.logged, 1)
            act.wait_ge(s.logged, 1)
            act.activation(rstd[:, :], rstd[:, :], ACT.Exp, scale=-0.5).then_inc(s.root, 1)

        @block.tensor
        def _(pe):
            if from_state:
                pe.wait_ge(s.fed, 1)
            for h in range(HG_HEADS):
                o = k.bank[h // 2][:, (h % 2) * SEQ:(h % 2 + 1) * SEQ]
                parts = [(k.v[:, s0 // P + i, h * P:(h + 1) * P], att[:, i, h, :]) for i in range(2)]
                if from_state:
                    parts += [(k.state[:, d, h, :], grow[:, d, h, :]) for d in range(2)]
                for i, (lhsT, rhs) in enumerate(parts):
                    last = pe.matmul(o, lhsT, rhs, start=(i == 0), stop=(i == len(parts) - 1))
            last.then_inc(s.mixed, 1)
            pe.wait_ge(s.squares, 1)
            for n in range(2):
                last = pe.matmul(k.bank[2 + n][:, :], k.ones, sq[:, 512 * n:512 * (n + 1)], start=True, stop=True)
            last.then_inc(s.sums, 1)


def hgrn_states(k, s0, key, bc):
    with ExitStack() as es, stage(k, "states", "grown fed turned took summed") as (block, s):
        dec = sbuf(k, es, "dec", [P, 2, HG_HEADS, SEQ])
        turned = sbuf(k, es, "turned", [P, 2, 2, HG_HEADS, P])

        @block.scalar
        def _(act):
            for h in range(HG_HEADS):
                act.activation(dec[:, 0, h, :], bc[:, 0, h, :], ACT.Exp, scale=-1.0, bias=bc[:, 0, h, SEQ - 1:SEQ])
            act.activation(dec[:, 1, :, :], bc[:, 1, :, :], ACT.Exp, scale=-1.0).then_inc(s.grown, 1)

        @block.vector
        def _(dve):
            dve.wait_ge(s.grown, 1)
            dve.tensor_tensor(dec[:, :, :, :], dec[:, :, :, :], key[:, :, :, :], ALU.mult).then_inc(s.fed, 1)
            for n in range(4):
                dve.wait_ge(s.turned, n + 1)
                dve.tensor_copy(turned[:, n // 2, n % 2, :, :],
                                k.bank[n][:, :].rearrange("p (h d) -> p h d", h=HG_HEADS)).then_inc(s.took, 1)
            dve.wait_ge(s.summed, 1)
            for d in range(2):
                dve.tensor_copy(k.state[:, d, :, :], k.bank[4 + d][:, :].rearrange("p (h d) -> p h d", h=HG_HEADS))

        @block.tensor
        def _(pe):
            pe.wait_ge(s.fed, 1)
            for n in range(4):
                for h in range(HG_HEADS):
                    i, d = n // 2, n % 2
                    last = pe.transpose(k.bank[n][:, h * P:(h + 1) * P], dec[:, d, h, i * P:(i + 1) * P], k.ident)
                last.then_inc(s.turned, 1)
            pe.wait_ge(s.took, 4)
            for d in range(2):
                for h in range(HG_HEADS):
                    for i in range(2):
                        last = pe.matmul(k.bank[4 + d][:, h * P:(h + 1) * P], turned[:, i, d, h, :],
                                         k.v[:, s0 // P + i, h * P:(h + 1) * P], start=(i == 0), stop=(i == 1))
            last.then_inc(s.summed, 1)


class ShortConv:

    def __init__(self, k, l, grid, cg, bg, hv, out):
        self.k, self.l, self.grid, self.cg, self.bg, self.hv, self.out = k, l, grid, cg, bg, hv, out

    def place(self, es):
        self.u = sbuf(self.k, es, "u", [P, 4, SEQ])
        self.y = sbuf(self.k, es, "y", [P, 4, SEQ])
        self.product = sbuf(self.k, es, "product", [P, 4, SEQ])

    def run(self, pool, s):
        u, y, product = self.u, self.y, self.product
        order = Order(pool, s.conv)
        order(pool.tensor_tensor(u[:, :, :], self.cg, self.hv, ALU.mult))
        w = self.k.small("conv_w").rearrange("p (l tap c) -> p l tap c", l=DEPTH, tap=3)
        weights = lambda tap: w[:, self.l, tap, :].unsqueeze(2).broadcast_to([P, 4, SEQ])
        order(pool.tensor_tensor(y[:, :, :], u[:, :, :], weights(1), ALU.mult))
        for tap in (0, 2):
            order(pool.tensor_tensor(product[:, :, :], u[:, :, :], weights(tap), ALU.mult))
            for c in (slice(0, 2), slice(2, 4)):
                step = GRID_W if self.grid and c.start == 2 else 1
                rows = SEQ // GRID_W if self.grid and c.start == 0 else 1
                pp = product[:, c, :].rearrange("p c (r w) -> p c r w", r=rows)
                yy = y[:, c, :].rearrange("p c (r w) -> p c r w", r=rows)
                width = SEQ // rows
                near, far = slice(0, width - step), slice(step, width)
                src, dst = (near, far) if tap == 0 else (far, near)
                last = pool.tensor_tensor(yy[:, :, :, dst], yy[:, :, :, dst], pp[:, :, :, src], ALU.add)
            order(last)
        pool.tensor_tensor(self.out, y[:, :, :], self.bg, ALU.mult)


def residual_project(k, name, x, gate, seqs):
    t0, t1 = seqs[0] * SEQ, (seqs[-1] + 1) * SEQ

    def evict(dve, c, bank, s):
        for q in seqs:
            half = slice(q * SEQ, (q + 1) * SEQ)
            last = dve.scalar_tensor_tensor(out=k.X[:, c, half], in0=bank[:, q * SEQ - t0:(q + 1) * SEQ - t0],
                                            scalar=gate[:, c, q:q + 1], in1=k.X[:, c, half], op0=ALU.mult, op1=ALU.add)
        return last

    project(k, name, [(1, P, 0, t1 - t0)] * KD, x[:, :, t0:t1], evict, by=lambda c: 1, tables=True)


def token_mixer_1(k, l, norm):
    with ExitStack() as es:
        proj = sbuf(k, es, "proj", [P, 28, TWO])
        H = k.H
        last_layer = l == DEPTH - 1
        outs = [(1, P, 0, TWO)] * 12 + [(1, P, SEQ, SEQ) if last_layer else (1, P, 0, TWO)] * 20
        with ExitStack() as inner:
            values = sbuf(k, inner, "values", [P, HG_HEADS, TWO])

            def evict(eng, c, bank, s):
                t0, n = outs[c][2:]
                return copy(k, eng, values[:, c, :] if c < 4 else proj[:, c - 4, t0:t0 + n], bank[:, 0:n])

            project(k, "w_in", outs, H[:, :, :], evict, norm=norm)
            transpose_chunks(k, "values", [(k.v[:, i, c * P:(c + 1) * P], values[:, c, i * P:(i + 1) * P])
                                           for i in range(4) for c in range(4)])
        bc = sbuf(k, es, "bc", [P, 2, HG_HEADS, SEQ])
        key = sbuf(k, es, "key", [P, 2, HG_HEADS, SEQ])
        for n, s0 in enumerate((0, SEQ)):
            part = lambda c: proj[:, c:c + 4, s0:s0 + SEQ]
            hgrn_gates(k, l, proj[:, 0:8, s0:s0 + SEQ], bc, key)
            if n == 1 or not last_layer:
                with ExitStack() as inner:
                    att = sbuf(k, inner, "att", [P, 2, HG_HEADS, SEQ])
                    hgrn_attention(k, part(8), key, bc, att, part(12))
                    conv = ShortConv(k, l, n == 1, part(16), part(20), part(24), H[:, 4:8, s0:s0 + SEQ])
                    hgrn_outputs(k, s0, part(8), part(12), key, bc, att, n == 1, H[:, 0:4, s0:s0 + SEQ], conv)
            if n == 0:
                hgrn_states(k, s0, key, bc)
    residual_project(k, "w_out", k.H, k.mods[:, l, 16:24, :], (1,) if last_layer else (0, 1))



GATHER = 8


def peer(k, a, l, tiles, norm):
    H = k.H
    with ExitStack() as es:
        T0, T = tiles[0] * P, len(tiles) * P
        qr = sbuf(k, es, "qr", [P, 2 * PEER_HEADS, T])
        project(k, "peer_wq", [(1, P, 0, T)] * (2 * PEER_HEADS), H[:, :, T0:T0 + T],
                lambda eng, c, bank, s: copy(k, eng, qr[:, c, :], bank[:, 0:T]), norm=norm)
        hT = sbuf(k, es, "hT", [P, len(tiles), D])
        transpose_chunks(k, "h_rows", [(hT[:, i, c * P:(c + 1) * P], H[:, c, t * P:(t + 1) * P])
                                       for i, t in enumerate(tiles) for c in range(KD)])
        peer_experts(k, a, l, tiles, qr, hT)


def peer_experts(k, a, l, tiles, qr, hT):
    NH = 2 * PEER_HEADS
    NT = len(tiles)
    pe_experts = [e for e in range(SEL) if e % 5 != 4]
    dve_experts = [e for e in range(SEL) if e % 5 == 4]
    slots = " ".join(f"landed{n}" for n in range(GATHER))
    with ExitStack() as es, stage(k, "experts", slots + " keys scored took order chosen spread grown dotted "
                                  "gelu weighed diag summed added out_rows turned") as (block, s):
        landed = [s.landed0, s.landed1, s.landed2, s.landed3, s.landed4, s.landed5, s.landed6, s.landed7]
        keys = sbuf(k, es, "subkeys", [P, NH, N_KEYS])
        scores = sbuf(k, es, "scores", [P, NH, N_KEYS])
        rows = sbuf(k, es, "rows", [P, GATHER, D])
        junk = sbuf(k, es, "junk", [P, 2, D])
        acc = sbuf(k, es, "acc", [P, D])
        out_rows = sbuf(k, es, "out_rows", [P, D])
        expert = sbuf(k, es, "expert", [P, 2, SEL], U32)
        best = sbuf(k, es, "best", [P, NH, TOPK])
        where = sbuf(k, es, "where", [P, NH, TOPK], U32)
        where_f = sbuf(k, es, "where_f", [P, NH, TOPK])
        cand = sbuf(k, es, "cand", [P, TOPK, TOPK])
        top = sbuf(k, es, "top", [P, PEER_HEADS, TOPK])
        largest = sbuf(k, es, "largest", [P, PEER_HEADS])
        pos = sbuf(k, es, "pos", [P, PEER_HEADS, TOPK], U32)
        part = sbuf(k, es, "part", [P, 2, TOPK], U32)
        part_f = sbuf(k, es, "part_f", [P, 2, TOPK])
        hot = sbuf(k, es, "hot", [P, 2, TOPK, TOPK])
        index = sbuf(k, es, "index", [P, 2, TOPK])
        total = sbuf(k, es, "total", [P, PEER_HEADS])
        products = sbuf(k, es, "products", [P, SEL])
        weight = sbuf(k, es, "weight", [P, SEL])
        diag = sbuf(k, es, "diag", [P, 4, P])
        table = (a.peer_u[l], a.peer_v[l])

        @block.sync
        def _(sp):
            sp.dma_start(keys[:, :, :], a.peer_subkeys[l]).then_inc(s.keys, 16)

        @block.gpsimd
        def _(pool):
            for n in range(2 * SEL * NT):
                i, e = n // (2 * SEL), n % SEL
                is_v = n % (2 * SEL) >= SEL
                if not is_v and e % TOPK == 0:
                    pool.wait_ge(s.chosen, PEER_HEADS * i + e // TOPK + 1)
                if n >= GATHER:
                    old_i, old_e = (n - GATHER) // (2 * SEL), (n - GATHER) % SEL
                    if (n - GATHER) % (2 * SEL) < SEL:
                        pool.wait_ge(s.dotted, SEL * old_i + old_e + 1)
                    elif old_e in pe_experts:
                        pool.wait_ge(s.summed, len(pe_experts) * old_i + pe_experts.index(old_e) + 1)
                    else:
                        pool.wait_ge(s.added, len(dve_experts) * old_i + dve_experts.index(old_e) + 1)
                pool.indirect_dma_start(rows[:, n % GATHER, :], None, table[is_v],
                                        bass.IndirectOffsetOnAxis(ap=expert[:, i % 2, e:e + 1], axis=0)
                                        ).then_inc(landed[n % GATHER], 16)

        @block.tensor
        def _(pe):
            def score(i):
                if i > 0:
                    pe.wait_ge(s.took, 4 * i)
                for c in range(NH):
                    last = pe.matmul(k.bank[2 + c // 4][:, (c % 4) * P:(c % 4 + 1) * P], qr[:, c, i * P:(i + 1) * P],
                                     keys[:, c, :], start=True, stop=True)
                    if c % 4 == 3:
                        last.then_inc(s.scored, 1)

            pe.wait_ge(s.keys, 16)
            score(0)
            for i in range(NT):
                if i + 1 < NT:
                    score(i + 1)
                if i > 0:
                    pe.wait_ge(s.out_rows, i)
                for j, e in enumerate(pe_experts):
                    n = (2 * i + 1) * SEL + e
                    done = len(pe_experts) * i + j
                    pe.wait_ge(s.diag, done + 1)
                    pe.wait_ge(landed[n % GATHER], 16 * (n // GATHER + 1))
                    for half in range(2):
                        last = pe.matmul(k.bank[half][:, :], diag[:, done % 4, :], rows[:, n % GATHER, half * 512:(half + 1) * 512],
                                         start=(j == 0), stop=(e == pe_experts[-1]))
                    last.then_inc(s.summed, 1)
                pe.wait_ge(s.out_rows, i + 1)
                for c in range(KD):
                    last = pe.transpose(k.bank[6 + c // 4][:, (c % 4) * P:(c % 4 + 1) * P], out_rows[:, c * P:(c + 1) * P], k.ident)
                last.then_inc(s.turned, 1)

        @block.scalar
        def _(act):
            def take_scores(i):
                if i > 0:
                    act.wait_ge(s.chosen, PEER_HEADS * i)
                for n in range(4):
                    act.wait_ge(s.scored, 4 * i + n + 1)
                    act.copy(scores[:, 4 * n:4 * n + 4, :], k.bank[2 + n][:, :].rearrange("p (c n) -> p c n", c=4)).then_inc(s.took, 1)

            def exps(i):
                act.wait_ge(s.spread, i + 1)
                act.activation(top[:, :, :], top[:, :, :], ACT.Exp).then_inc(s.grown, 1)

            take_scores(0)
            exps(0)
            for i in range(NT):
                if i + 1 < NT:
                    take_scores(i + 1)
                act.wait_ge(s.dotted, SEL * (i + 1))
                act.activation(products[:, :], products[:, :], ACT.Gelu).then_inc(s.gelu, 1)
                act.wait_ge(s.weighed, i + 1)
                for j, e in enumerate(pe_experts):
                    n = len(pe_experts) * i + j
                    if n >= 4:
                        act.wait_ge(s.summed, n - 3)
                    act.mul(diag[:, n % 4, :], k.ident, products[:, e:e + 1]).then_inc(s.diag, 1)
                if i + 1 < NT:
                    exps(i + 1)
                else:
                    load_tables(act)

        @block.vector
        def _(dve):
            order = Order(dve, s.order)

            def top16(*rows):
                order([dve.max(best[:, 0:8], values) for values, best, where in rows][-1])
                order([dve.max_index(where[:, 0:8], best[:, 0:8], values) for values, best, where in rows][-1])
                order([dve.match_replace(values, best[:, 0:8], values, -3e38) for values, best, where in rows][-1])
                order([dve.max(best[:, 8:16], values) for values, best, where in rows][-1])
                order([dve.max_index(where[:, 8:16], best[:, 8:16], values) for values, best, where in rows][-1])

            full = [P, TOPK, TOPK]

            def choose(i, h):
                dve.wait_ge(s.took, 4 * i + h // 2 + 1)
                top16(*((scores[:, c, :], best[:, c, :], where[:, c, :]) for c in (2 * h, 2 * h + 1)))
                dve.tensor_copy(where_f[:, 2 * h:2 * h + 2, :], where[:, 2 * h:2 * h + 2, :])
                order(dve.tensor_tensor(cand[:, :, :], best[:, 2 * h, :].unsqueeze(2).broadcast_to(full),
                                        best[:, 2 * h + 1, :].unsqueeze(1).broadcast_to(full), ALU.add))
                top16((cand[:, :, :].rearrange("p a b -> p (a b)"), top[:, h, :], pos[:, h, :]))
                dve.tensor_scalar(part[:, 0, :], pos[:, h, :], 4, None, ALU.logical_shift_right)
                order(dve.tensor_scalar(part[:, 1, :], pos[:, h, :], TOPK - 1, None, ALU.bitwise_and))
                order(dve.tensor_copy(part_f[:, :, :], part[:, :, :]))
                iota = k.const("iota").unsqueeze(1).broadcast_to(full)
                for half in range(2):
                    last = dve.tensor_tensor(hot[:, half, :, :], part_f[:, half, :].unsqueeze(2).broadcast_to(full), iota, ALU.is_equal)
                order(last)
                for half in range(2):
                    last = dve.tensor_tensor(hot[:, half, :, :], hot[:, half, :, :],
                                             where_f[:, 2 * h + half, :].unsqueeze(1).broadcast_to(full), ALU.mult)
                order(last)
                for half in range(2):
                    last = dve.tensor_reduce(index[:, half, :], hot[:, half, :, :], AX, ALU.add)
                order(last)
                if i >= 2 and h == 0:
                    dve.wait_ge(s.summed, len(pe_experts) * (i - 1))
                dve.scalar_tensor_tensor(out=expert[:, i % 2, h * TOPK:(h + 1) * TOPK], in0=index[:, 0, :], scalar=float(N_KEYS),
                                         in1=index[:, 1, :], op0=ALU.mult, op1=ALU.add).then_inc(s.chosen, 1)

            def spread(i):
                order(dve.tensor_copy(largest[:, :], top[:, :, 0]))
                dve.tensor_tensor(top[:, :, :], top[:, :, :],
                                  largest[:, :].unsqueeze(2).broadcast_to([P, PEER_HEADS, TOPK]), ALU.subtract).then_inc(s.spread, 1)

            def add_out(i):
                t = tiles[i]
                dve.wait_ge(s.turned, i + 1)
                cols = slice(t * P, (t + 1) * P)
                for c in range(KD):
                    dve.scalar_tensor_tensor(out=k.X[:, c, cols], in0=k.bank[6 + c // 4][:, (c % 4) * P:(c % 4 + 1) * P],
                                             scalar=k.mods[:, l, 40 + c, t // 2:t // 2 + 1], in1=k.X[:, c, cols],
                                             op0=ALU.mult, op1=ALU.add)

            choose(0, 0)
            for i in range(NT):
                for e in range(SEL):
                    n = 2 * i * SEL + e
                    if i == 0 and e % TOPK == 0:
                        if e + TOPK < SEL:
                            choose(0, e // TOPK + 1)
                        else:
                            spread(0)
                    dve.wait_ge(landed[n % GATHER], 16 * (n // GATHER + 1))
                    if i > 0 and e == 0:
                        dve.wait_ge(s.diag, len(pe_experts) * i)
                        dve.wait_ge(s.added, len(dve_experts) * i)
                    if SEL * i + e >= 2:
                        dve.wait_ge(s.dotted, SEL * i + e - 1)
                    dve.tensor_tensor_reduce(junk[:, e % 2, :], rows[:, n % GATHER, :], hT[:, i, :], 1.0, 0.0, ALU.mult, ALU.add,
                                             products[:, e:e + 1]).then_inc(s.dotted, 1)
                    if i > 0 and e == 2:
                        add_out(i - 1)
                dve.wait_ge(s.grown, i + 1)
                order(dve.tensor_reduce(total[:, :], top[:, :, :], AX, ALU.add))
                order(dve.reciprocal(total[:, :], total[:, :]))
                order(dve.tensor_tensor(weight[:, :].rearrange("p (h j) -> p h j", h=PEER_HEADS), top[:, :, :],
                                        total[:, :].unsqueeze(2).broadcast_to([P, PEER_HEADS, TOPK]), ALU.mult))
                dve.wait_ge(s.gelu, i + 1)
                dve.tensor_tensor(products[:, :], products[:, :], weight[:, :], ALU.mult).then_inc(s.weighed, 1)
                dve.wait_ge(s.weighed, i + 1)
                for j, e in enumerate(dve_experts):
                    if i + 1 < NT and j % 3 == 0 and j // 3 < PEER_HEADS:
                        choose(i + 1, j // 3)
                    n = (2 * i + 1) * SEL + e
                    done = len(dve_experts) * i + j
                    dve.wait_ge(landed[n % GATHER], 16 * (n // GATHER + 1))
                    if done > 0:
                        dve.wait_ge(s.added, done)
                    if i > 0 and j == 0:
                        dve.wait_ge(s.out_rows, i)
                    row, weight_e = rows[:, n % GATHER, :], products[:, e:e + 1]
                    if j == 0:
                        dve.tensor_scalar(acc[:, :], row, weight_e, None, ALU.mult).then_inc(s.added, 1)
                    else:
                        dve.scalar_tensor_tensor(out=acc[:, :], in0=row, scalar=weight_e, in1=acc[:, :],
                                                 op0=ALU.mult, op1=ALU.add).then_inc(s.added, 1)
                if i + 1 < NT:
                    spread(i + 1)
                dve.wait_ge(s.added, len(dve_experts) * (i + 1))
                dve.wait_ge(s.summed, len(pe_experts) * (i + 1))
                if i > 0:
                    dve.wait_ge(s.turned, i)
                for half in range(2):
                    cols = slice(512 * half, 512 * (half + 1))
                    last = dve.tensor_tensor(out_rows[:, cols], k.bank[half][:, :], acc[:, cols], ALU.add)
                last.then_inc(s.out_rows, 1)
            add_out(NT - 1)


def first_block(k, a):
    modulation(k)
    for l in range(DEPTH):
        gain = lambda n: both_ways(lambda c: k.gain[:, l, n, c, :])
        shift = lambda c0: both_ways(lambda c: k.mods[:, l, c0 + c, :])
        with ExitStack() as es:
            k.v = sbuf(k, es, "values", [P, 4, HG_HEADS * P])
            k.state = sbuf(k, es, "states", [P, 2, HG_HEADS, P])
            token_mixer_1(k, l, Norm(k, k.X[:, :, :], TWO, gain(0), shift(0), k.H[:, :, :]))
        if l < DEPTH - 1:
            peer(k, a, l, (0, 1, 2, 3), Norm(k, k.X[:, :, :], TWO, gain(1), shift(24), k.H[:, :, :]))
        else:
            second = lambda parts: lambda c: [(0, SEQ, parts(c)[1][2])]
            peer(k, a, l, (2, 3), Norm(k, k.X[:, :, SEQ:TWO], SEQ, second(gain(1)), second(shift(24)), k.H[:, :, SEQ:TWO]))



def project_residual_2(k, name, x, n_units=1, split_x=None):
    project(k, name, [(n_units, P, 0, T2)] * KD, x,
            lambda dve, c, bank, s: dve.tensor_tensor(k.Y[:, c, :], bank[:, 0:T2], k.Y[:, c, :], ALU.add),
            by=lambda c: 1, split_x=split_x, tables=True)


def turn_values(k, name, values, v):
    transpose_chunks(k, name, [(v[0:n, i, c * P:(c + 1) * P], values[:, c, t0:t0 + n])
                               for i, (t0, n) in enumerate(TILES2) for c in range(KD)])


def head_norms(k, name, sets, ones, width, mean=True, gated=None):
    chunks = [(x, c) for x, _ in sets for c in range(KD)]
    with ExitStack() as es, stage(k, name, "squares summed logged root normed") as (block, s):
        sq = sbuf(k, es, "sq", [P, len(chunks), T2])
        rstd = sbuf(k, es, "rstd", [P, len(chunks), T2])

        @block.scalar
        def _(act):
            load_tables(act)
            for n, (x, c) in enumerate(chunks):
                act.activation(sq[:, n, :], x[:, c, :], ACT.Square).then_inc(s.squares, 1)
            for n in range(len(chunks)):
                act.wait_ge(s.summed, n + 1)
                act.activation(rstd[:, n, :], k.bank[n % BANKS][:, 0:T2], ACT.Ln, scale=1.0 / width if mean else 1.0,
                               bias=k.eps[:, 0:1]).then_inc(s.logged, 1)
            for n in range(0, len(chunks), 2):
                act.wait_ge(s.logged, n + 2)
                act.activation(rstd[:, n:n + 2, :], rstd[:, n:n + 2, :], ACT.Exp, scale=-0.5).then_inc(s.root, 1)

        @block.tensor
        def _(pe):
            for n in range(len(chunks)):
                pe.wait_ge(s.squares, n + 1)
                if n >= BANKS:
                    pe.wait_ge(s.logged, n - BANKS + 1)
                pe.matmul(k.bank[n % BANKS][:, 0:T2], ones, sq[:, n, :], start=True, stop=True).then_inc(s.summed, 1)

        @block.vector
        def _(dve):
            for n in range(0, len(chunks), 2):
                dve.wait_ge(s.root, n // 2 + 1)
                x, c = chunks[n]
                dve.scalar_tensor_tensor(out=x[:, c:c + 2, :], in0=x[:, c:c + 2, :], scalar=sets[n // KD][1], in1=rstd[:, n:n + 2, :],
                                         op0=ALU.mult, op1=ALU.mult).then_inc(s.normed, 1)
            if gated is not None:
                out, gate = gated
                dve.wait_ge(s.normed, len(chunks) // 2)
                dve.tensor_tensor(out, sets[0][0], gate, ALU.mult)


def fox(k, a, j, norm):
    H = k.H
    with ExitStack() as es:
        q = sbuf(k, es, "q", [P, KD, T2])
        kk = sbuf(k, es, "k", [P, KD, T2])
        v = sbuf(k, es, "v", [P, 3, D])
        gate = sbuf(k, es, "gate", [P, KD, T2])
        f = sbuf(k, es, "f", [FOX_HEADS, 3, T2])
        with ExitStack() as inner:
            values = sbuf(k, inner, "values", [P, KD, T2])

            def evict(eng, c, bank, s):
                if c == 32:
                    return copy(k, eng, f[:, 0, :], bank[0:FOX_HEADS, 0:T2])
                return copy(k, eng, (q, kk, values, gate)[c // 8][:, c % 8, :], bank[:, 0:T2])

            project(k, "fox_in", [(1, P, 0, T2)] * 32 + [(1, FOX_HEADS, 0, T2)], H[:, :, 0:T2], evict, norm=norm)
            turn_values(k, "fox_values", values, v)
        gq, gk = k.small("fox_q_gain_2")[:, j:j + 1], k.small("fox_k_gain_2")[:, j:j + 1]
        with ExitStack() as es2, stage(k, "fox_gates", "order absd expd lned") as (block, s):
            tmp = sbuf(k, es2, "tmp", [FOX_HEADS, T2])

            @block.vector
            def _(dve):
                order = Order(dve, s.order)
                order(dve.tensor_scalar(k.qgain[:, 0:1], gq, DK_FOX ** -0.5, None, ALU.mult))
                order(dve.tensor_scalar(f[:, 0, :], f[:, 0, :], k.fox_b[:, j:j + 1], None, ALU.add))
                dve.scalar_tensor_tensor(out=tmp[:, :], in0=f[:, 0, :], scalar=-1.0, in1=f[:, 0, :], op0=ALU.mult, op1=ALU.max).then_inc(s.absd, 1)
                dve.wait_ge(s.lned, 1)
                order(dve.scalar_tensor_tensor(out=f[:, 0, :], in0=f[:, 0, :], scalar=0.0, in1=tmp[:, :], op0=ALU.min, op1=ALU.subtract))
                order(dve.tensor_tensor_scan(f[:, 1, :], k.ones[0:FOX_HEADS, 0:1].broadcast_to([FOX_HEADS, T2]), f[:, 0, :], 0.0, ALU.mult, ALU.add))
                order(dve.tensor_scalar(f[:, 2, :], f[:, 1, :], -1.0, None, ALU.mult))

            @block.scalar
            def _(act):
                load_tables(act)
                act.wait_ge(s.absd, 1)
                act.activation(tmp[:, :], tmp[:, :], ACT.Exp, scale=-1.0).then_inc(s.expd, 1)
                act.wait_ge(s.expd, 1)
                act.activation(tmp[:, :], tmp[:, :], ACT.Ln, bias=k.one[0:FOX_HEADS, 0:1]).then_inc(s.lned, 1)
                act.activation(gate[:, :, :], gate[:, :, :], ACT.Sigmoid)

        head_norms(k, "qk_norms", [(q[:, :, :], k.qgain[:, 0:1]), (kk[:, :, :], gk)], k.ones64, DK_FOX)
        fox_attention(k, q, kk, v, gate, f)
    project_residual_2(k, "fox_out", H[:, :, 0:T2])


def fox_attention(k, q, kk, v, gate, f):
    H = k.H
    steps = [(h, i) for h in range(FOX_HEADS) for i in range(3)]
    NS = len(steps)
    with ExitStack() as es, stage(k, "attention", "rows picked scored maxed negated exped rcp normed turned copied mixed gated") as (block, s):
        sc = sbuf(k, es, "sc", [P, 3, T2])
        pr = sbuf(k, es, "pr", [P, 3, T2])
        pT = sbuf(k, es, "pT", [P, 2, 3, T2])
        mx = sbuf(k, es, "mx", [P, 3])
        nmx = sbuf(k, es, "nmx", [P, 3])
        total = sbuf(k, es, "total", [P, 3])
        inv = sbuf(k, es, "inv", [P, 3])
        rows_q = sbuf(k, es, "rows_q", [80, T2])
        rows_k = sbuf(k, es, "rows_k", [80, T2])
        picked = sbuf(k, es, "picked", [80, 2, T2])

        @block.sync
        def _(sp):
            sp.wait_ge(s.rows, 2)
            sp.dma_start(rows_q[0:FOX_HEADS, :], f[:, 1, :]).then_inc(s.rows, 16)
            sp.dma_start(rows_k[64:80, :], f[:, 2, :]).then_inc(s.rows, 16)

        @block.gpsimd
        def _(pool):
            pool.memset(rows_q[:, :], 1.0).then_inc(s.rows, 1)
            pool.memset(rows_k[:, :], 1.0).then_inc(s.rows, 1)
            pool.wait_ge(s.rows, 34)
            for h in range(FOX_HEADS):
                if h >= 2:
                    pool.wait_ge(s.scored, 3 * (h - 1))
                pool.tensor_tensor(picked[:, h % 2, :], rows_q[:, :], k.const("pick")[0:80, h:h + 1].broadcast_to([80, T2]),
                                   ALU.mult).then_inc(s.picked, 1)

        def score(pe, n):
            h, i = steps[n]
            t0, nq = TILES2[i]
            nk = t0 + nq
            lo = (h % 2) * DK_FOX
            if n >= 3:
                pe.wait_ge(s.maxed, n - 2)
            bank = k.bank[n % 3][0:nq, 0:nk]
            pe.matmul(bank, q[lo:lo + DK_FOX, h // 2, t0:t0 + nq], kk[lo:lo + DK_FOX, h // 2, 0:nk], start=True, stop=False)
            pe.wait_ge(s.picked, h + 1)
            pe.matmul(bank, picked[:, h % 2, t0:t0 + nq], rows_k[:, 0:nk], start=False, stop=True).then_inc(s.scored, 1)

        def turn(pe, n):
            h, i = steps[n]
            t0, nq = TILES2[i]
            pe.wait_ge(s.normed, n + 1)
            if n >= 2:
                pe.wait_ge(s.copied, n - 1)
            for j in range(i + 1):
                k0, nk = TILES2[j]
                last = pe.transpose(k.bank[3 + n % 2][0:nk, j * P:j * P + nq], pr[0:nq, n % 3, k0:k0 + nk], k.ident[0:nq, 0:nq])
            last.then_inc(s.turned, 1)

        def mix(pe, h):
            pe.wait_ge(s.copied, 3 * h + 3)
            if h % 2 == 0 and h >= 4:
                pe.wait_ge(s.gated, h // 2 - 1)
            lo = (h % 2) * DK_FOX
            for j, (k0, nk) in enumerate(TILES2):
                last = pe.matmul(k.bank[5 + (h // 2) % 2][lo:lo + DK_FOX, k0:T2], v[0:nk, j, h * DK_FOX:(h + 1) * DK_FOX],
                                 pT[0:nk, h % 2, j, k0:T2], start=(j == 0), stop=(j == 2))
            last.then_inc(s.mixed, 1)

        @block.tensor
        def _(pe):
            for n in range(NS + 3):
                if n < NS:
                    score(pe, n)
                if 2 <= n < NS + 2:
                    turn(pe, n - 2)
                if n >= 3 and (n - 3) % 3 == 2:
                    mix(pe, (n - 3) // 3)

        @block.vector
        def _(dve):
            for n in range(NS + 3):
                if n < NS:
                    h, i = steps[n]
                    t0, nq = TILES2[i]
                    nk = t0 + nq
                    b = n % 3
                    dve.wait_ge(s.scored, n + 1)
                    if n >= 3:
                        dve.wait_ge(s.exped, n - 2)
                    dve.tensor_tensor_reduce(sc[0:nq, b, 0:nk], k.bank[n % 3][0:nq, 0:nk],
                                             k.causal[0:nq, 2 * P - t0:2 * P - t0 + nk], 1.0, NEG, ALU.add, ALU.max,
                                             mx[0:nq, b:b + 1]).then_inc(s.maxed, 1)
                if 1 <= n <= NS:
                    m = n - 1
                    i = steps[m][1]
                    t0, nq = TILES2[i]
                    nk = t0 + nq
                    b = m % 3
                    dve.wait_ge(s.exped, m + 1)
                    dve.reciprocal(inv[0:nq, b:b + 1], total[0:nq, b:b + 1]).then_inc(s.rcp, 1)
                if n < NS:
                    b, nq = n % 3, TILES2[steps[n][1]][1]
                    dve.wait_ge(s.maxed, n + 1)
                    dve.tensor_scalar(nmx[0:nq, b:b + 1], mx[0:nq, b:b + 1], -1.0, None, ALU.mult).then_inc(s.negated, 1)
                if 1 <= n <= NS:
                    b = m % 3
                    nq = TILES2[i][1]
                    dve.wait_ge(s.rcp, m + 1)
                    dve.tensor_scalar(pr[0:nq, b, 0:nk], pr[0:nq, b, 0:nk], inv[0:nq, b:b + 1], None, ALU.mult).then_inc(s.normed, 1)
                if n >= 3 and (n - 3) % 6 == 5:
                    pair = (n - 3) // 6
                    dve.wait_ge(s.mixed, 2 * pair + 2)
                    dve.tensor_tensor(H[:, pair, 0:T2], k.bank[5 + pair % 2][:, 0:T2], gate[:, pair, :], ALU.mult).then_inc(s.gated, 1)

        @block.scalar
        def _(act):
            for n in range(NS + 2):
                if n < NS:
                    i = steps[n][1]
                    t0, nq = TILES2[i]
                    nk = t0 + nq
                    b = n % 3
                    act.wait_ge(s.negated, n + 1)
                    if n >= 3:
                        act.wait_ge(s.turned, n - 2)
                    act.activation(pr[0:nq, b, 0:nk], sc[0:nq, b, 0:nk], ACT.Exp, bias=nmx[0:nq, b:b + 1],
                                   accum_out=total[0:nq, b:b + 1]).then_inc(s.exped, 1)
                if n >= 2:
                    m = n - 2
                    h, i = steps[m]
                    t0, nq = TILES2[i]
                    act.wait_ge(s.turned, m + 1)
                    if i == 0 and h >= 2:
                        act.wait_ge(s.mixed, h - 1)
                    for j in range(i + 1):
                        nk = TILES2[j][1]
                        last = act.copy(pT[0:nk, h % 2, j, t0:t0 + nq], k.bank[3 + m % 2][0:nk, j * P:j * P + nq])
                    last.then_inc(s.copied, 1)


def gla(k, a, norm):
    H = k.H
    NH = 4
    with ExitStack() as es:
        q = sbuf(k, es, "q", [P, NH, T2])
        kk = sbuf(k, es, "k", [P, NH, T2])
        v = sbuf(k, es, "v", [P, 3, D])
        r = sbuf(k, es, "r", [P, KD, T2])
        low = sbuf(k, es, "low", [16, T2])
        b = sbuf(k, es, "b", [P, NH, T2])
        att = sbuf(k, es, "att", [P, 3, NH, T2])
        o = sbuf(k, es, "o", [P, KD, T2])
        alpha = k.alpha
        with ExitStack() as inner:
            values = sbuf(k, inner, "values", [P, KD, T2])

            def evict(eng, c, bank, s):
                if c == 24:
                    return copy(k, eng, low[:, :], bank[0:16, 0:T2])
                if c >= NH:
                    out = kk[:, c - NH, :] if c < 8 else values[:, c - 8, :] if c < 16 else r[:, c - 16, :]
                    return copy(k, eng, out, bank[:, 0:T2])
                if eng is k.nc.scalar:
                    return eng.mul(q[:, c, :], bank[:, 0:T2], float(P) ** -0.5)
                return eng.tensor_scalar(q[:, c, :], bank[:, 0:T2], float(P) ** -0.5, None, ALU.mult)

            project(k, "gla_in", [(1, P, 0, T2)] * 24 + [(1, 16, 0, T2)], H[:, :, 0:T2], evict, norm=norm)
            turn_values(k, "gla_values", values, v)

        with ExitStack() as es2, stage(k, "gla_gates", "made order ready expd lned") as (block, s):
            tmp = sbuf(k, es2, "tmp", [P, NH, T2])
            z = sbuf(k, es2, "z", [P, NH, T2])

            @block.gpsimd
            def _(pool):
                pool.memset(att[:, :, :, :], 0.0)

            @block.tensor
            def _(pe):
                for h in range(NH):
                    last = pe.matmul(k.bank[h][:, 0:T2], alpha[:, h * P:(h + 1) * P], low[:, :], start=True, stop=True)
                last.then_inc(s.made, 1)

            @block.vector
            def _(dve):
                order = Order(dve, s.order)
                bias = k.small("gla_b_alpha_2")
                dve.wait_ge(s.made, 1)
                for h in range(NH):
                    last = dve.tensor_scalar(z[:, h, :], k.bank[h][:, 0:T2], bias[:, h:h + 1], None, ALU.add)
                order(last)
                dve.scalar_tensor_tensor(out=tmp[:, :, :], in0=z[:, :, :], scalar=-1.0, in1=z[:, :, :], op0=ALU.mult, op1=ALU.max).then_inc(s.ready, 1)
                dve.wait_ge(s.lned, 1)
                order(dve.tensor_scalar(z[:, :, :], z[:, :, :], 0.0, None, ALU.min))
                order(dve.tensor_tensor(z[:, :, :], z[:, :, :], tmp[:, :, :], ALU.subtract))
                order(dve.tensor_scalar(z[:, :, :], z[:, :, :], 1.0 / 16.0, None, ALU.mult))
                one = k.ones[:, 0:1].broadcast_to([P, T2])
                for h in range(NH):
                    last = dve.tensor_tensor_scan(b[:, h, :], one, z[:, h, :], 0.0, ALU.mult, ALU.add)
                order(last)

            @block.scalar
            def _(act):
                load_tables(act)
                act.wait_ge(s.ready, 1)
                act.activation(tmp[:, :, :], tmp[:, :, :], ACT.Exp, scale=-1.0).then_inc(s.expd, 1)
                act.wait_ge(s.expd, 1)
                act.activation(tmp[:, :, :], tmp[:, :, :], ACT.Ln, bias=k.one[:, 0:1]).then_inc(s.lned, 1)

        gla_attention(k, q, kk, b, att, r)

        with ExitStack() as es2, stage(k, "gla_mix", "mixed dve_took squares summed logged root") as (block, s):
            sq = sbuf(k, es2, "sq", [P, KD, T2])
            rstd = sbuf(k, es2, "rstd", [P, NH, T2])

            @block.tensor
            def _(pe):
                for c in range(KD):
                    h = c // 2
                    for i, (s0, n) in enumerate(TILES2):
                        last = pe.matmul(k.bank[c][:, s0:T2], v[0:n, i, c * P:(c + 1) * P], att[0:n, i, h, s0:T2],
                                         start=(i == 0), stop=(i == 2))
                    last.then_inc(s.mixed, 1)
                pe.wait_ge(s.squares, KD)
                pe.wait_ge(s.dve_took, KD)
                for h in range(NH):
                    for c in range(2):
                        last = pe.matmul(k.bank[h][:, 0:T2], k.ones, sq[:, 2 * h + c, :], start=(c == 0), stop=(c == 1))
                last.then_inc(s.summed, 1)

            @block.scalar
            def _(act):
                for c in range(KD):
                    act.wait_ge(s.mixed, c + 1)
                    act.activation(sq[:, c, :], k.bank[c][:, 0:T2], ACT.Square).then_inc(s.squares, 1)
                act.wait_ge(s.summed, 1)
                for h in range(NH):
                    last = act.activation(rstd[:, h, :], k.bank[h][:, 0:T2], ACT.Ln, scale=1.0 / (2 * P), bias=k.eps[:, 0:1])
                last.then_inc(s.logged, 1)
                act.wait_ge(s.logged, 1)
                act.activation(rstd[:, :, :], rstd[:, :, :], ACT.Exp, scale=-0.5).then_inc(s.root, 1)

            @block.vector
            def _(dve):
                gain = k.small("gla_o_gain_2")
                for c in range(KD):
                    dve.wait_ge(s.squares, c + 1)
                    dve.scalar_tensor_tensor(out=o[:, c, :], in0=k.bank[c][:, 0:T2], scalar=gain[:, c % 2:c % 2 + 1],
                                             in1=r[:, c, :], op0=ALU.mult, op1=ALU.mult).then_inc(s.dve_took, 1)
                dve.wait_ge(s.dve_took, KD)
                dve.wait_ge(s.root, 1)
                for c in range(KD):
                    dve.tensor_tensor(H[:, c, 0:T2], o[:, c, :], rstd[:, c // 2, :], ALU.mult)
    project_residual_2(k, "gla_out", H[:, :, 0:T2])


def gla_attention(k, q, kk, b, att, gate):
    NH = 4
    whole, full_tiles = T2, 2 * P
    steps = [("diag", 0)] + [("level", l) for l in range(LEVELS)] + [("cross", 0), ("cross", 1)]
    with ExitStack() as es, stage(k, "gla_attend", "apart decayed scaled scored took order") as (block, s):
        dif = sbuf(k, es, "dif", [P, 2, NH, T2])
        kh = sbuf(k, es, "kh", [P, 2, NH, T2])
        qh = sbuf(k, es, "qh", [P, 2, NH, T2])

        def spans(kind, l):
            if kind == "level":
                m = 1 << l
                n = whole if 2 * m <= META else full_tiles
                view = lambda ap, side: halves(ap[:, :, 0:n], m, side)
                return view, (lambda ap: view(ap, 0)[:, :, :, m - 1:m]), [P, NH, n // (2 * m), m], [P, NH, n // (2 * m), m]
            e = (l + 1) * P
            view = lambda ap, side: ap[:, :, l * P:e] if side == 0 else ap[:, :, e:T2]
            return view, (lambda ap: ap[:, :, e - 1:e]), [P, NH, P], [P, NH, T2 - e]

        def blocks(j):
            kind, l = steps[j]
            if kind == "cross":
                return [(0, P, 2 * P, P), (0, 2 * P, T2, P)] if l == 0 else [(1, 2 * P, T2, P)]
            tiles = TILES2 if kind == "diag" or (2 << l) <= META else TILES2[:2]
            return [(i, t0, t0 + n, n) for i, (t0, n) in enumerate(tiles)]

        def banks(j):
            return [k.bank[4 * (j % 2) + n] for n in range(3)]

        @block.gpsimd
        def _(pool):
            for j in range(1, len(steps)):
                view, middle, near, far = spans(*steps[j])
                if j >= 3:
                    pool.wait_ge(s.scaled, j - 1)
                out = dif[:, j % 2, :, :]
                pool.tensor_tensor(view(out, 0), middle(b[:, :, :]).broadcast_to(near), view(b[:, :, :], 0), ALU.subtract)
                pool.tensor_tensor(view(out, 1), view(b[:, :, :], 1), middle(b[:, :, :]).broadcast_to(far), ALU.subtract).then_inc(s.apart, 1)

        @block.scalar
        def _(act):
            act.activation(gate[:, :, :], gate[:, :, :], ACT.Silu)
            load_tables(act)
            for j in range(1, len(steps)):
                view, *_ = spans(*steps[j])
                act.wait_ge(s.apart, j)
                d = dif[:, j % 2, :, :]
                for side in range(2):
                    last = act.activation(view(d, side), view(d, side), ACT.Exp)
                last.then_inc(s.decayed, 1)

        @block.vector
        def _(dve):
            order = Order(dve, s.order)

            def factors(j):
                if j >= 2:
                    dve.wait_ge(s.scored, j - 1)
                ks, qs = kh[:, j % 2, :, :], qh[:, j % 2, :, :]
                if j == 0:
                    dve.tensor_copy(ks, kk[:, :, :])
                    dve.tensor_copy(qs, q[:, :, :]).then_inc(s.scaled, 1)
                    return
                view, *_ = spans(*steps[j])
                dve.wait_ge(s.decayed, j)
                d = dif[:, j % 2, :, :]
                dve.tensor_tensor(view(ks, 0), view(kk[:, :, :], 0), view(d, 0), ALU.mult)
                dve.tensor_tensor(view(qs, 1), view(q[:, :, :], 1), view(d, 1), ALU.mult).then_inc(s.scaled, 1)

            def take(j):
                kind, l = steps[j]
                dve.wait_ge(s.scored, j + 1)
                for n, (i, t0, t1, m) in enumerate(blocks(j)):
                    data = banks(j)[n][0:m, :].rearrange("p (h t) -> p h t", h=NH)[:, :, 0:t1 - t0]
                    out = att[0:m, i, :, t0:t1]
                    if kind == "level":
                        mask = k.fwd[0:m, l, 0:t1 - t0].bitcast(I32).unsqueeze(1).broadcast_to([m, NH, t1 - t0])
                        last = dve.copy_predicated(out, mask, data)
                    else:
                        last = dve.tensor_copy(out, data)
                last.then_inc(s.took, 1)
                dve.wait_ge(s.took, j + 1)

            def take_diag():
                dve.wait_ge(s.scored, 1)
                for n, (i, t0, t1, m) in enumerate(blocks(0)):
                    data = banks(0)[n][0:m, :].rearrange("p (h t) -> p h t", h=NH)[:, :, 0:t1 - t0]
                    mask = k.both[0:m, LEVELS, 0:t1 - t0].unsqueeze(1).broadcast_to([m, NH, t1 - t0])
                    last = dve.copy_predicated(att[0:m, i, :, t0:t1], mask, data)
                last.then_inc(s.took, 1)
                dve.wait_ge(s.took, 1)

            order(dve.memset(kh[:, 1, :, :], 0.0))
            order(dve.memset(qh[:, 1, :, :], 0.0))
            factors(0)
            for j in range(1, len(steps)):
                factors(j)
                take_diag() if j - 1 == 0 else take(j - 1)
            take(len(steps) - 1)

        @block.tensor
        def _(pe):
            for j in range(len(steps)):
                pe.wait_ge(s.scaled, j + 1)
                if j >= 2:
                    pe.wait_ge(s.took, j - 1)
                for n, (i, t0, t1, m) in enumerate(blocks(j)):
                    s0 = TILES2[i][0]
                    for h in range(NH):
                        last = pe.matmul(banks(j)[n][0:m, h * P:h * P + t1 - t0], kh[:, j % 2, h, s0:s0 + m],
                                         qh[:, j % 2, h, t0:t1], start=True, stop=True)
                last.then_inc(s.scored, 1)


def gdn(k, a, norm):
    H = k.H
    NH = GDN_HEADS
    with ExitStack() as es:
        qkv = sbuf(k, es, "qkv", [P, 24, T2])
        gate = sbuf(k, es, "gate", [P, NH, T2])
        rows = sbuf(k, es, "rows", [NH, 6, T2])
        o = sbuf(k, es, "o", [P, NH, T2])
        with ExitStack() as es1:
            raw = sbuf(k, es1, "raw", [P, 24, T2])

            w = k.small("gdn_conv_w_2").rearrange("p (tap c) -> p tap c", tap=4)

            def convolve(dve, j, s):
                dve.wait_ge(s.act_took, j + 1)
                dve.wait_ge(s.dve_took, j + 1)
                for c in (2 * j, 2 * j + 1):
                    last = dve.tensor_scalar(qkv[:, c, :], raw[:, c, :], w[:, 3, c:c + 1], None, ALU.mult)
                last.then_inc(s.tap, 1)
                for back in (1, 2, 3):
                    dve.wait_ge(s.tap, 3 * j + back)
                    for c in (2 * j, 2 * j + 1):
                        last = dve.scalar_tensor_tensor(out=qkv[:, c, back:T2], in0=raw[:, c, 0:T2 - back], scalar=w[:, 3 - back, c:c + 1],
                                                        in1=qkv[:, c, back:T2], op0=ALU.mult, op1=ALU.add)
                    last.then_inc(s.tap if back < 3 else s.convolved, 1)

            def evict(eng, c, bank, s):
                j = c // 2
                if eng is k.nc.vector and 1 <= j <= 12:
                    convolve(eng, j - 1, s)
                if eng is k.nc.scalar and 3 <= j <= 14:
                    eng.wait_ge(s.convolved, j - 2)
                    pair = qkv[:, 2 * j - 6:2 * j - 4, :]
                    eng.activation(pair, pair, ACT.Silu)
                if c >= 32:
                    return copy(k, eng, rows[:, c - 32, :], bank[0:NH, 0:T2])
                return copy(k, eng, raw[:, c, :] if c < 24 else gate[:, c - 24, :], bank[:, 0:T2])

            project(k, "gdn_in", [(1, P, 0, T2)] * 32 + [(1, NH, 0, T2)] * 2, H[:, :, 0:T2], evict, extra="tap convolved", norm=norm)
        head_norms(k, "qk_norms", [(qkv[:, 0:NH, :], float(P) ** -0.5), (qkv[:, NH:2 * NH, :], 1.0)], k.ones, P, mean=False)

        with ExitStack() as es2, stage(k, "gdn_gates", "ready lned expd order") as (block, s):
            tmp = sbuf(k, es2, "tmp", [NH, T2])
            ea = sbuf(k, es2, "ea", [NH, 1])

            @block.vector
            def _(dve):
                order = Order(dve, s.order)
                order(dve.tensor_scalar(rows[:, 0, :], rows[:, 0, :], k.gdn_ab[:, 1:2], None, ALU.add))
                dve.scalar_tensor_tensor(out=tmp[:, :], in0=rows[:, 0, :], scalar=-1.0, in1=rows[:, 0, :], op0=ALU.mult, op1=ALU.max).then_inc(s.ready, 1)
                dve.wait_ge(s.lned, 1)
                order(dve.scalar_tensor_tensor(out=rows[:, 0, :], in0=rows[:, 0, :], scalar=0.0, in1=tmp[:, :], op0=ALU.max, op1=ALU.add))
                order(dve.tensor_scalar(rows[:, 0, :], rows[:, 0, :], ea[:, 0:1], -1.0, ALU.mult, ALU.mult))
                for t0, n in TILES2:
                    last = dve.tensor_tensor_scan(rows[:, 2, t0:t0 + n], k.ones[0:NH, 0:1].broadcast_to([NH, n]),
                                                  rows[:, 0, t0:t0 + n], 0.0, ALU.mult, ALU.add)
                order(last)
                order(dve.tensor_scalar(rows[:, 3, :], rows[:, 2, :], -1.0, None, ALU.mult))

            @block.scalar
            def _(act):
                load_tables(act)
                act.activation(ea[:, :], k.gdn_ab[:, 0:1], ACT.Exp)
                act.wait_ge(s.ready, 1)
                act.activation(tmp[:, :], tmp[:, :], ACT.Exp, scale=-1.0).then_inc(s.expd, 1)
                act.wait_ge(s.expd, 1)
                act.activation(tmp[:, :], tmp[:, :], ACT.Ln, bias=k.one[0:NH, 0:1]).then_inc(s.lned, 1)
                act.activation(rows[:, 1, :], rows[:, 1, :], ACT.Sigmoid)
                act.activation(gate[:, :, :], gate[:, :, :], ACT.Silu)

        with ExitStack() as es3:
            state = sbuf(k, es3, "state", [P, NH, P])
            for i in range(3):
                gdn_tile(k, i, qkv, rows, state, o)
        head_norms(k, "o_norm", [(o[:, :, :], k.small("gdn_o_gain_2")[:, 0:1])], k.ones, P, gated=(H[:, :, 0:T2], gate[:, :, :]))
    project_residual_2(k, "gdn_out", H[:, :, 0:T2])


def gdn_tile(k, i, qkv, rows, state, o):
    NH = GDN_HEADS
    t0, n = TILES2[i]
    levels = LEVELS if n == P else 4
    cols = slice(t0, t0 + n)
    q, kk, v = (qkv[:, c * NH:(c + 1) * NH, cols] for c in range(3))
    G = 2

    with ExitStack() as es:
        kb = sbuf(k, es, "kb", [P, NH, P])
        kg = sbuf(k, es, "kg", [P, NH, P])
        qg = sbuf(k, es, "qg", [P, NH, P])
        last_decay = sbuf(k, es, "last_decay", [P, NH])
        kT = sbuf(k, es, "kT", [P, NH, P])
        vT = sbuf(k, es, "vT", [P, NH, P])
        A = sbuf(k, es, "A", [P, NH, P])
        U = sbuf(k, es, "U", [P, NH, P])
        X = sbuf(k, es, "X", [P, NH, P])
        XT = sbuf(k, es, "XT", [P, NH, P])
        four = lambda ap, g: ap[:, 4 * g:4 * g + 4, :]
        bank4 = lambda n_bank, m: k.bank[n_bank][0:m, :].rearrange("p (h t) -> p h t", h=4)

        with ExitStack() as es1, stage(k, "gdn_a", "spread grown apart faded order made products turned") as (block, s):
            EB = sbuf(k, es1, "EB", [P, NH, P])
            BB = sbuf(k, es1, "BB", [P, NH, P])
            kd = sbuf(k, es1, "kd", [P, NH, P])
            vb = sbuf(k, es1, "vb", [P, NH, P])
            fade = sbuf(k, es1, "fade", [P, NH, P])
            bl = sbuf(k, es1, "bl", [P, NH])

            @block.tensor
            def _(pe):
                for h in range(NH):
                    pick = k.ident[0:NH, h:h + 1]
                    at = slice((h % 4) * P, (h % 4) * P + n)
                    g = h // 4
                    pe.matmul(k.bank[g][:, at], pick.broadcast_to([NH, P]), rows[:, 2, cols], start=True, stop=True)
                    pe.matmul(k.bank[2 + g][:, at], pick.broadcast_to([NH, P]), rows[:, 1, cols], start=True, stop=True)
                    pe.matmul(k.bank[4 + g][0:n, at], pick.broadcast_to([NH, n]), rows[:, 2, cols], start=True, stop=False)
                    last = pe.matmul(k.bank[4 + g][0:n, at], rows[:, 3, cols], pick.broadcast_to([NH, n]), start=False, stop=True)
                last.then_inc(s.spread, 1)
                pe.wait_ge(s.made, 1)
                for h in range(NH):
                    at = slice((h % 4) * P, (h % 4) * P + n)
                    pe.matmul(k.bank[6 + h // 4][0:n, at], kk[:, h, :], kb[:, h, 0:n], start=True, stop=True)
                    last = pe.matmul(k.bank[2 + h // 4][0:n, at], kk[:, h, :], q[:, h, :], start=True, stop=True)
                last.then_inc(s.products, 1)
                pe.wait_ge(s.made, 2)
                for h in range(NH):
                    at = slice((h % 4) * P, (h % 4 + 1) * P)
                    pe.transpose(k.bank[0 + h // 4][0:n, at], kd[:, h, 0:n], k.ident)
                    last = pe.transpose(k.bank[4 + h // 4][0:n, at], vb[:, h, 0:n], k.ident)
                last.then_inc(s.turned, 1)

            @block.scalar
            def _(act):
                act.wait_ge(s.spread, 1)
                for g in range(G):
                    act.activation(four(EB, g)[:, :, 0:n], bank4(g, P)[:, :, 0:n], ACT.Exp)
                    last = act.copy(four(BB, g)[:, :, 0:n], bank4(2 + g, P)[:, :, 0:n])
                last.then_inc(s.grown, 1)
                act.wait_ge(s.apart, 1)
                act.activation(fade[0:n, :, 0:n], fade[0:n, :, 0:n], ACT.Exp).then_inc(s.faded, 1)
                act.wait_ge(s.apart, 2)
                act.activation(kd[:, :, 0:n], kd[:, :, 0:n], ACT.Exp).then_inc(s.faded, 1)
                act.activation(last_decay[:, :], bl[:, :], ACT.Exp)

            @block.vector
            def _(dve):
                order = Order(dve, s.order)
                dve.wait_ge(s.spread, 1)
                incl = k.const("decay_incl")[0:n, 0:n].unsqueeze(1).broadcast_to([n, 4, n])
                for g in range(G):
                    last = dve.tensor_tensor(fade[0:n, 4 * g:4 * g + 4, 0:n], bank4(4 + g, n)[:, :, 0:n], incl, ALU.add)
                last.then_inc(s.apart, 1)
                dve.wait_ge(s.grown, 1)
                for g in range(G):
                    last = dve.tensor_copy(bl[:, 4 * g:4 * g + 4], bank4(g, P)[:, :, n - 1])
                order(last)
                for g in range(G):
                    last = dve.tensor_tensor(four(kd, g)[:, :, 0:n], bl[:, 4 * g:4 * g + 4].unsqueeze(2).broadcast_to([P, 4, n]),
                                             bank4(g, P)[:, :, 0:n], ALU.subtract)
                last.then_inc(s.apart, 1)
                order(dve.tensor_tensor(kb[:, :, 0:n], kk, BB[:, :, 0:n], ALU.mult))
                dve.tensor_tensor(vb[:, :, 0:n], v, BB[:, :, 0:n], ALU.mult).then_inc(s.made, 1)
                dve.tensor_tensor(qg[:, :, 0:n], q, EB[:, :, 0:n], ALU.mult)
                dve.tensor_tensor(kg[:, :, 0:n], kb[:, :, 0:n], EB[:, :, 0:n], ALU.mult)
                dve.wait_ge(s.faded, 2)
                dve.tensor_tensor(kd[:, :, 0:n], kd[:, :, 0:n], kk, ALU.mult).then_inc(s.made, 1)
                dve.wait_ge(s.products, 1)
                strict = k.const("decay_strict")[0:n, 0:n].unsqueeze(1).broadcast_to([n, 4, n])
                for g in range(G):
                    f4 = fade[0:n, 4 * g:4 * g + 4, 0:n]
                    dve.tensor_tensor(A[0:n, 4 * g:4 * g + 4, 0:n], bank4(2 + g, n)[:, :, 0:n], f4, ALU.mult)
                    last = dve.tensor_tensor(U[0:n, 4 * g:4 * g + 4, 0:n], bank4(6 + g, n)[:, :, 0:n], f4, ALU.mult)
                order(last)
                for g in range(G):
                    u4 = U[0:n, 4 * g:4 * g + 4, 0:n]
                    dve.tensor_tensor(u4, u4, strict, ALU.mult)
                dve.wait_ge(s.turned, 1)
                for g in range(G):
                    dve.tensor_copy(kT[0:n, 4 * g:4 * g + 4, :], bank4(g, n))
                    dve.tensor_copy(vT[0:n, 4 * g:4 * g + 4, :], bank4(4 + g, n))
                eye = k.ident[0:n, 0:n].unsqueeze(1).broadcast_to([n, NH, n])
                dve.tensor_copy(X[0:n, :, 0:n], eye)
                dve.tensor_copy(XT[0:n, :, 0:n], eye)

        with ExitStack() as es1, stage(k, "gdn_inverse", "masked lower copied twice took") as (block, s):
            UM = sbuf(k, es1, "UM", [P, NH, P])
            Z = sbuf(k, es1, "Z", [P, NH, P])
            steps = [(l, g) for l in range(levels) for g in range(G)]
            grp = lambda ap, g: ap[0:n, 4 * g:4 * g + 4, 0:n]

            @block.gpsimd
            def _(pool):
                for j, (l, g) in enumerate(steps):
                    if j >= G:
                        pool.wait_ge(s.lower, j - G + 1)
                        if l == 1:
                            pool.wait_ge(s.took, j - G + 1)
                    mask = k.fwd[0:n, l, 0:n].unsqueeze(1).broadcast_to([n, 4, n])
                    pool.tensor_tensor(grp(UM, g), grp(U, g), mask, ALU.mult).then_inc(s.masked, 1)

            @block.tensor
            def _(pe):
                def lower(j):
                    l, g = steps[j]
                    pe.wait_ge(s.masked, j + 1)
                    if j >= G:
                        pe.wait_ge(s.took, j - G + 1)
                    for h in range(4):
                        last = pe.matmul(k.bank[g][0:n, h * P:h * P + n], UM[0:n, 4 * g + h, 0:n], X[0:n, 4 * g + h, 0:n],
                                         start=True, stop=True)
                    last.then_inc(s.lower, 1)

                def twice(j):
                    l, g = steps[j]
                    pe.wait_ge(s.copied, j - G + 1)
                    for h in range(4):
                        hh = 4 * g + h
                        if l < levels - 1:
                            pe.matmul(k.bank[2 + g][0:n, h * P:h * P + n], XT[0:n, hh, 0:n], Z[0:n, hh, 0:n], start=True, stop=True)
                        last = pe.matmul(k.bank[4 + g][0:n, h * P:h * P + n], Z[0:n, hh, 0:n], XT[0:n, hh, 0:n], start=True, stop=True)
                    last.then_inc(s.twice, 1)

                for j in range(0, len(steps), G):
                    for g in range(G):
                        lower(j + g)
                    for g in range(G if j > 0 else 0):
                        twice(j + g)

            @block.scalar
            def _(act):
                for j, (l, g) in enumerate(steps[G:], G):
                    act.wait_ge(s.lower, j + 1)
                    if j >= 2 * G:
                        act.wait_ge(s.twice, j - 2 * G + 1)
                    act.copy(grp(Z, g), bank4(g, n)[:, :, 0:n]).then_inc(s.copied, 1)

            @block.vector
            def _(dve):
                for j, (l, g) in enumerate(steps):
                    if l == 0:
                        dve.wait_ge(s.lower, j + 1)
                        lower, upper = bank4(g, n)[:, :, 0:n], grp(UM, g)
                    else:
                        dve.wait_ge(s.twice, j - G + 1)
                        lower, upper = bank4(2 + g, n)[:, :, 0:n], bank4(4 + g, n)[:, :, 0:n]
                    if l < levels - 1:
                        dve.tensor_tensor(grp(X, g), grp(X, g), lower, ALU.subtract)
                    dve.tensor_tensor(grp(XT, g), grp(XT, g), upper, ALU.subtract).then_inc(s.took, 1)
                    dve.wait_ge(s.took, j + 1)

        with ExitStack() as es1, stage(k, "gdn_step", "read rest solved new mixed updated order") as (block, s):
            R = sbuf(k, es1, "R", [P, NH, P])
            new = sbuf(k, es1, "new", [P, NH, P])

            @block.tensor
            def _(pe):
                if i > 0:
                    for h in range(NH):
                        last = pe.matmul(k.bank[h // 4][0:n, (h % 4) * P:(h % 4 + 1) * P], kg[:, h, 0:n], state[:, h, :], start=True, stop=True)
                    last.then_inc(s.read, 1)
                pe.wait_ge(s.rest, 1)
                for h in range(NH):
                    last = pe.matmul(k.bank[2 + h // 4][0:n, (h % 4) * P:(h % 4 + 1) * P], XT[0:n, h, 0:n], R[0:n, h, :], start=True, stop=True)
                last.then_inc(s.solved, 1)
                pe.wait_ge(s.new, 1)
                for h in range(NH):
                    out = k.bank[4 + h // 4][:, (h % 4) * P:(h % 4) * P + n]
                    last = pe.matmul(out, new[0:n, h, :], A[0:n, h, 0:n], start=True, stop=(i == 0))
                    if i > 0:
                        last = pe.matmul(out, state[:, h, :], qg[:, h, 0:n], start=False, stop=True)
                last.then_inc(s.mixed, 1)
                if i < 2:
                    for h in range(NH):
                        last = pe.matmul(k.bank[6 + h // 4][:, (h % 4) * P:(h % 4 + 1) * P], kT[0:n, h, :], new[0:n, h, :], start=True, stop=True)
                    last.then_inc(s.updated, 1)

            @block.vector
            def _(dve):
                order = Order(dve, s.order)
                if i > 0:
                    dve.wait_ge(s.read, 1)
                for g in range(G):
                    r4, v4 = R[0:n, 4 * g:4 * g + 4, :], vT[0:n, 4 * g:4 * g + 4, :]
                    if i > 0:
                        last = dve.tensor_tensor(r4, v4, bank4(g, n), ALU.subtract)
                    else:
                        last = dve.tensor_copy(r4, v4)
                last.then_inc(s.rest, 1)
                dve.wait_ge(s.solved, 1)
                for g in range(G):
                    last = dve.tensor_copy(new[0:n, 4 * g:4 * g + 4, :], bank4(2 + g, n))
                last.then_inc(s.new, 1)
                dve.wait_ge(s.mixed, 1)
                for g in range(G):
                    dve.tensor_copy(o[:, 4 * g:4 * g + 4, cols], bank4(4 + g, P)[:, :, 0:n])
                if i == 0:
                    dve.wait_ge(s.updated, 1)
                    for g in range(G):
                        dve.tensor_copy(state[:, 4 * g:4 * g + 4, :], bank4(6 + g, P))
                if i == 1:
                    dve.wait_ge(s.updated, 1)
                    order(dve.tensor_tensor(state[:, :, :], state[:, :, :], last_decay[:, :].unsqueeze(2).broadcast_to([P, NH, P]), ALU.mult))
                    for g in range(G):
                        dve.tensor_tensor(state[:, 4 * g:4 * g + 4, :], state[:, 4 * g:4 * g + 4, :], bank4(6 + g, P), ALU.add)


def swiglu(k, norm):
    with ExitStack() as es:
        high, low = (sbuf(k, es, n, [P, KF, T2], F32R) for n in ("hidden_high", "hidden_low"))
        gate = sbuf(k, es, "gate", [P, 2, T2])
        hidden = sbuf(k, es, "hidden", [P, 2, T2])

        def make_high(act, j, s):
            act.wait_ge(s.dve_took, j + 1)
            act.copy(high[:, j, :], hidden[:, j % 2, :]).then_inc(s.high, 1)

        def make_low(dve, j, s):
            dve.wait_ge(s.high, j + 1)
            dve.tensor_tensor(low[:, j, :], hidden[:, j % 2, :], high[:, j, :].bitcast(F32), ALU.subtract).then_inc(s.low, 1)

        def evict(eng, c, bank, s):
            j = c // 2
            if c % 2 == 0:
                if j >= 1:
                    make_high(eng, j - 1, s)
                return eng.activation(gate[:, j % 2, :], bank[:, 0:T2], ACT.Silu)
            if j >= 1:
                make_low(eng, j - 1, s)
            if j >= 2:
                eng.wait_ge(s.low, j - 1)
            eng.wait_ge(s.act_took, j + 1)
            return eng.tensor_tensor(hidden[:, j % 2, :], gate[:, j % 2, :], bank[:, 0:T2], ALU.mult)

        def finish(eng, s):
            if eng is k.nc.scalar:
                make_high(eng, KF - 1, s)
            else:
                make_low(eng, KF - 1, s)

        project(k, "gate_up", [(1, P, 0, T2)] * (2 * KF), k.H[:, :, 0:T2], evict, extra="high low", finish=finish, norm=norm)
        project_residual_2(k, "down", high[:, :, :], 3, split_x=(high, low))


def join_blocks(k, a):
    with stage(k, "meta", "loaded") as (block, s):
        @block.sync
        def _(sp):
            sp.dma_start(k.Y[:, :, 0:META], a.meta).then_inc(s.loaded, 16)
            sp.wait_ge(s.loaded, 16)
    g = k.small("final_g")
    rms_norm(k, "final", k.X[:, :, SEQ:TWO], SEQ, lambda c: [(0, SEQ, g[:, c:c + 1])], k.Y[:, :, META:T2])


def second_block(k, a):
    def norm(name, i):
        g = k.small(name)[:, i * KD:(i + 1) * KD]
        return Norm(k, k.Y[:, :, :], T2, lambda c: [(0, T2, g[:, c:c + 1])], None, k.H[:, :, 0:T2])

    for i in range(4):
        before = norm("norm_mix_2", i)
        (lambda: fox(k, a, i // 3, before), lambda: gla(k, a, before), lambda: gdn(k, a, before))[i % 3]()
        swiglu(k, norm("norm_ffn_2", i))



def build(nc, a, out, debug=None):
    k = Program(nc)
    with ExitStack() as es:
        k.small_sb = sbuf(k, es, "small", [P, N_SMALL])
        k.const_sb = sbuf(k, es, "const", [P, N_CONST])
        both = sbuf(k, es, "both", [P, LEVELS + 1, P], I32)
        k.fox_b = sbuf(k, es, "fox_b", [FOX_HEADS, 2])
        k.gdn_ab = sbuf(k, es, "gdn_ab", [GDN_HEADS, 2])
        k.X = sbuf(k, es, "X", [P, KD, TWO])
        k.H = sbuf(k, es, "H", [P, KD, TWO])
        k.ring = sbuf(k, es, "ring", [P, RING, D])
        k.alpha = sbuf(k, es, "alpha", [16, 4 * P])
        k.mods = sbuf(k, es, "mods", [P, DEPTH, 48, 2])
        k.gain = sbuf(k, es, "gain", [P, DEPTH, 2, KD, 2])
        k.lower = sbuf(k, es, "lower", [P, DEPTH, 8])
        k.upper = sbuf(k, es, "upper", [P, DEPTH, 8])
        k.back_total = sbuf(k, es, "back_total", [P, HG_HEADS])
        k.qgain = sbuf(k, es, "qgain", [P, 1])
        k.eps = sbuf(k, es, "eps", [P, 1])
        k.one = sbuf(k, es, "one", [P, 1])
        k.bank = [es.enter_context(nc.psum_tensor(f"bank{i}", [P, 512], F32)) for i in range(BANKS)]
        k.small = lambda name: k.small_sb[:, SMALL[name][0]:SMALL[name][0] + SMALL[name][1]]
        k.const = lambda name: k.const_sb[:, CONST[name][0]:CONST[name][0] + CONST[name][1]]
        k.ident, k.ones, k.ones64, k.causal = (k.const(n) for n in ("ident", "ones", "ones64", "causal"))
        k.fwd = k.const("fwd").rearrange("p (l n) -> p l n", l=LEVELS)
        k.both = both
        k.landed = [nc.alloc_semaphore(f"landed{i}") for i in range(RING)]
        k.unit_done = nc.alloc_semaphore("unit_done")
        k.stored = nc.alloc_semaphore("stored")
        k.units = plan_weights(a)

        with stage(k, "load", "loaded") as (block, s):
            @block.sync
            def _(sp):
                for dst, src in ((k.small_sb[:, :], a.small), (k.const_sb[:, :], a.const), (both[:, :, :], a.both),
                                 (k.fox_b[:, :], a.fox_b), (k.gdn_ab[:, :], a.gdn_ab), (k.alpha[:, :], a.gla_w_alpha2_2[0]), (k.X[:, :, :], a.tokens)):
                    sp.dma_start(dst, src).then_inc(s.loaded, 16)
                for u in range(RING):
                    load_unit(k, sp, u)
                sp.wait_ge(s.loaded, 16 * 7)

            @block.vector
            def _(dve):
                dve.memset(k.eps[:, :], EPS)
                dve.memset(k.one[:, :], 1.0)

        if debug is not None:
            debug(k, a, out)
            return
        first_block(k, a)
        k.Y = sbuf(k, es, "Y", [P, KD, T2])
        join_blocks(k, a)
        second_block(k, a)
        store(k, k.Y[:, :, META:T2], out)


def store(k, src, out):
    with stage(k, "store", "") as (block, s):
        @block.sync
        def _(sp):
            sp.dma_start(out, src).then_inc(k.stored, 16)
            sp.wait_ge(k.stored, 16)


def features(v):
    return np.asarray(v).reshape(-1, P).T


def weights(w, cols=None):
    w = np.asarray(w)
    *lead, K, N = w.shape
    w = w.reshape(*lead, K // P, P, N // P, P)
    n = len(lead)
    return np.ascontiguousarray(w.transpose(*range(n), n + 2, n + 1, n, n + 3).reshape(*lead, N // P, P, K))


def narrow(w):
    w = np.asarray(w)
    *lead, K, n = w.shape
    d = len(lead)
    return np.ascontiguousarray(w.reshape(*lead, K // P, P, n).transpose(*range(d), d + 1, d, d + 2).reshape(*lead, P, K // P * n))


def lay_out(i):
    A = {}
    i = {n: np.asarray(v) for n, v in i.items()}
    small = np.empty((P, N_SMALL), np.float32)
    twice = lambda v: np.concatenate([v, v], axis=-1)
    for name, (at, n) in SMALL.items():
        v = twice(i[name]) if name.startswith("fox_") else i[name]
        small[:, at:at + n] = features(v)
    A["small"] = small
    const, both = constants()
    A["const"], A["both"] = const, both.reshape(P, LEVELS + 1, P)
    A["fox_b"] = np.ascontiguousarray(i["fox_b_f_2"].T)
    A["gdn_ab"] = np.ascontiguousarray(np.concatenate([i["gdn_a_log_2"], i["gdn_dt_bias_2"]]).T)
    fm = lambda x: np.ascontiguousarray(x.T.reshape(KD, P, -1).transpose(1, 0, 2))
    A["tokens"] = fm(np.concatenate([i["ctx"][0], i["x"][0]]))
    A["meta"] = fm(i["meta_tokens_2"])
    for name in ("w_mod", "w_in", "w_out", "peer_wq", "w_gate_up_2", "w_down_2", "fox_w_out_2", "gla_w_out_2", "gdn_w_out_2"):
        A[name] = weights(i[name])
    for name, n, extra in (("fox_w_in_2", 4 * D, "fox_w_f"), ("gla_w_in_2", 3 * D, "gla_w_a"), ("gdn_w_in_2", 4 * D, "gdn_w_ab")):
        A[name] = weights(i[name][:, :, :n])
        over = i[name][:, :, n:]
        A[extra] = np.stack([narrow(over[:, :, c:c + 8]) for c in (0, 8)], 1) if extra == "gdn_w_ab" else narrow(over)[:, None]
    A["gla_w_alpha2_2"] = np.ascontiguousarray(i["gla_w_alpha2_2"])
    sk = i["peer_subkeys"]
    A["peer_subkeys"] = np.ascontiguousarray(sk.reshape(DEPTH, 2 * PEER_HEADS, N_KEYS, P).transpose(0, 3, 1, 2))
    for l in range(DEPTH):
        A[f"peer_u{l}"], A[f"peer_v{l}"] = np.ascontiguousarray(i["peer_u"][l]), np.ascontiguousarray(i["peer_v"][l])
    return A


def declare(nc, A):
    aps = {n: nc.dram_tensor(f"in_{n}", v.shape, mybir.dt.from_np(v.dtype), kind="ExternalInput").ap() for n, v in A.items()}
    aps["peer_u"] = [aps[f"peer_u{l}"] for l in range(DEPTH)]
    aps["peer_v"] = [aps[f"peer_v{l}"] for l in range(DEPTH)]
    return namedtuple("Inputs", list(aps))(**aps)


def kernel(**inputs):
    import concourse.bacc as bacc
    from concourse.bass_utils import run_bass_kernel_spmd as run

    nc = bacc.Bacc("TRN2", target_bir_lowering=False, num_devices=1)
    A = lay_out(inputs)
    a = declare(nc, A)
    out = nc.dram_tensor("out", (P, KD, SEQ), F32, kind="ExternalOutput").ap()
    build(nc, a, out)
    r = run(nc, [{f"in_{n}": v for n, v in A.items()}], core_ids=[0])
    y = np.asarray(r.results[0]["out"])
    return np.ascontiguousarray(y.transpose(2, 1, 0).reshape(1, SEQ, D))
```
